# Optimizing a Trainium2 kernel written in Bass

```python
import math
import jax, jax.numpy as jnp
from jax import lax
import numpy as np
import jax
import jax.numpy as jnp

D_MODEL = 1024
BATCH = 1
SEQ = 512
DEPTH = 1

PLE_DIM = 256
N_HEADS = 8
HEAD_DIM = 64
N_KV_HEADS = 2
HEADS_PER_GROUP = N_HEADS // N_KV_HEADS
L_CMP = 32
D_STRIDE = 16
CMP_HIDDEN = 256
L_SLC = 64
N_SEL = 16
WINDOW = 512
Q_BLOCK = 128
N_BUCKETS = 32
MAX_EXACT = N_BUCKETS // 2
MAX_DISTANCE = 128
D_CONV = D_MODEL // 2
CONV_WIDTH = 31
D_FF = 2816
FFN_CONV_WIDTH = 3

EPS = 1e-6
NEG = -1e30
FORCE = 1e4

N_CONV_IN = 2 * D_CONV
N_Q = N_HEADS * HEAD_DIM
N_KV = 6 * N_KV_HEADS * HEAD_DIM
N_NSA_GATE = 3 * N_HEADS
N_MERGE = 2 * D_MODEL
N_IN = N_CONV_IN + N_Q + N_KV + N_NSA_GATE + N_MERGE


def rmsnorm(x, g):
    xf = x.astype(jnp.float32)
    y = xf * lax.rsqrt(jnp.mean(xf * xf, axis=-1, keepdims=True) + EPS)
    return (y * g.astype(jnp.float32)).astype(x.dtype)

def layernorm(x, g, b):
    xf = x.astype(jnp.float32)
    mu = jnp.mean(xf, axis=-1, keepdims=True)
    var = jnp.mean(jnp.square(xf - mu), axis=-1, keepdims=True)
    y = (xf - mu) * lax.rsqrt(var + EPS)
    return (y * g.astype(jnp.float32) + b.astype(jnp.float32)).astype(x.dtype)

def causal_dwconv(x, w, b):
    k, c = w.shape
    y = lax.conv_general_dilated(x, w[:, None, :].astype(x.dtype), (1,), [(k - 1, 0)],
                                 dimension_numbers=('NWC', 'WIO', 'NWC'),
                                 feature_group_count=c)
    return y + b.astype(x.dtype)

def t5_bucket(dist):
    n = jnp.maximum(dist, 0)
    nf = jnp.maximum(n, MAX_EXACT).astype(jnp.float32)
    large = MAX_EXACT + (jnp.log(nf / MAX_EXACT) / math.log(MAX_DISTANCE / MAX_EXACT)
                         * (N_BUCKETS - MAX_EXACT)).astype(jnp.int32)
    large = jnp.minimum(large, N_BUCKETS - 1)
    return jnp.where(n < MAX_EXACT, n, large)

def masked_softmax(s, mask):
    p = jax.nn.softmax(jnp.where(mask, s, NEG), axis=-1)
    return jnp.where(mask, p, 0.0)

def compress(kv, pe, w1, w2):
    b, s, g, dh = kv.shape
    nc = (s - L_CMP) // D_STRIDE + 1
    idx = jnp.arange(nc)[:, None] * D_STRIDE + jnp.arange(L_CMP)[None, :]
    blocks = kv[:, idx] + pe[None, None, :, None, :]
    blocks = blocks.transpose(0, 1, 3, 2, 4).reshape(b, nc, g, L_CMP * dh)
    return jax.nn.gelu(blocks @ w1) @ w2

def nsa_attention(q, k_cmp, v_cmp, k_slc, v_slc, k_win, v_win, gates, rel_bias):
    b, s, g, hpg, dh = q.shape
    nc = k_cmp.shape[1]
    ns = s // L_SLC
    n_sel = min(N_SEL, ns)
    nqb = s // Q_BLOCK
    scale = 1.0 / math.sqrt(dh)

    c_start = jnp.arange(nc) * D_STRIDE
    c_end = c_start + L_CMP - 1
    s_start = jnp.arange(ns) * L_SLC
    agg = ((c_end[:, None] >= s_start[None, :]) &
           (c_start[:, None] <= s_start[None, :] + L_SLC - 1)).astype(jnp.float32)

    k_blocks = k_slc.reshape(b, ns, L_SLC, g, dh).transpose(0, 3, 1, 2, 4)
    v_blocks = v_slc.reshape(b, ns, L_SLC, g, dh).transpose(0, 3, 1, 2, 4)
    k_pad = jnp.pad(k_win, ((0, 0), (WINDOW, 0), (0, 0), (0, 0)))
    v_pad = jnp.pad(v_win, ((0, 0), (WINDOW, 0), (0, 0), (0, 0)))
    bias_grouped = rel_bias.reshape(N_BUCKETS, g, hpg).transpose(1, 0, 2)
    bi = jnp.arange(b)[:, None, None, None]
    gi = jnp.arange(g)[None, :, None, None]

    def head_bias(dist):
        bb = rel_bias[t5_bucket(dist)].astype(jnp.float32)
        return bb.reshape(dist.shape + (g, hpg)).transpose(2, 3, 0, 1)

    def block(qi):
        t0 = qi * Q_BLOCK
        qb = lax.dynamic_slice_in_dim(q, t0, Q_BLOCK, axis=1)
        gb = lax.dynamic_slice_in_dim(gates, t0, Q_BLOCK, axis=1)
        tpos = t0 + jnp.arange(Q_BLOCK)

        dist_c = tpos[:, None] - c_end[None, :]
        s_c = jnp.einsum('bqghd,bcgd->bghqc', qb, k_cmp).astype(jnp.float32) * scale
        p_c = masked_softmax(s_c + head_bias(dist_c), dist_c >= 0)
        o_c = jnp.einsum('bghqc,bcgd->bqghd', p_c.astype(v_cmp.dtype), v_cmp)

        imp = jnp.einsum('bghqc,cs->bgqs', p_c, agg)
        blk = jnp.arange(ns)[None, :]
        cur = (tpos // L_SLC)[:, None]
        valid = blk * L_SLC <= tpos[:, None]
        forced = (blk == 0) | (blk == cur) | (blk == cur - 1)
        imp = jnp.where(forced, FORCE, jnp.where(valid, imp, -FORCE))
        _, idx = lax.top_k(imp, n_sel)
        kb = k_blocks[bi, gi, idx].reshape(b, g, Q_BLOCK, n_sel * L_SLC, dh)
        vb = v_blocks[bi, gi, idx].reshape(b, g, Q_BLOCK, n_sel * L_SLC, dh)
        kpos = (idx[..., None] * L_SLC + jnp.arange(L_SLC)).reshape(b, g, Q_BLOCK, n_sel * L_SLC)
        dist_s = tpos[None, None, :, None] - kpos
        bias_s = bias_grouped[gi, t5_bucket(dist_s)].astype(jnp.float32).transpose(0, 1, 4, 2, 3)
        s_s = jnp.einsum('bqghd,bgqkd->bghqk', qb, kb).astype(jnp.float32) * scale + bias_s
        p_s = masked_softmax(s_s, (dist_s >= 0)[:, :, None])
        o_s = jnp.einsum('bghqk,bgqkd->bqghd', p_s.astype(vb.dtype), vb)

        kw = lax.dynamic_slice_in_dim(k_pad, t0, Q_BLOCK + WINDOW, axis=1)
        vw = lax.dynamic_slice_in_dim(v_pad, t0, Q_BLOCK + WINDOW, axis=1)
        kwpos = t0 - WINDOW + jnp.arange(Q_BLOCK + WINDOW)
        dist_w = tpos[:, None] - kwpos[None, :]
        mask_w = (dist_w >= 0) & (dist_w < WINDOW) & (kwpos[None, :] >= 0)
        s_w = jnp.einsum('bqghd,bkgd->bghqk', qb, kw).astype(jnp.float32) * scale
        p_w = masked_softmax(s_w + head_bias(dist_w), mask_w)
        o_w = jnp.einsum('bghqk,bkgd->bqghd', p_w.astype(vw.dtype), vw)

        return gb[..., 0:1] * o_c + gb[..., 1:2] * o_s + gb[..., 2:3] * o_w

    out = lax.map(block, jnp.arange(nqb))
    return jnp.moveaxis(out, 0, 1).reshape(b, s, g * hpg * dh)

def first_inputs(seed: int = 0) -> dict:
    key = jax.random.key(seed)
    ks = jax.random.split(key, 27)
    f32 = jnp.float32

    def nrm(k, shape, scale):
        return jax.random.normal(k, shape, f32) * scale

    def gain(k, shape):
        return 1.0 + 0.01 * jax.random.normal(k, shape, f32)

    L = DEPTH
    return {
        "x": nrm(ks[0], (BATCH, SEQ, D_MODEL), 1.0),
        "p": nrm(ks[1], (DEPTH, BATCH, SEQ, PLE_DIM), 1.0),
        "rel_bias": nrm(ks[2], (N_BUCKETS, N_HEADS), 0.1),
        "norm_mix": gain(ks[3], (L, D_MODEL)),
        "w_in": nrm(ks[4], (L, D_MODEL, N_IN), D_MODEL ** -0.5),
        "conv_dw_w": nrm(ks[5], (L, CONV_WIDTH, D_CONV), CONV_WIDTH ** -0.5),
        "conv_dw_b": nrm(ks[6], (L, D_CONV), 0.01),
        "conv_ln_g": gain(ks[7], (L, D_CONV)),
        "conv_ln_b": nrm(ks[8], (L, D_CONV), 0.01),
        "w_conv_out": nrm(ks[9], (L, D_CONV, D_MODEL), D_CONV ** -0.5),
        "cmp_pe_k": nrm(ks[10], (L, L_CMP, HEAD_DIM), 0.1),
        "cmp_pe_v": nrm(ks[11], (L, L_CMP, HEAD_DIM), 0.1),
        "w_ck1": nrm(ks[12], (L, L_CMP * HEAD_DIM, CMP_HIDDEN), (L_CMP * HEAD_DIM) ** -0.5),
        "w_ck2": nrm(ks[13], (L, CMP_HIDDEN, HEAD_DIM), CMP_HIDDEN ** -0.5),
        "w_cv1": nrm(ks[14], (L, L_CMP * HEAD_DIM, CMP_HIDDEN), (L_CMP * HEAD_DIM) ** -0.5),
        "w_cv2": nrm(ks[15], (L, CMP_HIDDEN, HEAD_DIM), CMP_HIDDEN ** -0.5),
        "w_attn_out": nrm(ks[16], (L, N_HEADS * HEAD_DIM, D_MODEL), (N_HEADS * HEAD_DIM) ** -0.5),
        "w_out": nrm(ks[17], (L, D_MODEL, D_MODEL), D_MODEL ** -0.5),
        "norm_ffn": gain(ks[18], (L, D_MODEL)),
        "w_up": nrm(ks[19], (L, D_MODEL, 2 * D_FF), D_MODEL ** -0.5),
        "ffn_dw_w": nrm(ks[20], (L, FFN_CONV_WIDTH, 2 * D_FF), FFN_CONV_WIDTH ** -0.5),
        "ffn_dw_b": nrm(ks[21], (L, 2 * D_FF), 0.01),
        "w_down": nrm(ks[22], (L, D_FF, D_MODEL), D_FF ** -0.5),
        "norm_ple": gain(ks[23], (L, D_MODEL)),
        "w_ple_gate": nrm(ks[24], (L, D_MODEL, D_MODEL), D_MODEL ** -0.5),
        "w_ple": nrm(ks[25], (L, PLE_DIM, D_MODEL), PLE_DIM ** -0.5),
        "norm_final": gain(ks[26], (D_MODEL,)),
    }

def first_block(x, p, rel_bias, norm_mix, w_in, conv_dw_w, conv_dw_b, conv_ln_g, conv_ln_b,
              w_conv_out, cmp_pe_k, cmp_pe_v, w_ck1, w_ck2, w_cv1, w_cv2, w_attn_out, w_out,
              norm_ffn, w_up, ffn_dw_w, ffn_dw_b, w_down, norm_ple, w_ple_gate, w_ple, norm_final):
    b, s, d = x.shape
    g, hpg, dh = N_KV_HEADS, HEADS_PER_GROUP, HEAD_DIM
    splits = [N_CONV_IN, N_CONV_IN + N_Q, N_CONV_IN + N_Q + N_KV,
              N_CONV_IN + N_Q + N_KV + N_NSA_GATE]
    for i in range(DEPTH):
        h = rmsnorm(x, norm_mix[i])
        z = h @ w_in[i]
        u, qf, kvf, ng, mg = jnp.split(z, splits, axis=-1)

        a = u[..., :D_CONV] * jax.nn.sigmoid(u[..., D_CONV:])
        a = causal_dwconv(a, conv_dw_w[i], conv_dw_b[i])
        a = jax.nn.silu(layernorm(a, conv_ln_g[i], conv_ln_b[i]))
        y_conv = a @ w_conv_out[i]

        q = qf.reshape(b, s, g, hpg, dh)
        kv = kvf.reshape(b, s, 6, g, dh)
        k_c, v_c, k_s, v_s, k_w, v_w = (kv[:, :, 0], kv[:, :, 1], kv[:, :, 2],
                                        kv[:, :, 3], kv[:, :, 4], kv[:, :, 5])
        k_cmp = compress(k_c, cmp_pe_k[i], w_ck1[i], w_ck2[i])
        v_cmp = compress(v_c, cmp_pe_v[i], w_cv1[i], w_cv2[i])
        nsa_gates = jax.nn.sigmoid(ng).reshape(b, s, g, hpg, 3)
        o = nsa_attention(q, k_cmp, v_cmp, k_s, v_s, k_w, v_w, nsa_gates, rel_bias)
        y_attn = o @ w_attn_out[i]

        y = jax.nn.sigmoid(mg[..., :d]) * y_conv + jax.nn.sigmoid(mg[..., d:]) * y_attn
        x = x + y @ w_out[i]

        hf = rmsnorm(x, norm_ffn[i])
        up = causal_dwconv(hf @ w_up[i], ffn_dw_w[i], ffn_dw_b[i])
        gate, val = jnp.split(up, 2, axis=-1)
        x = x + (jax.nn.gelu(gate) * val) @ w_down[i]

        pg = jax.nn.sigmoid(rmsnorm(x, norm_ple[i]) @ w_ple_gate[i])
        x = x + pg * (p[i] @ w_ple[i])
    return rmsnorm(x, norm_final)


_first_inputs = first_inputs


def first_inputs(seed=0):
    import zlib

    import numpy as np

    out = dict(_first_inputs(seed))
    spreads = {}
    factors = {'rel_bias': 8.0,
     'norm_mix': 8.0,
     'conv_dw_b': 8.0,
     'conv_ln_g': 8.0,
     'conv_ln_b': 8.0,
     'cmp_pe_k': 8.0,
     'cmp_pe_v': 3.595,
     'norm_ffn': 8.0,
     'ffn_dw_b': 7.92,
     'norm_ple': 8.0,
     'norm_final': 5.586}
    for name, (base, spread) in spreads.items():
        noise = np.random.default_rng([zlib.crc32(name.encode()), seed]).standard_normal(out[name].shape)
        drawn = base * np.exp(spread * noise) if base else spread * noise
        out[name] = __import__('jax').numpy.asarray(drawn.astype(out[name].dtype))
    for name, factor in factors.items():
        out[name] = (out[name] * factor).astype(out[name].dtype)
    return out


_narrow_inputs = first_inputs


def first_inputs(seed=0):

    out = dict(_narrow_inputs(seed))
    wider = {'p': 4.25,
     'conv_dw_b': 4.59,
     'conv_ln_g': 7.93,
     'conv_ln_b': 8.03,
     'norm_ffn': 4.68,
     'ffn_dw_b': 4.41,
     'norm_ple': 12.0,
     'w_ple_gate': 6.38,
     'w_ple': 4.24,
     'norm_final': 6.3}
    for name, times in wider.items():
        mean = out[name].mean()
        out[name] = (mean + times * (out[name] - mean)).astype(out[name].dtype)
    return out


DEPTH_2 = 2

N_MIXERS = 2
N_HYENA = (DEPTH_2 + 1) // 2
N_RWKV = DEPTH_2 // 2
RMS_EPS = 1e-6

HY_ORDER = 2
HY_N_PROJ = HY_ORDER + 1
HY_SHORT_CONV = 3
HY_EMB = 33
HY_BANDS = (HY_EMB - 1) // 2
HY_FILTER_WIDTH = 64
HY_DECAY_TARGET = 1e-2
HY_FAST_DECAY_PCT = 0.3
HY_SLOW_DECAY_PCT = 1.5

RW_HEAD = 64
RW_HEADS = D_MODEL // RW_HEAD
RW_DECAY_LORA = 64
RW_ICLR_LORA = 64
RW_VRES_LORA = 32
RW_GATE_LORA = 128
RW_GN_EPS = RW_HEAD * 1e-5
RW_N_LERP = 6

D_FF_2 = ((8 * D_MODEL // 3 + 255) // 256) * 256
FFN_CONV = 3


def _rmsnorm(x, g):
    x32 = x.astype(jnp.float32)
    y = x32 * lax.rsqrt(jnp.mean(x32 * x32, axis=-1, keepdims=True) + RMS_EPS)
    return (y * g.astype(jnp.float32)).astype(x.dtype)

def _dwconv_centred(x, w, b):
    K, C = w.shape
    y = lax.conv_general_dilated(
        x, w[:, None, :].astype(x.dtype), window_strides=(1,),
        padding=((K // 2, K // 2),), dimension_numbers=('NWC', 'WIO', 'NWC'),
        feature_group_count=C)
    return y + b.astype(x.dtype)

def _hyena_filter(L, w1, b1, w2, b2, w3, b3, w4, freq):
    f32 = jnp.float32
    n = jnp.arange(L, dtype=f32)
    t = (n / max(L - 1, 1))[:, None]
    fr = jnp.linspace(1e-4, HY_BANDS - 1, HY_BANDS, dtype=f32)
    ang = (2.0 * math.pi / L) * n[:, None] * fr[None, :]
    z = jnp.concatenate([t, jnp.cos(ang), -jnp.sin(ang)], axis=-1)
    fq = freq.astype(f32)
    hdn = jnp.sin(fq * (z @ w1.astype(f32) + b1.astype(f32)))
    hdn = jnp.sin(fq * (hdn @ w2.astype(f32) + b2.astype(f32)))
    hdn = jnp.sin(fq * (hdn @ w3.astype(f32) + b3.astype(f32)))
    k = hdn @ w4.astype(f32)
    D = w4.shape[-1] // 2
    deltas = jnp.abs(jnp.linspace(math.log(HY_DECAY_TARGET) / HY_SLOW_DECAY_PCT,
                                  math.log(HY_DECAY_TARGET) / HY_FAST_DECAY_PCT, D, dtype=f32))
    k = k * jnp.exp(-t * jnp.tile(deltas, 2)[None, :])
    return k[:, :D], k[:, D:]

def _bidir_fftconv(u, k_fwd, k_bwd):
    L = u.shape[1]
    n = 2 * L
    D = k_fwd.shape[1]
    k_c = jnp.concatenate([k_fwd.at[0].add(k_bwd[0]),
                           jnp.zeros((1, D), jnp.float32),
                           k_bwd[:0:-1]], axis=0)
    kf = jnp.fft.rfft(k_c, n=n, axis=0)
    uf = jnp.fft.rfft(u, n=n, axis=1)
    return jnp.fft.irfft(uf * kf[None], n=n, axis=1)[:, :L]

def _hyena_mixer(h, w_in, b_in, conv_w, conv_b, f_w1, f_b1, f_w2, f_b2, f_w3, f_b3,
                 f_w4, f_freq, skip, w_out, b_out):
    B, L, D = h.shape
    z = _dwconv_centred(h @ w_in + b_in, conv_w, conv_b)
    x0, x1, v = jnp.split(z, HY_N_PROJ, axis=-1)
    k_fwd, k_bwd = _hyena_filter(L, f_w1, f_b1, f_w2, f_b2, f_w3, f_b3, f_w4, f_freq)
    u = (v * x1).astype(jnp.float32)
    y = _bidir_fftconv(u, k_fwd, k_bwd) + u * skip.astype(jnp.float32)
    y = y.astype(h.dtype) * x0
    return y @ w_out + b_out

def _token_shift_delta(h):
    prev = jnp.pad(h[:, :-1], ((0, 0), (1, 0), (0, 0)))
    nxt = jnp.pad(h[:, 1:], ((0, 0), (0, 1), (0, 0)))
    return 0.5 * (prev + nxt) - h

def _decay(xw, w0, w1, w2):
    wl = w0.astype(jnp.float32) + (jnp.tanh(xw @ w1) @ w2).astype(jnp.float32)
    wl = -jax.nn.softplus(-wl) - 0.5
    return jnp.exp(-jnp.exp(wl))

def _wkv7_scan(r, w, k, v, kk, a):
    B, L, H, N = r.shape

    def step(state, inp):
        r_t, w_t, k_t, v_t, kk_t, a_t = inp
        sa = jnp.einsum('bhvk,bhk->bhv', state, kk_t)
        state = (state * w_t[:, :, None, :]
                 - sa[..., None] * (kk_t * a_t)[:, :, None, :]
                 + v_t[..., None] * k_t[:, :, None, :])
        return state, jnp.einsum('bhvk,bhk->bhv', state, r_t)

    xs = tuple(jnp.swapaxes(t, 0, 1) for t in (r, w, k, v, kk, a))
    s0 = jnp.zeros((B, H, N, N), jnp.float32)
    _, ys = lax.scan(step, s0, xs)
    return jnp.swapaxes(ys, 0, 1)

def _rwkv7_mixer(h, v_first, mu, w_r, w_k, w_v, w_o, w0, w1, w2, a0, a1, a2,
                 g1, g2, k_k, k_a, r_k, ln_w, ln_b, vres):
    B, L, D = h.shape
    H, N = RW_HEADS, RW_HEAD
    f32 = jnp.float32
    xx = _token_shift_delta(h)
    xr, xw, xk, xv, xa, xg = [h + xx * mu[j] for j in range(RW_N_LERP)]
    r = xr @ w_r
    k = xk @ w_k
    v = xv @ w_v
    a = jax.nn.sigmoid(a0 + (xa @ a1) @ a2)
    g = jax.nn.sigmoid(xg @ g1) @ g2
    if vres is None:
        v_first = v
    else:
        v0, v1, v2 = vres
        v = v + (v_first - v) * jax.nn.sigmoid(v0 + (xv @ v1) @ v2)

    def heads(t):
        return t.astype(f32).reshape(B, L, H, N)

    kk = heads(k * k_k)
    kk = kk / jnp.maximum(jnp.linalg.norm(kk, axis=-1, keepdims=True), 1e-12)
    k = k * (1.0 + (a - 1.0) * k_a)
    rh, kh, vh, ah = heads(r), heads(k), heads(v), heads(a)
    w_f = heads(_decay(xw, w0[0], w1[0], w2[0]))
    w_b = heads(_decay(xw, w0[1], w1[1], w2[1]))

    def flip(t):
        return jnp.flip(t, axis=1)

    y = _wkv7_scan(rh, w_f, kh, vh, kk, ah)
    y = y + flip(_wkv7_scan(flip(rh), flip(w_b), flip(kh), flip(vh), flip(kk), flip(ah)))
    mean = jnp.mean(y, axis=-1, keepdims=True)
    var = jnp.mean(jnp.square(y - mean), axis=-1, keepdims=True)
    y = ((y - mean) * lax.rsqrt(var + RW_GN_EPS)).reshape(B, L, D)
    y = y * ln_w.astype(f32) + ln_b.astype(f32)
    bonus = jnp.sum(rh * kh * r_k.astype(f32), axis=-1, keepdims=True) * vh
    y = y + bonus.reshape(B, L, D)
    return (y.astype(h.dtype) * g) @ w_o, v_first

def _conv_ffn(h, w_up, conv_w, conv_b, w_down):
    u = _dwconv_centred(h @ w_up, conv_w, conv_b)
    gate, val = jnp.split(u, 2, axis=-1)
    return (jax.nn.silu(gate) * val) @ w_down

def second_inputs(seed: int = 0) -> dict:
    key = jax.random.key(seed)
    ks = iter(jax.random.split(key, 64))
    f32 = jnp.float32

    def nrm(shape, scale):
        return scale * jax.random.normal(next(ks), shape, f32)

    D, F, W = D_MODEL, D_FF_2, HY_FILTER_WIDTH
    NH, NR = N_HYENA, N_RWKV
    C3 = HY_N_PROJ * D
    ramp = (jnp.arange(D, dtype=f32) / (D - 1)) ** 0.85
    return {
        'x': nrm((BATCH, SEQ, D), 1.0),
        'norm_mix_g': 1.0 + nrm((DEPTH_2, D), 0.02),
        'norm_ffn_g': 1.0 + nrm((DEPTH_2, D), 0.02),
        'final_norm_g': 1.0 + nrm((D,), 0.02),
        'hy_w_in': nrm((NH, D, C3), D ** -0.5),
        'hy_b_in': nrm((NH, C3), 0.02),
        'hy_conv_w': nrm((NH, HY_SHORT_CONV, C3), HY_SHORT_CONV ** -0.5),
        'hy_conv_b': nrm((NH, C3), 0.02),
        'hy_f_w1': nrm((NH, HY_EMB, W), HY_EMB ** -0.5),
        'hy_f_b1': nrm((NH, W), 0.1),
        'hy_f_w2': nrm((NH, W, W), W ** -0.5),
        'hy_f_b2': nrm((NH, W), 0.1),
        'hy_f_w3': nrm((NH, W, W), W ** -0.5),
        'hy_f_b3': nrm((NH, W), 0.1),
        'hy_f_w4': nrm((NH, W, 2 * D), 0.01),
        'hy_f_freq': 1.0 + nrm((NH, W), 0.1),
        'hy_skip': nrm((NH, D), 1.0),
        'hy_w_out': nrm((NH, D, D), D ** -0.5),
        'hy_b_out': nrm((NH, D), 0.02),
        'rw_mu': jax.random.uniform(next(ks), (NR, RW_N_LERP, D), f32),
        'rw_w_r': nrm((NR, D, D), D ** -0.5),
        'rw_w_k': nrm((NR, D, D), D ** -0.5),
        'rw_w_v': nrm((NR, D, D), D ** -0.5),
        'rw_w_o': nrm((NR, D, D), D ** -0.5),
        'rw_w0': -6.5 + 5.0 * ramp + nrm((NR, 2, D), 0.1),
        'rw_w1': nrm((NR, 2, D, RW_DECAY_LORA), D ** -0.5),
        'rw_w2': nrm((NR, 2, RW_DECAY_LORA, D), 0.5 * RW_DECAY_LORA ** -0.5),
        'rw_a0': nrm((NR, D), 0.1),
        'rw_a1': nrm((NR, D, RW_ICLR_LORA), D ** -0.5),
        'rw_a2': nrm((NR, RW_ICLR_LORA, D), 0.5 * RW_ICLR_LORA ** -0.5),
        'rw_v0': 1.0 + nrm((NR - 1, D), 0.1),
        'rw_v1': nrm((NR - 1, D, RW_VRES_LORA), D ** -0.5),
        'rw_v2': nrm((NR - 1, RW_VRES_LORA, D), 0.5 * RW_VRES_LORA ** -0.5),
        'rw_g1': nrm((NR, D, RW_GATE_LORA), D ** -0.5),
        'rw_g2': nrm((NR, RW_GATE_LORA, D), RW_GATE_LORA ** -0.5),
        'rw_k_k': 0.85 + nrm((NR, D), 0.02),
        'rw_k_a': 1.0 + nrm((NR, D), 0.02),
        'rw_r_k': -0.04 + nrm((NR, RW_HEADS, RW_HEAD), 0.1),
        'rw_ln_w': 1.0 + nrm((NR, D), 0.02),
        'rw_ln_b': nrm((NR, D), 0.02),
        'ff_w_up': nrm((DEPTH_2, D, 2 * F), D ** -0.5),
        'ff_conv_w': nrm((DEPTH_2, FFN_CONV, 2 * F), FFN_CONV ** -0.5),
        'ff_conv_b': nrm((DEPTH_2, 2 * F), 0.02),
        'ff_w_down': nrm((DEPTH_2, F, D), F ** -0.5),
    }

def second_block(x, norm_mix_g, norm_ffn_g, final_norm_g,
              hy_w_in, hy_b_in, hy_conv_w, hy_conv_b,
              hy_f_w1, hy_f_b1, hy_f_w2, hy_f_b2, hy_f_w3, hy_f_b3, hy_f_w4, hy_f_freq,
              hy_skip, hy_w_out, hy_b_out,
              rw_mu, rw_w_r, rw_w_k, rw_w_v, rw_w_o, rw_w0, rw_w1, rw_w2,
              rw_a0, rw_a1, rw_a2, rw_v0, rw_v1, rw_v2, rw_g1, rw_g2,
              rw_k_k, rw_k_a, rw_r_k, rw_ln_w, rw_ln_b,
              ff_w_up, ff_conv_w, ff_conv_b, ff_w_down):
    v_first = None
    for i in range(DEPTH_2):
        h = _rmsnorm(x, norm_mix_g[i])
        j = i // N_MIXERS
        if i % N_MIXERS == 0:
            y = _hyena_mixer(h, hy_w_in[j], hy_b_in[j], hy_conv_w[j], hy_conv_b[j],
                             hy_f_w1[j], hy_f_b1[j], hy_f_w2[j], hy_f_b2[j],
                             hy_f_w3[j], hy_f_b3[j], hy_f_w4[j], hy_f_freq[j],
                             hy_skip[j], hy_w_out[j], hy_b_out[j])
        else:
            vres = (rw_v0[j - 1], rw_v1[j - 1], rw_v2[j - 1]) if j > 0 else None
            y, v_first = _rwkv7_mixer(h, v_first, rw_mu[j], rw_w_r[j], rw_w_k[j], rw_w_v[j], rw_w_o[j],
                                      rw_w0[j], rw_w1[j], rw_w2[j], rw_a0[j], rw_a1[j], rw_a2[j],
                                      rw_g1[j], rw_g2[j], rw_k_k[j], rw_k_a[j], rw_r_k[j],
                                      rw_ln_w[j], rw_ln_b[j], vres)
        x = x + y
        h = _rmsnorm(x, norm_ffn_g[i])
        x = x + _conv_ffn(h, ff_w_up[i], ff_conv_w[i], ff_conv_b[i], ff_w_down[i])
    return _rmsnorm(x, final_norm_g)


_first_inputs_2 = second_inputs


def second_inputs(seed=0):
    import zlib

    import numpy as np

    out = dict(_first_inputs_2(seed))
    spreads = {}
    factors = {'norm_ffn_g': 3.204,
     'final_norm_g': 9.024,
     'hy_b_out': 2.838,
     'rw_w1': 5.03,
     'rw_w2': 4.976,
     'rw_a0': 4.448,
     'rw_k_k': 64.0,
     'rw_k_a': 20.231,
     'rw_ln_w': 39.858,
     'rw_ln_b': 36.951,
     'ff_conv_b': 3.385}
    for name, (base, spread) in spreads.items():
        noise = np.random.default_rng([zlib.crc32(name.encode()), seed]).standard_normal(out[name].shape)
        drawn = base * np.exp(spread * noise) if base else spread * noise
        out[name] = jnp.asarray(drawn.astype(out[name].dtype))
    for name, factor in factors.items():
        out[name] = (out[name] * factor).astype(out[name].dtype)
    return out


_narrow_inputs_2 = second_inputs


def second_inputs(seed=0):

    out = dict(_narrow_inputs_2(seed))
    wider = {'final_norm_g': 3.39, 'rw_k_k': 6.14, 'rw_ln_w': 3.3, 'rw_ln_b': 3.27}
    for name, times in wider.items():
        mean = out[name].mean()
        out[name] = (mean + times * (out[name] - mean)).astype(out[name].dtype)
    return out


M_HEADS = 4
M_HEAD_DIM = 512
M_WIDTH = M_HEADS * M_HEAD_DIM
M_CHUNK = 64
CONV_WIDTH_3 = 4
M_FORGET_BIAS_LO = 3.0
M_FORGET_BIAS_HI = 6.0
H_HEADS = 8
H_EXPAND = 128
H_VDIM = D_MODEL // H_HEADS
H_KWIDTH = H_HEADS * H_EXPAND
H_VWIDTH = H_HEADS * H_VDIM
H_CHUNK = 16
FFN_HIDDEN = -(-(8 * D_MODEL) // (3 * 256)) * 256
ALPHA = (2 * DEPTH) ** 0.25
BETA = (8 * DEPTH) ** -0.25
LN_EPS = 1e-5
HEAD_NORM_EPS = 1e-6
IN_SIZES = (M_WIDTH, M_WIDTH, M_WIDTH, M_WIDTH, M_HEADS, M_HEADS,
            H_KWIDTH, H_KWIDTH, H_VWIDTH, H_VWIDTH, D_MODEL, D_MODEL)
IN_WIDTH = sum(IN_SIZES)


def _in_offsets():
    return [int(o) for o in np.cumsum((0,) + IN_SIZES)]

def _split_heads(a, n_heads):
    return a.reshape(a.shape[:2] + (n_heads, -1))

def _to_chunks(a, chunk):
    b, s, h = a.shape[:3]
    a = a.reshape((b, s // chunk, chunk, h) + a.shape[3:])
    return jnp.moveaxis(a, (1, 3), (0, 2))

def _from_chunks(a):
    a = jnp.moveaxis(a, (0, 2), (1, 3))
    return a.reshape((a.shape[0], a.shape[1] * a.shape[2]) + a.shape[3:])

def _layernorm(x, g, b):
    xf = x.astype(jnp.float32)
    mu = jnp.mean(xf, axis=-1, keepdims=True)
    var = jnp.mean(jnp.square(xf - mu), axis=-1, keepdims=True)
    return ((xf - mu) * lax.rsqrt(var + LN_EPS) * g + b).astype(x.dtype)

def _head_layernorm(h, gain):
    mu = jnp.mean(h, axis=-1, keepdims=True)
    var = jnp.mean(jnp.square(h - mu), axis=-1, keepdims=True)
    hn = (h - mu) * lax.rsqrt(var + HEAD_NORM_EPS)
    return hn.reshape(h.shape[:2] + (-1,)) * gain

def _head_rmsnorm(h, gain):
    hn = h * lax.rsqrt(jnp.mean(jnp.square(h), axis=-1, keepdims=True) + HEAD_NORM_EPS)
    return hn.reshape(h.shape[:2] + (-1,)) * gain

def _causal_depthwise_conv(u, w, b):
    c = u.shape[-1]
    y = lax.conv_general_dilated(u, w[:, None, :].astype(u.dtype), window_strides=(1,),
                                 padding=[(CONV_WIDTH_3 - 1, 0)],
                                 dimension_numbers=('NWC', 'WIO', 'NWC'),
                                 feature_group_count=c)
    return y + b

def _hgrn_lower_bounds(lb_logits):
    p = jax.nn.softmax(lb_logits.astype(jnp.float32), axis=0)
    c = jnp.cumsum(p, axis=0)
    return c - c[0:1]

def _mlstm_chunkwise(q, k, v, i_pre, f_pre):
    f32 = jnp.float32
    bsz, _, n_heads, dh = q.shape
    q = q.astype(f32)
    k = k.astype(f32) * (dh ** -0.5)
    v = v.astype(f32)
    log_f = jax.nn.log_sigmoid(f_pre.astype(f32))
    log_i = i_pre.astype(f32)
    causal = jnp.tril(jnp.ones((M_CHUNK, M_CHUNK), dtype=bool))

    def step(carry, xs):
        c_mat, n_vec, m_prev = carry
        qc, kc, vc, ic, lfc = xs
        b = jnp.cumsum(lfc, axis=-1)
        log_w = jnp.where(causal, b[..., :, None] - b[..., None, :] + ic[..., None, :], -jnp.inf)
        log_inter = b + m_prev[..., None]
        m_t = jnp.maximum(log_inter, jnp.max(log_w, axis=-1))
        w = jnp.exp(log_w - m_t[..., None]) * jnp.einsum('bhtd,bhsd->bhts', qc, kc)
        s_inter = jnp.exp(log_inter - m_t)
        num = (jnp.einsum('bhts,bhsd->bhtd', w, vc)
               + s_inter[..., None] * jnp.einsum('bhtk,bhkv->bhtv', qc, c_mat))
        den = jnp.sum(w, axis=-1) + s_inter * jnp.einsum('bhtk,bhk->bht', qc, n_vec)
        h = num / jnp.maximum(jnp.abs(den), jnp.exp(-m_t))[..., None]
        b_end = b[..., -1]
        log_g = b_end[..., None] - b + ic
        m_new = jnp.maximum(b_end + m_prev, jnp.max(log_g, axis=-1))
        decay = jnp.exp(b_end + m_prev - m_new)
        g = jnp.exp(log_g - m_new[..., None])
        c_mat = decay[..., None, None] * c_mat + jnp.einsum('bhs,bhsk,bhsv->bhkv', g, kc, vc)
        n_vec = decay[..., None] * n_vec + jnp.einsum('bhs,bhsk->bhk', g, kc)
        return (c_mat, n_vec, m_new), h

    init = (jnp.zeros((bsz, n_heads, dh, dh), f32),
            jnp.zeros((bsz, n_heads, dh), f32),
            jnp.zeros((bsz, n_heads), f32))
    xs = (_to_chunks(q, M_CHUNK), _to_chunks(k, M_CHUNK), _to_chunks(v, M_CHUNK),
          _to_chunks(log_i, M_CHUNK), _to_chunks(log_f, M_CHUNK))
    _, h = lax.scan(step, init, xs)
    return _from_chunks(h)

def _hgrn2_chunkwise(q, k, v, log_f):
    f32 = jnp.float32
    bsz, _, n_heads, kd = q.shape
    vd = v.shape[-1]
    causal = jnp.tril(jnp.ones((H_CHUNK, H_CHUNK), dtype=bool))[:, :, None]

    def step(state, xs):
        qc, kc, vc, lfc = xs
        a = jnp.cumsum(lfc, axis=2)
        rel = jnp.where(causal, a[:, :, :, None, :] - a[:, :, None, :, :], -jnp.inf)
        scores = jnp.einsum('bhtk,bhtsk,bhsk->bhts', qc, jnp.exp(rel), kc)
        o = (jnp.einsum('bhts,bhsv->bhtv', scores, vc)
             + jnp.einsum('bhtk,bhkv->bhtv', qc * jnp.exp(a), state))
        a_end = a[:, :, -1:, :]
        state = (jnp.exp(a_end[:, :, 0, :])[..., None] * state
                 + jnp.einsum('bhsk,bhsv->bhkv', kc * jnp.exp(a_end - a), vc))
        return state, o

    init = jnp.zeros((bsz, n_heads, kd, vd), f32)
    xs = tuple(_to_chunks(t.astype(f32), H_CHUNK) for t in (q, k, v, log_f))
    _, o = lax.scan(step, init, xs)
    return _from_chunks(o)

def third_inputs(seed: int = 0) -> dict:
    key = jax.random.key(seed)
    ks = jax.random.split(key, 18)
    f32 = jnp.float32
    off = _in_offsets()

    def nrm(k, shape, scale):
        return jax.random.normal(k, shape, f32) * scale

    x = nrm(ks[0], (BATCH, SEQ, D_MODEL), 1.0)
    w_in = nrm(ks[1], (DEPTH, D_MODEL, IN_WIDTH), D_MODEL ** -0.5)
    w_in = w_in.at[:, :, off[2]:off[3]].multiply(BETA)
    w_in = w_in.at[:, :, off[8]:off[9]].multiply(BETA)
    b_in = nrm(ks[2], (DEPTH, IN_WIDTH), 0.01)
    b_in = b_in.at[:, off[5]:off[6]].add(
        jnp.linspace(M_FORGET_BIAS_LO, M_FORGET_BIAS_HI, M_HEADS, dtype=f32))
    conv_w = nrm(ks[3], (DEPTH, CONV_WIDTH_3, 2 * M_WIDTH), CONV_WIDTH_3 ** -0.5)
    conv_b = nrm(ks[4], (DEPTH, 2 * M_WIDTH), 0.01)
    m_norm_g = 1.0 + nrm(ks[5], (DEPTH, M_WIDTH), 0.02)
    lb_logits = nrm(ks[6], (DEPTH, H_KWIDTH), 0.1)
    h_norm_g = 1.0 + nrm(ks[7], (DEPTH, H_VWIDTH), 0.02)
    w_proj_a = nrm(ks[8], (DEPTH, M_WIDTH, D_MODEL), BETA * M_WIDTH ** -0.5)
    w_proj_b = nrm(ks[9], (DEPTH, H_VWIDTH, D_MODEL), BETA * H_VWIDTH ** -0.5)
    w_out = nrm(ks[10], (DEPTH, D_MODEL, D_MODEL), BETA * D_MODEL ** -0.5)
    ln1_g = 1.0 + nrm(ks[11], (DEPTH, D_MODEL), 0.02)
    ln1_b = nrm(ks[12], (DEPTH, D_MODEL), 0.02)
    w_ffn_gate = nrm(ks[13], (DEPTH, D_MODEL, FFN_HIDDEN), D_MODEL ** -0.5)
    w_ffn_up = nrm(ks[14], (DEPTH, D_MODEL, FFN_HIDDEN), BETA * D_MODEL ** -0.5)
    w_ffn_down = nrm(ks[15], (DEPTH, FFN_HIDDEN, D_MODEL), BETA * FFN_HIDDEN ** -0.5)
    ln2_g = 1.0 + nrm(ks[16], (DEPTH, D_MODEL), 0.02)
    ln2_b = nrm(ks[17], (DEPTH, D_MODEL), 0.02)
    return {'x': x, 'w_in': w_in, 'b_in': b_in, 'conv_w': conv_w, 'conv_b': conv_b,
            'm_norm_g': m_norm_g, 'lb_logits': lb_logits, 'h_norm_g': h_norm_g,
            'w_proj_a': w_proj_a, 'w_proj_b': w_proj_b, 'w_out': w_out,
            'ln1_g': ln1_g, 'ln1_b': ln1_b, 'w_ffn_gate': w_ffn_gate, 'w_ffn_up': w_ffn_up,
            'w_ffn_down': w_ffn_down, 'ln2_g': ln2_g, 'ln2_b': ln2_b}

def third_block(x, w_in, b_in, conv_w, conv_b, m_norm_g, lb_logits, h_norm_g, w_proj_a, w_proj_b,
              w_out, ln1_g, ln1_b, w_ffn_gate, w_ffn_up, w_ffn_down, ln2_g, ln2_b):
    split_points = _in_offsets()[1:-1]
    lower_bounds = _hgrn_lower_bounds(lb_logits)
    for layer in range(DEPTH):
        u = x @ w_in[layer] + b_in[layer]
        (mq, mk, mv, mo, mi, mf, hq, hf, hi, hg, ga, gb) = jnp.split(u, split_points, axis=-1)

        qk = jax.nn.silu(_causal_depthwise_conv(jnp.concatenate([mq, mk], axis=-1),
                                                conv_w[layer], conv_b[layer]))
        mq, mk = jnp.split(qk, 2, axis=-1)
        h_a = _mlstm_chunkwise(_split_heads(mq, M_HEADS), _split_heads(mk, M_HEADS),
                               _split_heads(mv, M_HEADS), mi, mf)
        h_a = (_head_layernorm(h_a, m_norm_g[layer]) * jax.nn.sigmoid(mo)).astype(x.dtype)

        lb = lower_bounds[layer]
        log_f = jnp.logaddexp(jnp.log(lb), jnp.log1p(-lb) + jax.nn.log_sigmoid(hf.astype(jnp.float32)))
        h_b = _hgrn2_chunkwise(_split_heads(jax.nn.silu(hq), H_HEADS),
                               _split_heads(-jnp.expm1(log_f), H_HEADS),
                               _split_heads(hi, H_HEADS),
                               _split_heads(log_f, H_HEADS))
        h_b = (_head_rmsnorm(h_b, h_norm_g[layer]) * jax.nn.sigmoid(hg)).astype(x.dtype)

        mixed = (jax.nn.sigmoid(ga) * (h_a @ w_proj_a[layer])
                 + jax.nn.sigmoid(gb) * (h_b @ w_proj_b[layer]))
        x = _layernorm(ALPHA * x + mixed @ w_out[layer], ln1_g[layer], ln1_b[layer])

        ffn = (jax.nn.silu(x @ w_ffn_gate[layer]) * (x @ w_ffn_up[layer])) @ w_ffn_down[layer]
        x = _layernorm(ALPHA * x + ffn, ln2_g[layer], ln2_b[layer])
    return x


_first_inputs_3 = third_inputs


def third_inputs(seed=0):
    import zlib

    import numpy as np

    out = dict(_first_inputs_3(seed))
    spreads = {}
    factors = {'conv_b': 23.961,
     'm_norm_g': 39.79,
     'h_norm_g': 41.435,
     'ln1_g': 2.791,
     'ln1_b': 2.84,
     'ln2_g': 8.207,
     'ln2_b': 8.223}
    for name, (base, spread) in spreads.items():
        noise = np.random.default_rng([zlib.crc32(name.encode()), seed]).standard_normal(out[name].shape)
        drawn = base * np.exp(spread * noise) if base else spread * noise
        out[name] = __import__('jax').numpy.asarray(drawn.astype(out[name].dtype))
    for name, factor in factors.items():
        out[name] = (out[name] * factor).astype(out[name].dtype)
    return out


_narrow_inputs_3 = third_inputs


def third_inputs(seed=0):

    out = dict(_narrow_inputs_3(seed))
    wider = {'m_norm_g': 4.08, 'h_norm_g': 4.07, 'ln2_g': 3.23, 'ln2_b': 3.23}
    for name, times in wider.items():
        mean = out[name].mean()
        out[name] = (mean + times * (out[name] - mean)).astype(out[name].dtype)
    return out


def setup_inputs(seed=0):
    out = dict(first_inputs(seed))
    for name, value in second_inputs(seed + 1).items():
        if name != "x":
            out[name + "_2"] = value
    for name, value in third_inputs(seed + 2).items():
        if name != "x":
            out[name + "_3"] = value
    return out


def reference(
    x, p, rel_bias, norm_mix, w_in, conv_dw_w, conv_dw_b, conv_ln_g, conv_ln_b, w_conv_out,
    cmp_pe_k, cmp_pe_v, w_ck1, w_ck2, w_cv1, w_cv2, w_attn_out, w_out, norm_ffn, w_up, ffn_dw_w,
    ffn_dw_b, w_down, norm_ple, w_ple_gate, w_ple, norm_final, norm_mix_g_2, norm_ffn_g_2,
    final_norm_g_2, hy_w_in_2, hy_b_in_2, hy_conv_w_2, hy_conv_b_2, hy_f_w1_2, hy_f_b1_2,
    hy_f_w2_2, hy_f_b2_2, hy_f_w3_2, hy_f_b3_2, hy_f_w4_2, hy_f_freq_2, hy_skip_2, hy_w_out_2,
    hy_b_out_2, rw_mu_2, rw_w_r_2, rw_w_k_2, rw_w_v_2, rw_w_o_2, rw_w0_2, rw_w1_2, rw_w2_2,
    rw_a0_2, rw_a1_2, rw_a2_2, rw_v0_2, rw_v1_2, rw_v2_2, rw_g1_2, rw_g2_2, rw_k_k_2, rw_k_a_2,
    rw_r_k_2, rw_ln_w_2, rw_ln_b_2, ff_w_up_2, ff_conv_w_2, ff_conv_b_2, ff_w_down_2, w_in_3,
    b_in_3, conv_w_3, conv_b_3, m_norm_g_3, lb_logits_3, h_norm_g_3, w_proj_a_3, w_proj_b_3,
    w_out_3, ln1_g_3, ln1_b_3, w_ffn_gate_3, w_ffn_up_3, w_ffn_down_3, ln2_g_3, ln2_b_3,
):
    x = first_block(
        x, p, rel_bias, norm_mix, w_in, conv_dw_w, conv_dw_b, conv_ln_g, conv_ln_b, w_conv_out,
        cmp_pe_k, cmp_pe_v, w_ck1, w_ck2, w_cv1, w_cv2, w_attn_out, w_out, norm_ffn, w_up,
        ffn_dw_w, ffn_dw_b, w_down, norm_ple, w_ple_gate, w_ple, norm_final,
    )
    x = second_block(
        x, norm_mix_g_2, norm_ffn_g_2, final_norm_g_2, hy_w_in_2, hy_b_in_2, hy_conv_w_2,
        hy_conv_b_2, hy_f_w1_2, hy_f_b1_2, hy_f_w2_2, hy_f_b2_2, hy_f_w3_2, hy_f_b3_2,
        hy_f_w4_2, hy_f_freq_2, hy_skip_2, hy_w_out_2, hy_b_out_2, rw_mu_2, rw_w_r_2, rw_w_k_2,
        rw_w_v_2, rw_w_o_2, rw_w0_2, rw_w1_2, rw_w2_2, rw_a0_2, rw_a1_2, rw_a2_2, rw_v0_2,
        rw_v1_2, rw_v2_2, rw_g1_2, rw_g2_2, rw_k_k_2, rw_k_a_2, rw_r_k_2, rw_ln_w_2, rw_ln_b_2,
        ff_w_up_2, ff_conv_w_2, ff_conv_b_2, ff_w_down_2,
    )
    return third_block(
        x, w_in_3, b_in_3, conv_w_3, conv_b_3, m_norm_g_3, lb_logits_3, h_norm_g_3, w_proj_a_3,
        w_proj_b_3, w_out_3, ln1_g_3, ln1_b_3, w_ffn_gate_3, w_ffn_up_3, w_ffn_down_3, ln2_g_3,
        ln2_b_3,
    )


_drawn_inputs = setup_inputs


def setup_inputs(seed=0):
    import zlib

    import numpy as np

    out = dict(_drawn_inputs(seed))
    spreads = {}
    factors = {}
    for name, (base, spread) in spreads.items():
        noise = np.random.default_rng([zlib.crc32(name.encode()), seed]).standard_normal(out[name].shape)
        drawn = base * np.exp(spread * noise) if base else spread * noise
        out[name] = jnp.asarray(drawn.astype(out[name].dtype))
    for name, factor in factors.items():
        out[name] = (out[name] * factor).astype(out[name].dtype)
    return out
```

```python
from contextlib import ExitStack

import numpy as np

import concourse.bass as bass
from concourse import mybir

ALU = mybir.AluOpType
ACT = mybir.ActivationFunctionType
F32 = mybir.dt.float32
U32 = mybir.dt.uint32
AX = mybir.AxisListType.X

P = 128
SEQ = 512
D = 1024
KT = D // P
JT = SEQ // P
SLOTS = 2
CHUNK = 4096
FF = 2816
FT = FF // P
UP_CHUNKS = FT // 2
DOWN_CHUNKS = -(-FT // 4)
EPS = 1e-6
NEG = -1e30


class Link:

    def __init__(self, eng, sem):
        self.eng, self.sem, self.base, self.n = eng, sem, 0, 0

    def start(self, base):
        self.base, self.n = base, 0

    def mark(self, ins):
        ins.then_inc(self.sem, 1)
        self.n += 1
        return self.n

    def settle(self, upto=None):
        self.eng.wait_ge(self.sem, self.base + (self.n if upto is None else upto))

    def __call__(self, ins):
        self.mark(ins)
        self.settle()


def pairs(eng, count, body):
    if count >= 4:
        with eng.Fori(0, count // 2) as i:
            body(0, i)
            body(1, i)
    else:
        for i in range(count // 2):
            body(0, i)
            body(1, i)
    if count % 2:
        body(0, count // 2)


class Core:

    def __init__(self, nc, aps, layout, ctx):
        self.nc, self.aps, self.layout, self.ctx = nc, aps, layout, ctx
        self.weights = aps["weights"]
        self.total = self.weights.shape[0]
        self.first = 0
        self.cleared = []
        sb = self.sb
        self.ring = sb("weight_ring", [P, SLOTS, CHUNK])
        self.cols = sb("columns_sb", list(aps["columns"].shape))
        self.const = sb("constants_sb", list(aps["constants"].shape))
        self.banks = ctx.enter_context(nc.psum_tensor("banks", [P, 8, 512], F32))
        self.landed = [ctx.enter_context(nc.semaphore(f"weights_landed_{s}")) for s in range(SLOTS)]
        self.x = sb("residual", [P, KT, SEQ])
        self.hT = sb("normed", [P, KT, SEQ])

    def sb(self, name, shape, dt=F32, ctx=None):
        return (ctx or self.ctx).enter_context(self.nc.sbuf_tensor(name, shape, dt))

    def col(self, name, i=0, n=1):
        at = self.layout["columns"][name][0]
        return self.cols[:, bass.ds(i + at, n)] if not isinstance(i, int) else self.cols[:, at + i:at + i + n]

    def con(self, name):
        at, n = self.layout["constants"][name]
        return self.const[:, at:at + n]

    def slot(self, p):
        return (self.first + p) % SLOTS

    def chunk(self, p, k):
        return self.ring[:, self.slot(p), :].rearrange("p (k n) -> p k n", k=k)

    def arrived(self, pe, p, i):
        pe.wait_ge(self.landed[self.slot(p)], 16 * (i + (self.first + p) // SLOTS + 1))

    def feed(self, sp, count, used, per=1, base=0):
        def load(p, i):
            n = self.first + p + 2 * i
            if isinstance(i, int) and n + SLOTS >= self.total:
                return
            sp.wait_ge(used, base + per * (p + 2 * i + 1))
            sp.dma_start(self.ring[:, self.slot(p), :], self.weights[n + SLOTS]).then_inc(self.landed[self.slot(p)], 16)

        if self.first + count + SLOTS > self.total:
            for c in range(count):
                load(c % 2, c // 2)
        else:
            pairs(sp, count, load)


class Shared:
    pass


def stage(G, name, ctx, *semaphores):
    S = {s: G.nc.alloc_semaphore(f"{name}_{s}") for s in semaphores}

    def retire():
        for sem in G.cleared:
            G.nc.release_semaphore(sem)
        G.cleared = list(S.values())
        for sem in G.cleared:
            G.nc.gpsimd.sem_clear(sem)

    ctx.callback(retire)
    return S


def rms_act(act, G, S, sq):
    for k in range(KT):
        act.activation(sq[:, k, :], G.x[:, k, :], ACT.Square).then_inc(S["squared"], 1)


def rms_root(act, G, S, rstd):
    act.wait_ge(S["mean_done"], 1)
    act.activation(rstd[:, :], rstd[:, :], ACT.Sqrt).then_inc(S["root_done"], 1)


def rms_pe(pe, G, S, sq, bank):
    for k in range(KT):
        pe.wait_ge(S["squared"], k + 1)
        mm = pe.matmul(G.banks[:, bank, :], G.con("ones"), sq[:, k, :], start=(k == 0), stop=(k == KT - 1))
    mm.then_inc(S["summed"], 1)


def rms_dve(dve, G, S, rstd, bank, gain, out):
    dve.wait_ge(S["summed"], 1)
    dve.tensor_scalar(rstd[:, :], G.banks[:, bank, :], 1.0 / D, EPS, ALU.mult, ALU.add).then_inc(S["mean_done"], 1)
    dve.wait_ge(S["root_done"], 1)
    dve.reciprocal(rstd[:, :], rstd[:, :]).then_inc(S["rstd_done"], 1)
    dve.wait_ge(S["rstd_done"], 1)
    for k in range(KT):
        dve.scalar_tensor_tensor(out=out[:, k, :], in0=G.x[:, k, :], scalar=G.col(gain, k), in1=rstd[:, :],
                                 op0=ALU.mult, op1=ALU.mult).then_inc(S["h_ready"], 1)


RMS = ("squared", "summed", "mean_done", "root_done", "rstd_done", "h_ready")


def project(pe, G, p, m, bank, rhs, k_tiles=KT, first_wait=None):
    w = G.chunk(p, max(k_tiles, 4))
    for k in range(k_tiles):
        if first_wait is not None:
            pe.wait_ge(first_wait, k + 1)
        mm = pe.matmul(G.banks[:, bank, :], w[:, k, m * P:(m + 1) * P], rhs[:, k, :],
                       start=(k == 0), stop=(k == k_tiles - 1))
    return mm


def feed_forward(G, name, gain, taps, act_func, shift=0, keep=1.0):
    nc = G.nc
    conv = taps is not None
    with ExitStack() as ctx:
        S = stage(G, name, ctx, *RMS, "gate_val", "gate_free", "value_free", "centre", "tap", "activated", "hidden",
                  "down_used", "down_done", "added")
        gT = G.sb(name + "_hidden", [P, FT, SEQ], ctx=ctx)
        sq = gT[:, 0:KT, :]
        rstd = G.sb(name + "_rstd", [P, SEQ], ctx=ctx)
        gc = G.sb(name + "_gate", [P, 2, SEQ], ctx=ctx)
        vc = G.sb(name + "_value", [P, 2, SEQ], ctx=ctx)
        block = ctx.enter_context(nc.Block())

        @block.sync
        def _(sp):
            G.feed(sp, UP_CHUNKS, S["gate_val"], per=4)
            G.first += UP_CHUNKS
            G.feed(sp, DOWN_CHUNKS - 1, S["down_used"])
            G.first += DOWN_CHUNKS - 1
            G.feed(sp, 1, S["down_done"], per=KT)
            G.first -= DOWN_CHUNKS - 1
            G.first -= UP_CHUNKS

        @block.tensor
        def _(pe):
            if gain is not None:
                rms_pe(pe, G, S, sq, 7)

            def up(p, i):
                G.arrived(pe, p, i)
                for m in range(4):
                    pe.wait_ge(S["value_free"] if conv and m % 2 else S["gate_free"], 4 * i + 2 * p + m // 2 + 1)
                    project(pe, G, p, m, 4 * p + m, G.x if gain is None else G.hT).then_inc(S["gate_val"], 1)

            if gain is not None:
                pe.wait_ge(S["h_ready"], KT)
            pairs(pe, UP_CHUNKS, up)
            G.first += UP_CHUNKS
            pe.wait_ge(S["gate_free"], 4 + FT)
            if conv:
                pe.wait_ge(S["value_free"], 4 + FT)

            def down(p, i, start, tiles):
                G.arrived(pe, p, i)
                w = G.chunk(p, 4)
                c = 2 * i + p
                for kk in range(tiles):
                    pe.wait_ge(S["hidden"], 2 + 4 * c + kk + 1)
                    for m in range(KT):
                        rhs = gT[:, 4 * c + kk, :]
                        mm = pe.matmul(G.banks[:, m, :], w[:, kk, m * P:(m + 1) * P], rhs,
                                       start=start and kk == 0, stop=(tiles < 4 and kk == tiles - 1),
                                       skip_group_check=True)
                        if tiles < 4 and kk == tiles - 1:
                            mm.then_inc(S["down_done"], 1)
                if tiles == 4:
                    mm.then_inc(S["down_used"], 1)

            down(0, 0, True, 4)
            down(1, 0, False, 4)
            with pe.Fori(1, DOWN_CHUNKS // 2 - 1) as i:
                down(0, i, False, 4)
                down(1, i, False, 4)
            down(0, DOWN_CHUNKS // 2 - 1, False, 4)
            down(1, DOWN_CHUNKS // 2 - 1, False, FT - 4 * (DOWN_CHUNKS - 1))
            G.first -= UP_CHUNKS

        @block.scalar
        def _(act):
            if gain is not None:
                rms_act(act, G, S, sq)
                rms_root(act, G, S, rstd)

            def chunk(p, i):
                for h in range(2):
                    t = 4 * i + 2 * p + h
                    b = 4 * p + 2 * h
                    act.wait_ge(S["gate_val"], 8 * i + 4 * p + 2 * h + 2)
                    act.wait_ge(S["hidden"], t + 1)
                    if conv:
                        act.activation(gc[:, h, :], G.banks[:, b, :], ACT.Identity, bias=G.col(taps, 8 * t + 3),
                                       scale=G.col(taps, 8 * t + 2 - shift)).then_inc(S["centre"], 1)
                        act.activation(vc[:, h, :], G.banks[:, b + 1, :], ACT.Identity, bias=G.col(taps, 8 * t + 7),
                                       scale=G.col(taps, 8 * t + 6 - shift)).then_inc(S["centre"], 1)
                        act.wait_ge(S["gate_free"], 4 + t + 1)
                        act.activation(gc[:, h, :], gc[:, h, :], act_func).then_inc(S["activated"], 1)
                    else:
                        act.activation(gc[:, h, :], G.banks[:, b, :], act_func).then_inc(S["activated"], 1)

            pairs(act, UP_CHUNKS, chunk)

        @block.vector
        def _(dve):
            dve.sem_inc(S["gate_free"], 4)
            dve.sem_inc(S["value_free"], 4)
            dve.sem_inc(S["hidden"], 2)
            if gain is not None:
                rms_dve(dve, G, S, rstd, 7, gain, G.hT)
            n = SEQ
            if shift == 0:
                sides = [(0, slice(2, n), slice(0, n - 2)), (1, slice(1, n), slice(0, n - 1))]
            else:
                sides = [(0, slice(1, n), slice(0, n - 1)), (2, slice(0, n - 1), slice(1, n))]

            def chunk(p, i):
                for h in range(2):
                    t = 4 * i + 2 * p + h
                    b = 4 * p + 2 * h
                    if conv:
                        dve.wait_ge(S["centre"], 2 * t + 2)
                        for s, (tap, to, of) in enumerate(sides):
                            for q, buf in enumerate((gc, vc)):
                                if s == 1:
                                    dve.wait_ge(S["tap"], 2 * t + q + 1)
                                ins = dve.scalar_tensor_tensor(
                                    out=buf[:, h, to], in0=G.banks[:, b + q, of], scalar=G.col(taps, 8 * t + 4 * q + tap),
                                    in1=buf[:, h, to], op0=ALU.mult, op1=ALU.add)
                                if s == 0:
                                    ins.then_inc(S["tap"], 1)
                                else:
                                    ins.then_inc((S["gate_free"], S["value_free"])[q], 1)
                        dve.wait_ge(S["activated"], t + 1)
                        dve.wait_ge(S["value_free"], 4 + t + 1)
                        value = vc[:, h, :]
                    else:
                        dve.wait_ge(S["gate_val"], 2 * t + 2)
                        dve.wait_ge(S["activated"], t + 1)
                        value = G.banks[:, b + 1, :]
                    dve.tensor_tensor(gT[:, t, :], gc[:, h, :], value, ALU.mult).then_inc(S["hidden"], 1)
                    if not conv:
                        dve.wait_ge(S["hidden"], 2 + t + 1)
                        dve.sem_inc(S["gate_free"], 1)

            pairs(dve, UP_CHUNKS, chunk)
            for m in range(KT):
                dve.wait_ge(S["down_done"], m + 1)
                dve.scalar_tensor_tensor(out=G.x[:, m, :], in0=G.x[:, m, :], scalar=keep, in1=G.banks[:, m, :],
                                         op0=ALU.mult, op1=ALU.add).then_inc(S["added"], 1)

        G.first += UP_CHUNKS + DOWN_CHUNKS



class Layout:
    def __init__(self):
        self.chunks, self.column_parts, self.columns, self.n_columns = [], [], {}, 0
        self.constant_parts, self.constants, self.n_constants = [], {}, 0

    def chunk(self, *parts):
        c = np.zeros((P, CHUNK), np.float32)
        at = 0
        for part in parts:
            c[:part.shape[0], at:at + part.shape[1]] = part
            at += part.shape[1]
        assert at <= CHUNK
        self.chunks.append(c)

    def matrix(self, w):
        k = w.shape[0] // P
        return w.reshape(k, P, w.shape[1]).transpose(1, 0, 2).reshape(P, k * w.shape[1])

    def column_chunks(self, w, order=None):
        if order is not None:
            w = w[:, order]
        for c in range(0, w.shape[1], 512):
            self.chunk(self.matrix(w[:, c:c + 512]))

    def row_chunks(self, w):
        for r in range(0, w.shape[0], 512):
            self.chunk(self.matrix(w[r:r + 512]))

    def column(self, name, value):
        self.columns[name] = (self.n_columns, value.shape[1])
        c = np.zeros((P, value.shape[1]), np.float32)
        c[:value.shape[0]] = value
        self.column_parts.append(c)
        self.n_columns += value.shape[1]

    def vector(self, name, v):
        self.column(name, v.reshape(-1, P).T)

    def constant(self, name, value):
        self.constants[name] = (self.n_constants, value.shape[1])
        c = np.zeros((P, value.shape[1]), np.float32)
        c[:value.shape[0]] = value
        self.constant_parts.append(c)
        self.n_constants += value.shape[1]

    def up_order(self):
        t = np.arange(FT)
        return (np.stack([t, t + FT], 1).reshape(-1, 1) * P + np.arange(P)).reshape(-1)

    def ff_taps(self, name, w, b):
        four = np.concatenate([w, b[None]], 0).reshape(4, 2, FT, P)
        self.column(name, four.transpose(3, 2, 1, 0).reshape(P, FT * 8))



HEADS, GROUPS, DH = 8, 2, 64
PER_GROUP = HEADS // GROUPS
L_CMP, D_STRIDE = 32, 16
N_CMP = (SEQ - L_CMP) // D_STRIDE + 1
TAPS = 31
CT = 4
BIAS_W = 896
BIAS_ROW = 1024


def lay_first(L, a):
    w_in = a["w_in"][0]
    tile = lambda at, t: at + t * P + np.arange(P)
    q0, kv0, ng0, mg0 = 1024, 1536, 2304, 2328
    for c in range(2):
        L.column_chunks(w_in, np.concatenate([tile(0, 2 * c), tile(512, 2 * c), tile(0, 2 * c + 1), tile(512, 2 * c + 1)]))
    d = np.arange(DH)
    L.column_chunks(w_in, np.concatenate([q0 + (g * PER_GROUP + t) * DH + d for t in range(PER_GROUP) for g in range(GROUPS)]))
    L.column_chunks(w_in, np.concatenate([kv0 + (s * GROUPS + g) * DH + d for s in (0, 1) for g in range(GROUPS) for _ in range(2)]))
    L.column_chunks(w_in, np.concatenate([kv0 + s * P + np.arange(P) for s in (2, 4, 3, 5)]))
    L.column_chunks(w_in[:, mg0:mg0 + 2 * D])
    L.chunk(L.matrix(np.ascontiguousarray(w_in[:, ng0:ng0 + 24])), L.matrix(a["w_ck2"][0]), L.matrix(a["w_cv2"][0]))
    L.chunk(L.matrix(a["w_ck1"][0]))
    L.chunk(L.matrix(a["w_cv1"][0]))
    L.row_chunks(a["w_conv_out"][0])
    L.row_chunks(a["w_attn_out"][0])
    L.column_chunks(a["w_out"][0])
    L.column_chunks(a["w_up"][0], L.up_order())
    L.row_chunks(a["w_down"][0])
    L.column_chunks(a["w_ple_gate"][0])
    L.chunk(L.matrix(a["w_ple"][0]))
    L.vector("norm_mix", a["norm_mix"][0])
    L.column("conv_w", a["conv_dw_w"][0].reshape(TAPS, CT, P).transpose(2, 1, 0).reshape(P, CT * TAPS))
    for n in ("conv_dw_b", "conv_ln_g", "conv_ln_b", "norm_ffn", "norm_ple"):
        L.vector(n, a[n][0])
    L.vector("pe_k", a["cmp_pe_k"][0].reshape(-1))
    L.vector("pe_v", a["cmp_pe_v"][0].reshape(-1))
    L.ff_taps("ffn_taps", a["ffn_dw_w"][0], a["ffn_dw_b"][0])
    L.vector("norm_final", a["norm_final"])
    L.column("rel_bias", np.concatenate([a["rel_bias"], np.full((1, HEADS), NEG, np.float32)]))
    L.constant("seen_cmp", (np.arange(P) >= L_CMP - 1).astype(np.float32)[:, None])


def bucket_rows():
    n = 511 - np.arange(BIAS_ROW)
    m = np.maximum(n, 0)
    far = 16 + (np.log(np.maximum(m, 16).astype(np.float32) / np.float32(16)) / np.float32(np.log(8.0)) * np.float32(16)).astype(np.int32)
    b = np.where(m < 16, m, np.minimum(far, 31))
    b = np.where(n < 0, 32, b)
    return (np.arange(33)[:, None] == b[None]).astype(np.float32)


def bias_tiles(G, W):
    nc = G.nc
    rows_dram = nc.dram_tensor("bias_rows", [HEADS, 2, BIAS_ROW], F32, kind="Internal")
    with ExitStack() as ctx:
        S = stage(G, "bias", ctx, "loaded", "looked_up", "copied", "stored", "spread")
        onehot = G.sb("bucket_onehot", [33, BIAS_ROW], ctx=ctx)
        rows = G.sb("bias_rows_sb", [HEADS, BIAS_ROW], ctx=ctx)
        block = ctx.enter_context(nc.Block())

        @block.sync
        def _(sp):
            sp.dma_start(onehot[:, :], G.aps["buckets"]).then_inc(S["loaded"], 16)
            sp.wait_ge(S["copied"], 2)
            for c in range(2):
                sp.dma_start(rows_dram.ap()[:, c, :], rows[:, :]).then_inc(S["stored"], 16)
            sp.wait_ge(S["stored"], 32)
            for h in range(HEADS):
                sp.dma_start(W[:, h, :], bass.AP(tensor=rows_dram, offset=h * 2 * BIAS_ROW + P - 1,
                                                 ap=[[BIAS_ROW - P // 2, 2], [-1, P // 2], [1, BIAS_W]])).then_inc(S["spread"], 16)
            sp.wait_ge(S["spread"], 16 * HEADS)

        @block.tensor
        def _(pe):
            pe.wait_ge(S["loaded"], 16)
            for n in range(2):
                pe.matmul(G.banks[0:HEADS, n, :], G.col("rel_bias", 0, HEADS)[0:33, :], onehot[:, n * 512:(n + 1) * 512],
                          start=True, stop=True).then_inc(S["looked_up"], 1)

        @block.scalar
        def _(act):
            for n in range(2):
                act.wait_ge(S["looked_up"], n + 1)
                act.activation(rows[:, n * 512:(n + 1) * 512], G.banks[0:HEADS, n, :], ACT.Copy).then_inc(S["copied"], 1)


def in_projection(G, T):
    nc = G.nc
    with ExitStack() as ctx:
        S = stage(G, "in", ctx, *RMS, "tile_done", "gate_done", "glu_done", "evacuated", "padded", "tap_done")
        sq = T.mgT[:, 0:KT, :]
        rstd = G.sb("in_rstd", [P, SEQ], ctx=ctx)
        sg = G.sb("in_glu_gate", [P, 2, SEQ], ctx=ctx)
        block = ctx.enter_context(nc.Block())
        STRAIGHT, MERGE = 5, 4

        @block.sync
        def _(sp):
            G.feed(sp, STRAIGHT, S["tile_done"], per=4)
            G.first += STRAIGHT
            G.feed(sp, MERGE, S["tile_done"], per=4, base=4 * STRAIGHT)
            G.first -= STRAIGHT

        @block.tensor
        def _(pe):
            rms_pe(pe, G, S, sq, 7)
            for c in range(STRAIGHT):
                p, i = c % 2, c // 2
                G.arrived(pe, p, i)
                if c in (2, 3):
                    pe.wait_ge(S["glu_done"], 2 * (c - 1))
                if c == 4:
                    pe.wait_ge(S["evacuated"], 4)
                for m in range(4 if c < 4 else 2):
                    project(pe, G, p, m, 4 * p + m, G.hT, first_wait=S["h_ready"] if c == 0 and m == 0 else None)\
                        .then_inc(S["tile_done"], 1)
            w = G.chunk(p, KT)
            for j in range(JT):
                for k in range(KT):
                    mm = pe.matmul(G.banks[:, 4 * p + 2 + j // 2, (j % 2) * 256:(j % 2) * 256 + 256],
                                   G.hT[:, k, j * P:(j + 1) * P], w[:, k, 256:512], start=(k == 0), stop=(k == KT - 1))
                if j % 2:
                    mm.then_inc(S["tile_done"], 1)
            G.first += STRAIGHT

            def merge(p, i):
                G.arrived(pe, p, i)
                pe.wait_ge(S["evacuated"], 8 * i + 4 * p + 8)
                for m in range(4):
                    project(pe, G, p, m, 4 * ((STRAIGHT + p) % 2) + m, G.hT).then_inc(S["tile_done"], 1)

            pairs(pe, MERGE, merge)
            G.first -= STRAIGHT

        @block.scalar
        def _(act):
            rms_act(act, G, S, sq)
            rms_root(act, G, S, rstd)
            for c in range(2):
                for h in range(2):
                    act.wait_ge(S["tile_done"], 4 * c + 2 * h + 2)
                    if c:
                        act.wait_ge(S["glu_done"], h + 1)
                    act.activation(sg[:, h, :], G.banks[:, 4 * c + 2 * h + 1, :], ACT.Sigmoid).then_inc(S["gate_done"], 1)
            for m in range(4):
                act.wait_ge(S["tile_done"], 8 + m + 1)
                act.activation(T.qT[:, m, :], G.banks[:, m, :], ACT.Copy).then_inc(S["evacuated"], 1)
            for m in range(4):
                act.wait_ge(S["tile_done"], 12 + m + 1)
                for odd in range(2):
                    rows = slice(64 * odd, 64 * odd + 64)
                    of = bass.AP(tensor=G.banks[rows, 4 + m, odd:odd + 1].tensor, offset=G.banks[rows, 4 + m, odd:odd + 1].offset,
                                 ap=[G.banks[rows, 4 + m, :].ap[0], [2, L_CMP // 2], [D_STRIDE, N_CMP]])
                    ins = act.activation(T.kcol[rows, m // 2, :, m % 2, 0:N_CMP], of, ACT.Copy)
                ins.then_inc(S["evacuated"], 1)
            for m in range(2):
                act.wait_ge(S["tile_done"], 16 + m + 1)
                act.activation(T.ksw[:, m, :], G.banks[:, m, :], ACT.Copy).then_inc(S["evacuated"], 1)
            for m in range(2):
                act.wait_ge(S["tile_done"], 18 + m + 1)
                act.activation(T.vtok[:, 2 * m:2 * m + 2, :], G.banks[:, 2 + m, :].rearrange("p (j n) -> p j n", j=2),
                               ACT.Copy).then_inc(S["evacuated"], 1)

            def merge(p, i):
                for m in range(4):
                    act.wait_ge(S["tile_done"], 20 + 8 * i + 4 * p + m + 1)
                    act.activation(T.mgT[:, 8 * i + 4 * p + m, :], G.banks[:, 4 * ((STRAIGHT + p) % 2) + m, :], ACT.Sigmoid)\
                       .then_inc(S["evacuated"], 1)

            pairs(act, MERGE, merge)

        @block.vector
        def _(dve):
            dve.memset(T.apad[:, :, 0:TAPS - 1], 0.0).then_inc(S["padded"], 1)
            rms_dve(dve, G, S, rstd, 7, "norm_mix", G.hT)
            for c in range(2):
                for h in range(2):
                    dve.wait_ge(S["gate_done"], 2 * c + h + 1)
                    dve.tensor_tensor(T.apad[:, 2 * c + h, TAPS - 1:], G.banks[:, 4 * c + 2 * h, :], sg[:, h, :], ALU.mult)\
                       .then_inc(S["glu_done"], 1)
            for s, name in enumerate(("pe_k", "pe_v")):
                for g in range(GROUPS):
                    dve.tensor_copy(T.kcol[:, s, :, g, N_CMP], G.col(name, 0, L_CMP // 2)).then_inc(S["padded"], 1)
            dve.wait_ge(S["padded"], 1)
            dve.wait_ge(S["glu_done"], 4)
            done = Link(dve, S["tap_done"])
            for tap in range(TAPS):
                for t in range(CT):
                    of, w = T.apad[:, t, tap:tap + SEQ], G.col("conv_w", t * TAPS + tap)
                    if tap == 0:
                        done.mark(dve.tensor_scalar(T.conv[:, t, :], of, w, G.col("conv_dw_b", t), ALU.mult, ALU.add))
                    else:
                        done.settle(done.n - CT + 1)
                        done.mark(dve.scalar_tensor_tensor(out=T.conv[:, t, :], in0=of, scalar=w, in1=T.conv[:, t, :],
                                                           op0=ALU.mult, op1=ALU.add))

        G.first += STRAIGHT + MERGE


def compress_and_convolution(G, T):
    nc = G.nc
    with ExitStack() as ctx:
        S = stage(G, "cmp", ctx, "gates_sum", "gates_done", "w2_copied", "hidden_sum", "hidden_bias",
                  "hidden_done", "kv_sum", "kv_done", "summed", "mean_done", "centred", "squared", "squares_summed", "var_done",
                  "root_done", "rstd_done", "scaled", "silu_done", "out_done", "mixed")
        w2 = G.sb("cmp_w2", [P, 2, 2, DH], ctx=ctx)
        bias = G.sb("cmp_bias", [P, 2, 4], ctx=ctx)
        hid = G.sb("cmp_hidden", [P, 2, 2, GROUPS, N_CMP], ctx=ctx)
        sq = G.sb("conv_squares", [P, CT, SEQ], ctx=ctx)
        mu = G.sb("conv_mean", [P, SEQ], ctx=ctx)
        rstd = G.sb("conv_rstd", [P, SEQ], ctx=ctx)
        block = ctx.enter_context(nc.Block())
        half = [G.banks[:, 1 + s, 0:4 * 32].rearrange("p (m g c) -> p m g c", m=2, g=GROUPS) for s in range(2)]

        @block.sync
        def _(sp):
            sp.wait_ge(S["w2_copied"], 2)
            G.feed(sp, 1, S["gates_sum"])
            G.first += 1
            G.feed(sp, 2, S["hidden_sum"])
            G.first += 2
            G.feed(sp, 1, S["out_done"], per=KT)
            G.first -= 3

        @block.tensor
        def _(pe):
            for t in range(CT):
                mm = pe.matmul(G.banks[:, 5, :], G.con("ones"), T.conv[:, t, :], start=(t == 0), stop=(t == CT - 1))
            mm.then_inc(S["summed"], 1)
            G.arrived(pe, 0, 0)
            w = G.ring[:, G.slot(0), 0:KT * 24].rearrange("p (k n) -> p k n", k=KT)
            for j in range(JT):
                for k in range(KT):
                    mm = pe.matmul(G.banks[:, 0, j * 24:(j + 1) * 24], G.hT[:, k, j * P:(j + 1) * P], w[:, k, :],
                                   start=(k == 0), stop=(k == KT - 1))
            mm.then_inc(S["gates_sum"], 1)
            for s in range(2):
                G.arrived(pe, (1 + s) % 2, (1 + s) // 2)
                w = G.chunk((1 + s) % 2, 16)
                for m in range(2):
                    for l in range(16):
                        mm = pe.matmul(G.banks[:, 1 + s, m * 64:(m + 1) * 64], w[:, l, m * P:(m + 1) * P],
                                       T.kcol[:, s, l, :, :], start=(l == 0), stop=(l == 15))
                    if m:
                        mm.then_inc(S["hidden_sum"], 1)
            pe.wait_ge(S["centred"], CT)
            for t in range(CT):
                pe.wait_ge(S["squared"], t + 1)
                mm = pe.matmul(G.banks[:, 6, :], G.con("ones"), sq[:, t, :], start=(t == 0), stop=(t == CT - 1))
            mm.then_inc(S["squares_summed"], 1)
            pe.wait_ge(S["hidden_done"], 8)
            pe.wait_ge(S["w2_copied"], 2)
            for g in range(GROUPS):
                for m in range(2):
                    pe.matmul(G.banks[g * DH:(g + 1) * DH, 3, 0:N_CMP], w2[:, 0, m, :], hid[:, 0, m, g, :],
                              start=(m == 0), stop=(m == 1))
                for m in range(2):
                    mm = pe.matmul(G.banks[0:N_CMP, 4, g * DH:(g + 1) * DH], hid[:, 1, m, g, :], w2[:, 1, m, :],
                                   start=(m == 0), stop=(m == 1))
            mm.then_inc(S["kv_sum"], 1)
            G.arrived(pe, 1, 1)
            pe.wait_ge(S["silu_done"], CT)
            pe.wait_ge(S["kv_done"], 2)
            for m in range(KT):
                project(pe, G, 1, m, m, sq, k_tiles=CT).then_inc(S["out_done"], 1)

        @block.scalar
        def _(act):
            act.wait_ge(G.landed[G.slot(0)], 16 * (G.first // SLOTS + 1))
            for s in range(2):
                at = KT * 24 + s * 2 * DH
                act.activation(w2[:, s, :, :], G.ring[:, G.slot(0), at:at + 2 * DH].rearrange("p (m n) -> p m n", m=2), ACT.Copy)\
                   .then_inc(S["w2_copied"], 1)
            act.wait_ge(S["gates_sum"], 1)
            act.activation(T.gates[:, :, :], G.banks[:, 0, 0:JT * 24].rearrange("p (j n) -> p j n", j=JT), ACT.Sigmoid)\
               .then_inc(S["gates_done"], 1)
            act.wait_ge(S["centred"], CT)
            for t in range(CT):
                act.activation(sq[:, t, :], T.conv[:, t, :], ACT.Square).then_inc(S["squared"], 1)
            for s in range(2):
                act.wait_ge(S["hidden_sum"], s + 1)
                act.activation(bias[:, s, :].rearrange("p (m g) -> p m g", m=2), half[s][:, :, :, N_CMP], ACT.Copy)\
                   .then_inc(S["hidden_bias"], 1)
                act.wait_ge(S["hidden_bias"], s + 1)
                for m in range(2):
                    for g in range(GROUPS):
                        act.activation(hid[:, s, m, g, :], half[s][:, m, g, 0:N_CMP], ACT.Gelu_apprx_tanh,
                                       bias=bias[:, s, 2 * m + g:2 * m + g + 1]).then_inc(S["hidden_done"], 1)
            act.wait_ge(S["var_done"], 1)
            act.activation(rstd[:, :], rstd[:, :], ACT.Sqrt).then_inc(S["root_done"], 1)
            act.wait_ge(S["kv_sum"], 1)
            act.activation(T.kcT[:, :], G.banks[:, 3, 0:N_CMP], ACT.Copy).then_inc(S["kv_done"], 1)
            act.activation(T.vc[0:N_CMP, :], G.banks[0:N_CMP, 4, 0:GROUPS * DH], ACT.Copy).then_inc(S["kv_done"], 1)
            for t in range(CT):
                act.wait_ge(S["scaled"], t + 1)
                act.activation(sq[:, t, :], T.conv[:, t, :], ACT.Silu, bias=G.col("conv_ln_b", t), scale=G.col("conv_ln_g", t))\
                   .then_inc(S["silu_done"], 1)

        @block.vector
        def _(dve):
            dve.wait_ge(S["summed"], 1)
            dve.tensor_scalar(mu[:, :], G.banks[:, 5, :], 1.0 / (CT * P), None, ALU.mult).then_inc(S["mean_done"], 1)
            dve.wait_ge(S["mean_done"], 1)
            for t in range(CT):
                dve.tensor_tensor(T.conv[:, t, :], T.conv[:, t, :], mu[:, :], ALU.subtract).then_inc(S["centred"], 1)
            dve.wait_ge(S["gates_done"], 1)
            seen = T.gates[:, 0, :].rearrange("p (h b) -> p h b", b=3)[:, :, 0]
            dve.tensor_scalar(seen, seen, G.con("seen_cmp"), None, ALU.mult).then_inc(S["gates_done"], 1)
            dve.wait_ge(S["squares_summed"], 1)
            dve.tensor_scalar(rstd[:, :], G.banks[:, 6, :], 1.0 / (CT * P), EPS, ALU.mult, ALU.add).then_inc(S["var_done"], 1)
            dve.wait_ge(S["root_done"], 1)
            dve.reciprocal(rstd[:, :], rstd[:, :]).then_inc(S["rstd_done"], 1)
            dve.wait_ge(S["rstd_done"], 1)
            for t in range(CT):
                dve.tensor_tensor(T.conv[:, t, :], T.conv[:, t, :], rstd[:, :], ALU.mult).then_inc(S["scaled"], 1)
            for m in range(KT):
                dve.wait_ge(S["out_done"], m + 1)
                dve.tensor_tensor(G.hT[:, m, :], G.banks[:, m, :], T.mgT[:, m, :], ALU.mult).then_inc(S["mixed"], 1)

        G.first += 4


def attention(G, T):
    nc = G.nc
    CMP, SLC, WIN = range(3)
    units = [(j, b, g) for j in range(JT) for b in (SLC, WIN, CMP) for g in range(GROUPS)]
    U = len(units)
    width = lambda u: N_CMP if units[u][1] == CMP else P * (units[u][0] + 1)
    with ExitStack() as ctx:
        S = stage(G, "attn", ctx, "staged", "scored", "biased", "max_done", "negated", "expd", "turned", "copied", "weighed",
                  "inverted", "coefficient", "combined")
        qs = G.sb("attn_q", [P, SEQ], ctx=ctx)
        sc = G.sb("attn_scores", [P, 2, SEQ], ctx=ctx)
        pT = G.sb("attn_probs_T", [P, 2, SEQ], ctx=ctx)
        stat = G.sb("attn_stats", [P, 4, U], ctx=ctx)
        top, bottom, total, coef = (stat[:, n, :] for n in range(4))
        block = ctx.enter_context(nc.Block())
        SCORE, TURN, OUT = 0, 2, 4

        @block.tensor
        def _(pe):
            def scores(u, i):
                j, b, g = units[u]
                rows = slice(g * DH, (g + 1) * DH)
                if u == 0:
                    pe.wait_ge(S["staged"], i + 1)
                if u >= 2:
                    pe.wait_ge(S["biased"], U * i + u - 1)
                keys = T.kcT[rows, :] if b == CMP else T.ksw[rows, b - 1, 0:width(u)]
                pe.matmul(G.banks[:, SCORE + u % 2, 0:width(u)], qs[rows, j * P:(j + 1) * P], keys, start=True, stop=True)\
                  .then_inc(S["scored"], 1)

            def turn(u, i):
                pe.wait_ge(S["expd"], U * i + u + 1)
                if u >= 2:
                    pe.wait_ge(S["copied"], U * i + u - 1)
                n = width(u)
                for at in range(0, n, P):
                    w = min(P, n - at)
                    mm = pe.transpose(G.banks[0:w, TURN + u % 2, at:at + P], sc[:, u % 2, at:at + w], G.con("ident"))
                mm.then_inc(S["turned"], 1)

            def values(u, i):
                j, b, g = units[u]
                pe.wait_ge(S["copied"], U * i + u + 1)
                if u >= 2:
                    pe.wait_ge(S["combined"], U * i + u)
                out = G.banks[:, OUT + u % 2, 0:DH]
                cols = slice(g * DH, (g + 1) * DH)
                if b == CMP:
                    pe.matmul(out, pT[0:N_CMP, u % 2, 0:P], T.vc[0:N_CMP, cols], start=True, stop=True).then_inc(S["weighed"], 1)
                else:
                    for s in range(j + 1):
                        at = (b - 1) * P + g * DH
                        mm = pe.matmul(out, pT[:, u % 2, s * P:(s + 1) * P], T.vtok[:, s, at:at + DH],
                                       start=(s == 0), stop=(s == j))
                    mm.then_inc(S["weighed"], 1)

            with pe.Fori(0, PER_GROUP) as i:
                for u in range(U + 2):
                    if u < U:
                        scores(u, i)
                    if 1 <= u <= U:
                        turn(u - 1, i)
                    if u >= 2:
                        values(u - 2, i)

        @block.scalar
        def _(act):
            def exps(u, i):
                act.wait_ge(S["negated"], U * i + u + 1)
                s = sc[:, u % 2, 0:width(u)]
                act.activation(s, s, ACT.Exp, bias=bottom[:, u:u + 1], accum_out=total[:, u:u + 1]).then_inc(S["expd"], 1)

            def copy(u, i):
                act.wait_ge(S["turned"], U * i + u + 1)
                if u >= 2:
                    act.wait_ge(S["weighed"], U * i + u - 1)
                j, b, g = units[u]
                rows, n = (N_CMP, P) if b == CMP else (P, width(u))
                act.activation(pT[0:rows, u % 2, 0:n], G.banks[0:rows, TURN + u % 2, 0:n], ACT.Copy).then_inc(S["copied"], 1)

            with act.Fori(0, PER_GROUP) as i:
                act.wait_ge(S["combined"], U * i + 1)
                act.activation(qs[:, :], T.qT[:, i, :], ACT.Copy).then_inc(S["staged"], 1)
                for u in range(U + 1):
                    if u < U:
                        exps(u, i)
                    if u >= 1:
                        copy(u - 1, i)

        @block.vector
        def _(dve):
            dve.sem_inc(S["combined"], 1)

            def bias(u, i):
                j, b, g = units[u]
                dve.wait_ge(S["scored"], U * i + u + 1)
                if u >= 2:
                    dve.wait_ge(S["turned"], U * i + u - 1)
                if b == CMP:
                    y = 3 * P + L_CMP - 1 - j * P
                    w = T.W[:, g * PER_GROUP + i, y:y + D_STRIDE * (N_CMP - 1) + 1:D_STRIDE]
                else:
                    w = T.W[:, g * PER_GROUP + i, (JT - 1 - j) * P:SEQ]
                s = sc[:, u % 2, 0:width(u)]
                dve.scalar_tensor_tensor(out=s, in0=G.banks[:, SCORE + u % 2, 0:width(u)], scalar=DH ** -0.5, in1=w,
                                         op0=ALU.mult, op1=ALU.add).then_inc(S["biased"], 1)
                dve.wait_ge(S["biased"], U * i + u + 1)
                dve.tensor_reduce(top[:, u:u + 1], s, AX, ALU.max).then_inc(S["max_done"], 1)
                dve.wait_ge(S["max_done"], U * i + u + 1)
                dve.tensor_scalar(bottom[:, u:u + 1], top[:, u:u + 1], -1.0, None, ALU.mult).then_inc(S["negated"], 1)

            def combine(u, i):
                j, b, g = units[u]
                head = g * PER_GROUP + i
                dve.wait_ge(S["weighed"], U * i + u + 1)
                dve.reciprocal(coef[:, u:u + 1], total[:, u:u + 1]).then_inc(S["inverted"], 1)
                dve.wait_ge(S["inverted"], U * i + u + 1)
                dve.tensor_scalar(coef[:, u:u + 1], coef[:, u:u + 1], T.gates[:, j, bass.ds(3 * head + b, 1)], None, ALU.mult)\
                   .then_inc(S["coefficient"], 1)
                dve.wait_ge(S["coefficient"], U * i + u + 1)
                o = T.o[:, j, bass.ds(head * DH, DH)]
                out = G.banks[:, OUT + u % 2, 0:DH]
                if b == SLC:
                    ins = dve.tensor_scalar(o, out, coef[:, u:u + 1], None, ALU.mult)
                else:
                    dve.wait_ge(S["combined"], U * i + u)
                    ins = dve.scalar_tensor_tensor(out=o, in0=out, scalar=coef[:, u:u + 1], in1=o, op0=ALU.mult, op1=ALU.add)
                ins.then_inc(S["combined"], 1)

            with dve.Fori(0, PER_GROUP) as i:
                for u in range(U + 2):
                    if u < U:
                        bias(u, i)
                    if u >= 2:
                        combine(u - 2, i)


def merge_branches(G, T):
    nc = G.nc
    with ExitStack() as ctx:
        S = stage(G, "mix", ctx, "turned", "copied", "attn_done", "gated", "mixed", "out_done", "added")
        oT = G.sb("mix_oT", [P, CT, SEQ], ctx=ctx)
        yg = G.sb("mix_gated", [P, 2, SEQ], ctx=ctx)
        block = ctx.enter_context(nc.Block())

        @block.sync
        def _(sp):
            G.feed(sp, 1, S["attn_done"], per=KT)
            G.first += 1
            G.feed(sp, 2, S["out_done"], per=4)
            G.first -= 1

        @block.tensor
        def _(pe):
            for t in range(CT):
                for j in range(JT):
                    mm = pe.transpose(G.banks[:, t, j * P:(j + 1) * P], T.o[:, j, t * P:(t + 1) * P], G.con("ident"))
                mm.then_inc(S["turned"], 1)
            G.arrived(pe, 0, 0)
            pe.wait_ge(S["copied"], CT)
            for m in range(KT):
                project(pe, G, 0, m, m, oT, k_tiles=CT).then_inc(S["attn_done"], 1)
            pe.wait_ge(S["mixed"], KT)
            for m in range(KT):
                if m % 4 == 0:
                    G.arrived(pe, 1 + m // 4, 0) if m == 0 else G.arrived(pe, 0, 1)
                project(pe, G, 1 if m < 4 else 0, m % 4, m, G.hT).then_inc(S["out_done"], 1)

        @block.scalar
        def _(act):
            for t in range(CT):
                act.wait_ge(S["turned"], t + 1)
                act.activation(oT[:, t, :], G.banks[:, t, :], ACT.Copy).then_inc(S["copied"], 1)

        @block.vector
        def _(dve):
            for m in range(KT):
                dve.wait_ge(S["attn_done"], m + 1)
                if m >= 2:
                    dve.wait_ge(S["mixed"], m - 1)
                dve.tensor_tensor(yg[:, m % 2, :], G.banks[:, m, :], T.mgT[:, KT + m, :], ALU.mult).then_inc(S["gated"], 1)
                dve.wait_ge(S["gated"], m + 1)
                dve.tensor_tensor(G.hT[:, m, :], G.hT[:, m, :], yg[:, m % 2, :], ALU.add).then_inc(S["mixed"], 1)
            for m in range(KT):
                dve.wait_ge(S["out_done"], m + 1)
                dve.tensor_tensor(G.x[:, m, :], G.x[:, m, :], G.banks[:, m, :], ALU.add).then_inc(S["added"], 1)

        G.first += 3


def layer_embedding(G):
    nc = G.nc
    with ExitStack() as ctx:
        S = stage(G, "ple", ctx, *RMS, "p_loaded", "gate_sum", "gate_done", "embedded", "gated", "added")
        pT = G.sb("ple_pT", [P, 2, SEQ], ctx=ctx)
        sg = G.sb("ple_gate", [P, KT, SEQ], ctx=ctx)
        rstd = G.sb("ple_rstd", [P, SEQ], ctx=ctx)
        block = ctx.enter_context(nc.Block())

        @block.sync
        def _(sp):
            sp.dma_start(pT[:, :, :], G.aps["pT"].rearrange("(k p) n -> p k n", p=P)).then_inc(S["p_loaded"], 16)
            G.feed(sp, 2, S["gate_sum"], per=4)
            G.first += 2
            G.feed(sp, 1, S["embedded"], per=KT)
            G.first -= 2

        @block.tensor
        def _(pe):
            rms_pe(pe, G, S, sg, 7)
            for m in range(KT):
                if m % 4 == 0:
                    G.arrived(pe, m // 4, 0)
                if m == 7:
                    pe.wait_ge(S["h_ready"], KT)
                project(pe, G, m // 4, m % 4, m, G.hT, first_wait=S["h_ready"] if m == 0 else None).then_inc(S["gate_sum"], 1)
            pe.wait_ge(S["p_loaded"], 16)
            G.arrived(pe, 0, 1)
            for m in range(KT):
                pe.wait_ge(S["gate_done"], m + 1)
                project(pe, G, 0, m, m, pT, k_tiles=2).then_inc(S["embedded"], 1)

        @block.scalar
        def _(act):
            rms_act(act, G, S, sg)
            rms_root(act, G, S, rstd)
            for m in range(KT):
                act.wait_ge(S["gate_sum"], m + 1)
                act.activation(sg[:, m, :], G.banks[:, m, :], ACT.Sigmoid).then_inc(S["gate_done"], 1)

        @block.vector
        def _(dve):
            rms_dve(dve, G, S, rstd, 7, "norm_ple", G.hT)
            for m in range(KT):
                dve.wait_ge(S["embedded"], m + 1)
                dve.tensor_tensor(sg[:, m, :], sg[:, m, :], G.banks[:, m, :], ALU.mult).then_inc(S["gated"], 1)
                dve.wait_ge(S["gated"], m + 1)
                dve.tensor_tensor(G.x[:, m, :], G.x[:, m, :], sg[:, m, :], ALU.add).then_inc(S["added"], 1)

        G.first += 3


def norm_in_place(G, name, gain):
    nc = G.nc
    with ExitStack() as ctx:
        S = stage(G, name, ctx, *RMS)
        sq = G.sb(name + "_squares", [P, KT, SEQ], ctx=ctx)
        rstd = G.sb(name + "_rstd", [P, SEQ], ctx=ctx)
        block = ctx.enter_context(nc.Block())

        @block.tensor
        def _(pe):
            rms_pe(pe, G, S, sq, 7)

        @block.scalar
        def _(act):
            rms_act(act, G, S, sq)
            rms_root(act, G, S, rstd)

        @block.vector
        def _(dve):
            rms_dve(dve, G, S, rstd, 7, gain, G.x)


def first_block(G):
    with ExitStack() as ctx:
        T = Shared()
        T.W = G.sb("bias_tiles", [P, HEADS, BIAS_W], ctx=ctx)
        T.qT = G.sb("qT", [P, PER_GROUP, SEQ], ctx=ctx)
        T.kcol = G.sb("compress_columns", [P, 2, L_CMP // 2, GROUPS, N_CMP + 1], ctx=ctx)
        T.ksw = G.sb("keys_T", [P, 2, SEQ], ctx=ctx)
        T.vtok = G.sb("values", [P, JT, 256], ctx=ctx)
        T.mgT = G.sb("merge_gates", [P, 2 * KT, SEQ], ctx=ctx)
        T.gates = G.sb("branch_gates", [P, JT, 3 * HEADS], ctx=ctx)
        T.kcT = G.sb("compressed_keys_T", [P, N_CMP], ctx=ctx)
        T.vc = G.sb("compressed_values", [P, GROUPS * DH], ctx=ctx)
        bias_tiles(G, T.W)
        with ExitStack() as conv:
            T.apad = G.sb("glu_padded", [P, CT, SEQ + TAPS - 1], ctx=conv)
            T.conv = G.sb("convolved", [P, CT, SEQ], ctx=conv)
            in_projection(G, T)
            compress_and_convolution(G, T)
        T.o = G.sb("attn_out", [P, JT, SEQ], ctx=ctx)
        attention(G, T)
        merge_branches(G, T)
    feed_forward(G, "ffn1", "norm_ffn", "ffn_taps", ACT.Gelu_apprx_tanh, 0)
    layer_embedding(G)
    norm_in_place(G, "final1", "norm_final")



FILTER = 64
EMB = 33
TWO_PI = 6.283185307179586
TURN_HI = 6.28125
TURN_LO = TWO_PI - TURN_HI
ROUND = 1.5 * 2.0 ** 23


def dft_tables():
    n, f = np.arange(SEQ), np.arange(SEQ)
    ang = 2 * np.pi * ((n[:, None] * f[None]) % (2 * SEQ)) / (2 * SEQ)
    last = np.where(n % 2 == 0, 1.0, -1.0)
    re, im = np.cos(ang), -np.sin(ang)
    im[:, 0] = last
    share = np.where(f == 0, 1.0, 2.0)[:, None] / (2 * SEQ)
    inv_re, inv_im = share * np.cos(ang).T, -share * np.sin(ang).T
    inv_im[0] = last / (2 * SEQ)
    return np.concatenate([re, im], 1).astype(np.float32), np.concatenate([inv_re, inv_im], 1).astype(np.float32)


def filter_tables():
    f = np.float32
    n = np.arange(SEQ, dtype=f)
    t = n / f(SEQ - 1)
    fr = np.linspace(1e-4, 15, 16, dtype=f)
    ang = f(2.0 * np.pi / SEQ) * n[:, None] * fr[None]
    z = np.concatenate([t[:, None], np.cos(ang), -np.sin(ang)], 1)
    deltas = np.abs(np.linspace(np.log(1e-2) / 1.5, np.log(1e-2) / 0.3, D, dtype=f))
    return np.ascontiguousarray(z.T), np.exp(-t[:, None] * deltas[None]).astype(f)


def second_extra():
    return {"decay": filter_tables()[1], "scan_masks": scan_masks()}


def lay_second(L, a):
    tile = lambda at, t: at + t * P + np.arange(P)
    wide = lambda v: np.concatenate([v, np.zeros((P - v.shape[0], v.shape[1]), np.float32)]) if v.shape[0] < P else v
    L.chunk(*(wide(v) for v in (filter_tables()[0], a["hy_f_w1"][0], a["hy_f_w2"][0], a["hy_f_w3"][0], a["hy_f_w4"][0])))
    order = np.concatenate([tile(at, t) for t in range(KT) for at in (D, 2 * D)])
    L.column_chunks(a["hy_w_in"][0], order)
    L.column_chunks(a["hy_w_in"][0][:, :D])
    for table in dft_tables():
        L.chunk(L.matrix(table))
    L.column_chunks(a["hy_w_out"][0])
    L.vector("hy_norm", a["norm_mix_g"][0])
    five = np.concatenate([a["hy_conv_w"][0], a["hy_conv_b"], a["hy_b_in"]]).reshape(5, 3 * KT, P)
    seq = [s * KT + t for t in range(KT) for s in (1, 2)] + list(range(KT))
    L.column("hy_conv", five[:, seq].transpose(2, 1, 0).reshape(P, 15 * KT))
    L.column("hy_filter", np.stack([a["hy_f_b1"][0], a["hy_f_b2"][0], a["hy_f_b3"][0], a["hy_f_freq"][0]], 1))
    L.vector("hy_skip", a["hy_skip"][0])
    L.vector("hy_b_out", a["hy_b_out"][0])
    lay_ff2(L, a, 0)
    lay_rwkv(L, a)
    lay_ff2(L, a, 1)
    L.vector("final_norm_2", a["final_norm_g"])


def lay_ff2(L, a, i):
    L.column_chunks(a["ff_w_up"][i], L.up_order())
    L.row_chunks(a["ff_w_down"][i])
    L.vector(f"ff_norm_{i}", a["norm_ffn_g"][i])
    L.ff_taps(f"ff_taps_{i}", a["ff_conv_w"][i], a["ff_conv_b"][i])


def hyena_filters(G, T):
    nc = G.nc
    with ExitStack() as ctx:
        S = stage(G, "filt", ctx, "decay_loaded", "layer_sum", "step", "sine_in", "sine_done", "filter_sum", "scaled", "added")
        decay = G.sb("filt_decay", [P, JT, D], ctx=ctx)
        arg = G.sb("filt_arg", [FILTER, 3, SEQ], ctx=ctx)
        scaled = G.sb("filt_scaled", [P, 2, 2, SEQ], ctx=ctx)
        block = ctx.enter_context(nc.Block())
        w = G.ring[:, G.slot(0), :]
        zT, w123, w4 = w[0:EMB, 0:SEQ], SEQ, SEQ + 3 * FILTER
        ROUNDS = [(j, half) for j in range(JT) for half in range(2)]

        @block.sync
        def _(sp):
            sp.dma_start(decay[:, :, :], G.aps["decay"].rearrange("(j p) n -> p j n", p=P)).then_inc(S["decay_loaded"], 16)
            G.feed(sp, 1, S["filter_sum"], per=2 * len(ROUNDS))

        @block.tensor
        def _(pe):
            G.arrived(pe, 0, 0)
            for n in range(3):
                if n:
                    pe.wait_ge(S["sine_done"], n)
                rows = EMB if n == 0 else FILTER
                pe.matmul(G.banks[0:FILTER, n, :], w[0:rows, w123 + n * FILTER:w123 + (n + 1) * FILTER],
                          zT if n == 0 else arg[:, 2, :], start=True, stop=True).then_inc(S["layer_sum"], 1)
            pe.wait_ge(S["sine_done"], 3)
            for n, (j, half) in enumerate(ROUNDS):
                if n >= 4:
                    pe.wait_ge(S["scaled"], 2 * (n - 3))
                for s in range(2):
                    at = w4 + s * D + half * 512
                    pe.matmul(G.banks[:, 2 * (n % 4) + s, :], arg[:, 2, j * P:(j + 1) * P], w[0:FILTER, at:at + 512],
                              start=True, stop=True).then_inc(S["filter_sum"], 1)

        @block.scalar
        def _(act):
            for n in range(3):
                act.wait_ge(S["sine_in"], n + 1)
                act.activation(arg[:, 2, :], arg[:, 0, :], ACT.Sin).then_inc(S["sine_done"], 1)

        @block.vector
        def _(dve):
            step = Link(dve, S["step"])
            freq = G.col("hy_filter", 3)[0:FILTER, :]
            a, turns = arg[:, 0, :], arg[:, 1, :]
            for n in range(3):
                dve.wait_ge(S["layer_sum"], n + 1)
                step(dve.tensor_scalar(a, G.banks[0:FILTER, n, :], G.col("hy_filter", n)[0:FILTER, :], freq, ALU.add, ALU.mult))
                step(dve.tensor_scalar(turns, a, 1.0 / TWO_PI, ROUND, ALU.mult, ALU.add))
                step(dve.tensor_scalar(turns, turns, -ROUND, None, ALU.add))
                step(dve.scalar_tensor_tensor(out=a, in0=turns, scalar=-TURN_HI, in1=a, op0=ALU.mult, op1=ALU.add))
                step(dve.scalar_tensor_tensor(out=a, in0=turns, scalar=-TURN_LO, in1=a, op0=ALU.mult, op1=ALU.add))
                dve.tensor_scalar(a, a, 3.1415925, -3.1415925, ALU.min, ALU.max).then_inc(S["sine_in"], 1)
            dve.wait_ge(S["decay_loaded"], 16)
            for n, (j, half) in enumerate(ROUNDS):
                cols = slice(half * 512, half * 512 + 512)
                if n >= 2:
                    dve.wait_ge(S["added"], 2 * n - 2)
                for s in range(2):
                    dve.wait_ge(S["filter_sum"], 2 * n + s + 1)
                    dve.tensor_tensor(scaled[:, n % 2, s, :], G.banks[:, 2 * (n % 4) + s, :], decay[:, j, cols], ALU.mult)\
                       .then_inc(S["scaled"], 1)
                dve.wait_ge(S["scaled"], 2 * n + 2)
                dve.tensor_tensor(T.ksum[:, j, cols], scaled[:, n % 2, 0, :], scaled[:, n % 2, 1, :], ALU.add).then_inc(S["added"], 1)
                dve.tensor_tensor(T.kdiff[:, j, cols], scaled[:, n % 2, 0, :], scaled[:, n % 2, 1, :], ALU.subtract)\
                   .then_inc(S["added"], 1)

        G.first += 1


def hyena_projection(G, T):
    nc = G.nc
    U_CHUNKS, X_CHUNKS = 4, 2
    with ExitStack() as ctx:
        S = stage(G, "hyin", ctx, *RMS, "edges", "tile_sum", "biased", "centre", "left", "right", "product")
        sq = T.uT
        rstd = G.sb("hyin_rstd", [P, SEQ], ctx=ctx)
        z = G.sb("hyin_z", [P, 8, SEQ + 2], ctx=ctx)
        c = G.sb("hyin_conv", [P, 4, SEQ], ctx=ctx)
        block = ctx.enter_context(nc.Block())

        @block.sync
        def _(sp):
            G.feed(sp, U_CHUNKS + X_CHUNKS, S["tile_sum"], per=4)

        @block.tensor
        def _(pe):
            rms_pe(pe, G, S, sq, 7)
            pe.wait_ge(S["h_ready"], KT)

            def chunk(p, i):
                G.arrived(pe, p, i)
                for m in range(4):
                    pe.wait_ge(S["biased"], 8 * i + 4 * p + m + 1)
                    project(pe, G, p, m, 4 * p + m, G.hT).then_inc(S["tile_sum"], 1)

            pairs(pe, U_CHUNKS + X_CHUNKS, chunk)

        @block.scalar
        def _(act):
            act.sem_inc(S["biased"], 8)
            rms_act(act, G, S, sq)
            rms_root(act, G, S, rstd)
            act.wait_ge(S["edges"], 1)

            def chunk(p, i):
                for m in range(4):
                    n = 8 * i + 4 * p + m
                    act.wait_ge(S["tile_sum"], n + 1)
                    act.wait_ge(S["right"], n + 1)
                    act.activation(z[:, 4 * p + m, 1:SEQ + 1], G.banks[:, 4 * p + m, :], ACT.Identity,
                                   bias=G.col("hy_conv", 5 * n + 4)).then_inc(S["biased"], 1)

            pairs(act, U_CHUNKS + X_CHUNKS, chunk)

        @block.vector
        def _(dve):
            dve.memset(z[:, :, 0:SEQ + 2:SEQ + 1], 0.0).then_inc(S["edges"], 1)
            dve.sem_inc(S["right"], 8)
            rms_dve(dve, G, S, rstd, 7, "hy_norm", G.hT)

            def convolve(p, i, m, n, to):
                b = z[:, 4 * p + m, :]
                dve.wait_ge(S["biased"], 8 + n + 1)
                dve.tensor_scalar(to, b[:, 1:SEQ + 1], G.col("hy_conv", 5 * n + 1), G.col("hy_conv", 5 * n + 3),
                                  ALU.mult, ALU.add).then_inc(S["centre"], 1)
                dve.wait_ge(S["centre"], n + 1)
                dve.scalar_tensor_tensor(out=to, in0=b[:, 0:SEQ], scalar=G.col("hy_conv", 5 * n), in1=to,
                                         op0=ALU.mult, op1=ALU.add).then_inc(S["left"], 1)
                dve.wait_ge(S["left"], n + 1)
                dve.scalar_tensor_tensor(out=to, in0=b[:, 2:SEQ + 2], scalar=G.col("hy_conv", 5 * n + 2), in1=to,
                                         op0=ALU.mult, op1=ALU.add).then_inc(S["right"], 1)

            def u_chunk(p, i):
                for m in range(4):
                    n = 8 * i + 4 * p + m
                    convolve(p, i, m, n, c[:, m, :])
                    if m % 2:
                        dve.wait_ge(S["right"], 8 + n + 1)
                        dve.tensor_tensor(T.uT[:, 4 * i + 2 * p + m // 2, :], c[:, m - 1, :], c[:, m, :], ALU.mult)\
                           .then_inc(S["product"], 1)
                        dve.wait_ge(S["product"], 4 * i + 2 * p + m // 2 + 1)

            pairs(dve, U_CHUNKS, u_chunk)
            for m in range(4 * X_CHUNKS):
                n = 4 * U_CHUNKS + m
                convolve(m // 4, U_CHUNKS // 2, m % 4, n, T.x0T[:, m, :])

        G.first += U_CHUNKS + X_CHUNKS


def hyena_convolution(G, T):
    nc = G.nc
    with ExitStack() as ctx:
        S = stage(G, "long", ctx, "turned", "copied", "last_sum", "last_done", "spectra", "u_copied", "step", "bank_free",
                  "back", "skipped", "gated", "out_done", "added")
        ut = G.sb("long_u", [P, JT, D], ctx=ctx)
        yr = G.sb("long_re", [P, 4, D], ctx=ctx)
        yi = G.sb("long_im", [P, 4, D], ctx=ctx)
        us = G.sb("long_us", [P, 2, 2, SEQ], ctx=ctx)
        tmp = G.sb("long_tmp", [P, 4, SEQ], ctx=ctx)
        last = G.sb("long_last", [1, D], ctx=ctx)
        block = ctx.enter_context(nc.Block())
        ROUNDS = [(f, half) for f in range(4) for half in range(2)]

        @block.sync
        def _(sp):
            G.feed(sp, 1, S["spectra"], per=len(ROUNDS))
            G.first += 1
            G.feed(sp, 1, S["back"], per=KT)
            G.first += 1
            G.feed(sp, 2, S["out_done"], per=4)
            G.first -= 2

        @block.tensor
        def _(pe):
            for t in range(KT):
                for j in range(JT):
                    mm = pe.transpose(G.banks[:, t, j * P:(j + 1) * P], T.uT[:, t, j * P:(j + 1) * P], G.con("ident"))
                mm.then_inc(S["turned"], 1)
            G.arrived(pe, 0, 0)
            w = G.chunk(0, 4)
            pe.wait_ge(S["copied"], KT)
            for half in range(2):
                for s in range(4):
                    mm = pe.matmul(G.banks[0:1, half, :], w[:, s, SEQ:SEQ + 1], T.ksum[:, s, half * 512:half * 512 + 512],
                                   start=(s == 0), stop=(s == 3))
                mm.then_inc(S["last_sum"], 1)
            pe.wait_ge(S["last_done"], 2)
            for n, (f, half) in enumerate(ROUNDS):
                if n >= 2:
                    pe.wait_ge(S["bank_free"], n - 1)
                cols = slice(half * 512, half * 512 + 512)
                for b, (at, of) in enumerate(((0, ut), (SEQ, ut), (0, T.ksum), (SEQ, T.kdiff))):
                    for s in range(4):
                        mm = pe.matmul(G.banks[:, 4 * (n % 2) + b, :], w[:, s, at + f * P:at + (f + 1) * P], of[:, s, cols],
                                       start=(s == 0), stop=(s == 3))
                mm.then_inc(S["spectra"], 1)
            G.arrived(pe, 1, 0)
            w = G.chunk(1, 4)
            pe.wait_ge(S["bank_free"], len(ROUNDS))
            for m in range(KT):
                for n in range(8):
                    of = yr if n < 4 else yi
                    mm = pe.matmul(G.banks[:, m, :], of[:, n % 4, m * P:(m + 1) * P], w[:, n % 4, (n // 4) * 512:(n // 4) * 512 + 512],
                                   start=(n == 0), stop=(n == 7))
                mm.then_inc(S["back"], 1)
            pe.wait_ge(S["gated"], KT)
            for m in range(KT):
                if m % 4 == 0:
                    G.arrived(pe, m // 4, 1)
                project(pe, G, m // 4, m % 4, m, G.hT).then_inc(S["out_done"], 1)

        @block.scalar
        def _(act):
            for t in range(KT):
                act.wait_ge(S["turned"], t + 1)
                act.activation(ut[:, :, t * P:(t + 1) * P], G.banks[:, t, :].rearrange("p (j n) -> p j n", j=JT), ACT.Copy)\
                   .then_inc(S["copied"], 1)
            for half in range(2):
                act.wait_ge(S["last_sum"], half + 1)
                act.activation(last[:, half * 512:half * 512 + 512], G.banks[0:1, half, :], ACT.Copy).then_inc(S["last_done"], 1)
            for n in range(len(ROUNDS)):
                act.wait_ge(S["spectra"], n + 1)
                if n >= 2:
                    act.wait_ge(S["bank_free"], n - 1)
                for s in range(2):
                    act.activation(us[:, n % 2, s, :], G.banks[:, 4 * (n % 2) + s, :], ACT.Copy).then_inc(S["u_copied"], 1)

        @block.vector
        def _(dve):
            step = Link(dve, S["step"])
            for n, (f, half) in enumerate(ROUNDS):
                cols = slice(half * 512, half * 512 + 512)
                dve.wait_ge(S["u_copied"], 2 * n + 2)
                kr, ki = G.banks[:, 4 * (n % 2) + 2, :], G.banks[:, 4 * (n % 2) + 3, :]
                ur, ui = us[:, n % 2, 0, :], us[:, n % 2, 1, :]
                step.mark(dve.tensor_tensor(tmp[:, 0, :], ur, kr, ALU.mult))
                step.mark(dve.tensor_tensor(tmp[:, 1, :], ui, ki, ALU.mult))
                step.mark(dve.tensor_tensor(tmp[:, 2, :], ur, ki, ALU.mult))
                step(dve.tensor_tensor(tmp[:, 3, :], ui, kr, ALU.mult))
                step.mark(dve.tensor_tensor(yr[:, f, cols], tmp[:, 0, :], tmp[:, 1, :], ALU.subtract))
                step(dve.tensor_tensor(yi[:, f, cols], tmp[:, 2, :], tmp[:, 3, :], ALU.add))
                if f == 0:
                    dve.wait_ge(S["last_done"], 2)
                    step.mark(dve.tensor_copy(yr[0:1, 0, cols], tmp[0:1, 0, :]))
                    step(dve.tensor_tensor(yi[0:1, 0, cols], ui[0:1, :], last[0:1, cols], ALU.mult))
                dve.sem_inc(S["bank_free"], 1)
            for m in range(KT):
                dve.wait_ge(S["back"], m + 1)
                dve.scalar_tensor_tensor(out=tmp[:, m % 4, :], in0=T.uT[:, m, :], scalar=G.col("hy_skip", m), in1=G.banks[:, m, :],
                                         op0=ALU.mult, op1=ALU.add).then_inc(S["skipped"], 1)
                dve.wait_ge(S["skipped"], m + 1)
                dve.tensor_tensor(G.hT[:, m, :], tmp[:, m % 4, :], T.x0T[:, m, :], ALU.mult).then_inc(S["gated"], 1)
                dve.wait_ge(S["gated"], m + 1)
            for m in range(KT):
                dve.wait_ge(S["out_done"], m + 1)
                dve.scalar_tensor_tensor(out=G.x[:, m, :], in0=G.banks[:, m, :], scalar=G.col("hy_b_out", m), in1=G.x[:, m, :],
                                         op0=ALU.add, op1=ALU.add).then_inc(S["added"], 1)

        G.first += 4


def hyena(G):
    with ExitStack() as ctx:
        T = Shared()
        T.ksum = G.sb("filter_sum", [P, JT, D], ctx=ctx)
        T.kdiff = G.sb("filter_difference", [P, JT, D], ctx=ctx)
        T.uT = G.sb("hyena_u_T", [P, KT, SEQ], ctx=ctx)
        T.x0T = G.sb("hyena_x0_T", [P, KT, SEQ], ctx=ctx)
        hyena_filters(G, T)
        hyena_projection(G, T)
        hyena_convolution(G, T)



RW_CHUNK = 64
RW_N = 64
N_CHUNKS = SEQ // RW_CHUNK
LEVELS = 6
LORA, GATE_LORA = 64, 128
RW_GN_EPS = RW_N * 1e-5
DECAY_SCALE = -float(np.exp(-0.5))
FWD, BWD = 0, 1
SPILLED = 5


def scan_masks():
    s, t = np.arange(P)[:, None], np.arange(P)[None]
    same = (s // RW_CHUNK) == (t // RW_CHUNK)
    out = []
    for l in range(LEVELS):
        b = 1 << l
        m = ((s // (2 * b)) == (t // (2 * b))) & (s % (2 * b) >= b) & (t % (2 * b) < b)
        out += [m, m.T]
    for before, upto in ((same & (s < t), same & (s <= t)), (same & (s > t), same & (s >= t))):
        before, upto = before.astype(np.float32), upto.astype(np.float32)
        out += [-before, upto, before, upto]
    out.append(np.broadcast_to((np.arange(SEQ) % RW_CHUNK != 0)[None], (P, SEQ)))
    out.append(np.tile(np.eye(RW_N), (2, 1)))
    return np.concatenate([o.astype(np.float32) for o in out], 1)


def lay_rwkv(L, a):
    wide = lambda v: np.concatenate([v, np.zeros((P - v.shape[0], v.shape[1]), np.float32)])
    for n in ("r", "k", "v"):
        L.column_chunks(a[f"rw_w_{n}"][0])
    L.chunk(L.matrix(a["rw_w1"][0, 0]), L.matrix(a["rw_w1"][0, 1]), L.matrix(a["rw_a1"][0]), L.matrix(a["rw_g1"][0]), a["rw_g2"][0])
    L.chunk(wide(a["rw_w2"][0, 0]), wide(a["rw_w2"][0, 1]), wide(a["rw_a2"][0]))
    L.column_chunks(a["rw_w_o"][0])
    L.vector("rw_norm", a["norm_mix_g"][1])
    L.vector("rw_mu", a["rw_mu"][0].reshape(-1))
    L.vector("rw_w0", a["rw_w0"][0].reshape(-1))
    for n in ("a0", "k_k", "k_a", "ln_w", "ln_b"):
        L.vector("rw_" + n, a["rw_" + n][0])
    L.vector("rw_r_k", a["rw_r_k"][0].reshape(-1))
    same = np.arange(P)[:, None] // RW_N == np.arange(P)[None] // RW_N
    L.constant("mean64", same.astype(np.float32) / RW_N)


def spread(ap, n):
    return bass.AP(tensor=ap.tensor, offset=ap.offset, ap=[ap.ap[0], [0, n], ap.ap[1]])


def rwkv_projection(G, T):
    nc = G.nc
    R, K, V, W0, W1, A1, G1, A2 = 0, 8, 16, 24, 25, 26, 27, 28
    N_OUT = A2 + KT
    LERPS = ("r", "k", "v", "w", "a", "g")
    MU = (0, 2, 3, 1, 4, 5)
    with ExitStack() as ctx:
        S = stage(G, "rwin", ctx, *RMS, "delta", "lerped", "out_sum", "out_done", "g2_copied", "raw", "keys_squared", "norm_sum",
                  "floored", "rooted", "step", "mixed", "unit", "spilled")
        big = {n: G.sb("rwin_" + n, [P, KT, SEQ], ctx=ctx) for n in ("xx", "x0", "x1", "r", "k", "v", "a")}
        xx = big["xx"]
        rstd = G.sb("rwin_rstd", [P, SEQ], ctx=ctx)
        al = G.sb("rwin_a_lora", [LORA, SEQ], ctx=ctx)
        block = ctx.enter_context(nc.Block())
        lora_at = {W0: (0, LORA), W1: (KT * LORA, LORA), A1: (2 * KT * LORA, LORA), G1: (3 * KT * LORA, GATE_LORA)}
        last_use = {0: R + KT, 1: K + KT, 2: V + KT, 3: W1 + 1, 4: A1 + 1}

        @block.sync
        def _(sp):
            sp.dma_start(T.x_dram.ap().rearrange("t p n -> p t n"), G.x[:, :, :]).then_inc(S["spilled"], 16)
            G.feed(sp, 6, S["out_sum"], per=4)
            sp.wait_ge(S["out_done"], N_OUT)
            sp.wait_ge(S["g2_copied"], 1)
            G.first += 6
            G.feed(sp, 1, S["out_sum"], base=G1)
            G.first -= 6
            sp.wait_ge(S["mixed"], KT)
            sp.wait_ge(S["unit"], 2 * KT)
            for n, name in enumerate(("r", "x1", "x0", "a", "v")):
                sp.dma_start(T.spill.ap()[:, :, n * SEQ:(n + 1) * SEQ].rearrange("t p n -> p t n"), big[name][:, :, :])\
                  .then_inc(S["spilled"], 16)
            sp.wait_ge(S["spilled"], 16 * (SPILLED + 1))

        @block.tensor
        def _(pe):
            rms_pe(pe, G, S, xx, 7)
            n = 0

            def bank():
                if n >= 8:
                    pe.wait_ge(S["out_done"], n - 7)
                return n % 8

            for l in range(3):
                for m in range(KT):
                    c = 2 * l + m // 4
                    if m % 4 == 0:
                        G.arrived(pe, c % 2, c // 2)
                    if m == 0:
                        pe.wait_ge(S["lerped"], KT * (l + 1))
                    project(pe, G, c % 2, m % 4, bank(), big[f"x{l % 2}"]).then_inc(S["out_sum"], 1)
                    n += 1
            G.arrived(pe, 0, 3)
            w = G.ring[:, G.slot(0), :]
            for l, outs in ((3, (W0, W1)), (4, (A1,)), (5, (G1,))):
                pe.wait_ge(S["lerped"], KT * (l + 1))
                for o in outs:
                    at, width = lora_at[o]
                    b = bank()
                    for k in range(KT):
                        mm = pe.matmul(G.banks[0:width, b, :], w[:, at + k * width:at + (k + 1) * width], big[f"x{l % 2}"][:, k, :],
                                       start=(k == 0), stop=(k == KT - 1))
                    mm.then_inc(S["out_sum"], 1)
                    n += 1
            G.arrived(pe, 1, 3)
            w2 = G.ring[0:LORA, G.slot(1), :]
            pe.wait_ge(S["out_done"], A1 + 1)
            for m in range(KT):
                b = bank()
                pe.matmul(G.banks[:, b, :], w2[:, 2 * D + m * P:2 * D + (m + 1) * P], al[:, :], start=True, stop=True)\
                  .then_inc(S["out_sum"], 1)
                n += 1
            pe.wait_ge(S["out_done"], N_OUT)
            for m in range(KT):
                pe.wait_ge(S["keys_squared"], m + 1)
                pe.matmul(G.banks[:, m, :], G.con("mean64"), xx[:, m, :], start=True, stop=True).then_inc(S["norm_sum"], 1)

        @block.scalar
        def _(act):
            rms_act(act, G, S, xx)
            rms_root(act, G, S, rstd)
            for n in range(N_OUT):
                act.wait_ge(S["out_sum"], n + 1)
                of = G.banks[:, n % 8, :]
                if n < W0:
                    ins = act.activation(big["rkv"[n // KT]][:, n % KT, :], of, ACT.Copy)
                elif n < A1:
                    ins = act.activation(T.tanh[:, n - W0, :], of[0:LORA, :], ACT.Tanh)
                elif n == A1:
                    ins = act.activation(al[:, :], of[0:LORA, :], ACT.Copy)
                elif n == G1:
                    ins = act.activation(T.sg[:, :], of, ACT.Sigmoid)
                else:
                    ins = act.activation(big["a"][:, n - A2, :], of, ACT.Sigmoid, bias=G.col("rw_a0", n - A2))
                ins.then_inc(S["out_done"], 1)
            at = 3 * KT * LORA + KT * GATE_LORA
            act.activation(T.g2[:, :], G.ring[:, G.slot(0), at:at + D], ACT.Copy).then_inc(S["g2_copied"], 1)
            for m in range(KT):
                act.wait_ge(S["raw"], m + 1)
                act.activation(xx[:, m, :], big["x0"][:, m, :], ACT.Square).then_inc(S["keys_squared"], 1)
            for m in range(KT):
                act.wait_ge(S["floored"], m + 1)
                act.activation(xx[:, m, :], xx[:, m, :], ACT.Sqrt).then_inc(S["rooted"], 1)

        @block.vector
        def _(dve):
            rms_dve(dve, G, S, rstd, 7, "rw_norm", G.hT)
            h, n = G.hT, SEQ
            dve.wait_ge(S["h_ready"], KT)
            dve.tensor_tensor(xx[:, :, 1:n - 1], h[:, :, 0:n - 2], h[:, :, 2:n], ALU.add).then_inc(S["delta"], 1)
            dve.tensor_copy(xx[:, :, 0:1], h[:, :, 1:2]).then_inc(S["delta"], 1)
            dve.tensor_copy(xx[:, :, n - 1:n], h[:, :, n - 2:n - 1]).then_inc(S["delta"], 1)
            dve.wait_ge(S["delta"], 3)
            for k in range(KT):
                dve.scalar_tensor_tensor(out=xx[:, k, :], in0=xx[:, k, :], scalar=0.5, in1=h[:, k, :],
                                         op0=ALU.mult, op1=ALU.subtract).then_inc(S["delta"], 1)
            dve.wait_ge(S["delta"], 3 + KT)
            for l in range(len(LERPS)):
                if l >= 2:
                    dve.wait_ge(S["out_sum"], last_use[l - 2])
                for k in range(KT):
                    dve.scalar_tensor_tensor(out=big[f"x{l % 2}"][:, k, :], in0=xx[:, k, :], scalar=G.col("rw_mu", MU[l] * KT + k),
                                             in1=h[:, k, :], op0=ALU.mult, op1=ALU.add).then_inc(S["lerped"], 1)
            dve.wait_ge(S["out_done"], N_OUT)
            dve.wait_ge(S["lerped"], KT * len(LERPS))
            kk, mixed, b = big["x0"], big["x1"], big["a"]
            step = Link(dve, S["step"])
            for m in range(KT):
                dve.tensor_scalar(kk[:, m, :], big["k"][:, m, :], G.col("rw_k_k", m), None, ALU.mult).then_inc(S["raw"], 1)
                step(dve.tensor_scalar(mixed[:, m, :], b[:, m, :], -1.0, G.col("rw_k_a", m), ALU.add, ALU.mult))
                dve.scalar_tensor_tensor(out=mixed[:, m, :], in0=mixed[:, m, :], scalar=1.0, in1=big["k"][:, m, :],
                                         op0=ALU.add, op1=ALU.mult).then_inc(S["mixed"], 1)
            for m in range(KT):
                dve.wait_ge(S["norm_sum"], m + 1)
                dve.tensor_scalar(xx[:, m, :], G.banks[:, m, :], float(RW_N), 1e-24, ALU.mult, ALU.max).then_inc(S["floored"], 1)
            for m in range(KT):
                dve.wait_ge(S["rooted"], m + 1)
                step(dve.reciprocal(xx[:, m, :], xx[:, m, :]))
                dve.tensor_tensor(kk[:, m, :], kk[:, m, :], xx[:, m, :], ALU.mult).then_inc(S["unit"], 1)
                dve.wait_ge(S["unit"], 2 * m + 1)
                dve.tensor_tensor(b[:, m, :], b[:, m, :], kk[:, m, :], ALU.mult).then_inc(S["unit"], 1)

        G.first += 7


def rwkv_scan(G, T):
    nc = G.nc
    PER = dict(loaded=16, staged=2, decay_sum=2, decay_gate=2, exponents=2, sums_read=4, exps=2, operands=2, bonus_in=1, bonus_sum=1, bonus_done=1,
               token_sum=7, token_done=7, gram_sum=16, gram_done=16, z_sum=24, z_done=24, x_sum=16, x_done=16, y_sum=24, y_done=24,
               nv_sum=2, nv_done=2, ua_sum=4, ua_done=4, phi_sum=4, phi_done=4, psi_done=4, own_sum=2, own_done=2, read_sum=2,
               read_done=2, state_sum=12, state_done=12, past_sum=2, turn_done=1, bonus_stored=16)
    with ExitStack() as ctx:
        S = stage(G, "scan", ctx, "masks_loaded", "step", "go", *PER)
        ld = G.sb("scan_in", [P, SPILLED, SEQ], ctx=ctx)
        early = G.sb("scan_early", [P, 9 * SEQ], ctx=ctx)
        ex = early[:, :].rearrange("p (n t) -> p n t", n=9)
        MH = early[:, 0:8 * SEQ].rearrange("p (d h j w t) -> p d h j w t", d=2, h=2, j=JT, w=2)
        NG = G.sb("scan_NG", [P, 2, 2, JT, 2, P], ctx=ctx)
        AR = G.sb("scan_AR", [P, 2, JT, 2, P], ctx=ctx)
        KB = G.sb("scan_KB", [P, 2, 2, SEQ], ctx=ctx)
        ZF = KB[:, :, :, :].rearrange("p d h (j t) -> p d h j t", j=JT)
        hat = G.sb("scan_hat", [P, 2, 2, SEQ], ctx=ctx)
        phi = hat[:, :, 0, :].rearrange("p d (c k) -> p d c k", c=N_CHUNKS)
        psi = hat[:, :, 1, :].rearrange("p d (c k) -> p d c k", c=N_CHUNKS)
        X = G.sb("scan_X", [P, 2, 2, JT, P], ctx=ctx)
        Y = G.sb("scan_Y", [P, 2, 2, JT, P], ctx=ctx)
        NA = G.sb("scan_NA", [P, 2, 2, JT, P], ctx=ctx)
        tok = G.sb("scan_tok", [P, 2, 2, JT, P], ctx=ctx)
        vt = G.sb("scan_v", [P, JT, P], ctx=ctx)
        pe_end = G.sb("scan_decay", [P, 2, N_CHUNKS], ctx=ctx)
        state = G.sb("scan_state", [P, 2, N_CHUNKS, RW_N], ctx=ctx)
        bonus = G.sb("scan_bonus", [P, SEQ], ctx=ctx)
        w2 = G.sb("scan_w2", [LORA, 2, P], ctx=ctx)
        masks = G.sb("scan_masks_sb", list(G.aps["scan_masks"].shape), ctx=ctx)
        block = ctx.enter_context(nc.Block())
        B = lambda d, n: G.banks[:, 4 * d + n, :]
        at = 2 * LEVELS * P
        level_mask = lambda l, d: masks[:, (2 * l + d) * P:(2 * l + d + 1) * P]
        gram_mask = lambda d, w: masks[:, at + (2 * d + w) * 2 * P:at + (2 * d + w + 1) * 2 * P]
        reset = masks[:, at + 8 * P:at + 8 * P + SEQ]
        eye = masks[:, at + 8 * P + SEQ:at + 8 * P + SEQ + RW_N]
        order = [list(range(N_CHUNKS)), list(range(N_CHUNKS))[::-1]]
        heads = [slice(0, RW_N), slice(RW_N, P)]
        b_slot = G.slot(0)

        def exponents(d):
            lw, F, E1, E2 = (ex[:, 4 * d + n, :] for n in range(4))
            return lw, F, E1, E2, F if d == FWD else ex[:, 8, :]

        def needer(eng, i):
            return lambda name, n: eng.wait_ge(S[name], PER[name] * i + n)

        @block.sync
        def _(sp):
            sp.dma_start(masks[:, :], G.aps["scan_masks"]).then_inc(S["masks_loaded"], 16)
            with sp.Fori(0, KT) as i:
                sp.wait_ge(S["turn_done"], i + 1)
                sp.dma_start(ld[:, :, :], T.spill.ap()[i].rearrange("p (a n) -> p a n", a=SPILLED)).then_inc(S["loaded"], 16)
                sp.wait_ge(S["bonus_done"], i + 1)
                sp.dma_start(T.bonus_dram.ap()[i], bonus[:, :]).then_inc(S["bonus_stored"], 16)
            sp.wait_ge(S["bonus_stored"], 16 * KT)
            G.feed(sp, 1, S["turn_done"], per=KT + 1)

        @block.tensor
        def _(pe):
            G.arrived(pe, 0, 0)
            pe.wait_ge(S["masks_loaded"], 16)
            with pe.Fori(0, KT) as i:
                need = needer(pe, i)
                for d in (FWD, BWD):
                    need("staged", d + 1)
                    pe.matmul(B(d, 0), w2[:, d, :], T.tanh[:, d, :], start=True, stop=True).then_inc(S["decay_sum"], 1)
                need("bonus_in", 1)
                pe.matmul(B(0, 2), G.con("mean64"), bonus[:, :], start=True, stop=True).then_inc(S["bonus_sum"], 1)
                need("loaded", 16)
                for j in range(JT):
                    mm = pe.transpose(B(0, 1)[:, j * P:(j + 1) * P], ld[:, 4, j * P:(j + 1) * P], G.con("ident"))
                mm.then_inc(S["token_sum"], 1)
                need("token_done", 1)
                need("bonus_done", 1)
                for d in (FWD, BWD):
                    need("operands", d + 1)
                    for n, of in enumerate((AR[:, d, :, 0, :], hat[:, d, 0, :], hat[:, d, 1, :])):
                        for j in range(JT):
                            src = of[:, j, :] if n == 0 else of[:, j * P:(j + 1) * P]
                            mm = pe.transpose(B(d, 1 + n)[:, j * P:(j + 1) * P], src, G.con("ident"))
                        mm.then_inc(S["token_sum"], 1)
                for w, left in ((0, 1), (1, 0)):
                    for d in (FWD, BWD):
                        if w == 0:
                            need("token_done", 1 + 3 * (d + 1))
                        for h in range(2):
                            for j in range(JT):
                                if w == 1 and j % 2 == 0:
                                    need("gram_done", 4 * d + 2 * h + j // 2 + 1)
                                mm = pe.matmul(B(d, 2 * h + j // 2)[:, (j % 2) * 256:(j % 2) * 256 + 256],
                                               KB[heads[h], d, left, j * P:(j + 1) * P], AR[heads[h], d, j, :, :],
                                               start=True, stop=True)
                                if j % 2:
                                    mm.then_inc(S["gram_sum"], 1)
                for l in range(LEVELS):
                    for d in (FWD, BWD):
                        for h in range(2):
                            if l == 0:
                                need("gram_done", 8 + 4 * d + 4)
                            else:
                                need("y_done", 4 * (l - 1) + 2 * d + h + 1)
                                if l == 1:
                                    need("z_done", 2 * d + h + 1)
                                else:
                                    need("x_done", 4 * (l - 2) + 2 * d + h + 1)
                            for j in range(JT):
                                mm = pe.matmul(B(d, h)[:, j * P:(j + 1) * P], MH[:, d, h, j, 0, :],
                                               G.con("ident") if l == 0 else X[:, d, h, j, :], start=True, stop=True)
                            mm.then_inc(S["z_sum"], 1)
                    for d in (FWD, BWD):
                        factor = X if l == 0 else ZF
                        if 1 <= l < LEVELS - 1:
                            for h in range(2):
                                need("z_done", 4 * l + 2 * d + h + 1)
                                for j in range(JT):
                                    mm = pe.matmul(B(d, 2 + h)[:, j * P:(j + 1) * P], Y[:, d, h, j, :], factor[:, d, h, j, :],
                                                   start=True, stop=True)
                                mm.then_inc(S["x_sum"], 1)
                        for h in range(2):
                            need("z_done", 4 * l + 2 * d + h + 1)
                            for j in range(JT):
                                mm = pe.matmul(B(d, h)[:, j * P:(j + 1) * P], factor[:, d, h, j, :],
                                               G.con("ident") if l == 0 else Y[:, d, h, j, :], start=True, stop=True)
                            mm.then_inc(S["y_sum"], 1)
                for d in (FWD, BWD):
                    need("x_done", 4 * (LEVELS - 3) + 2 * d + 2)
                    for h in range(2):
                        for j in range(JT):
                            mm = pe.matmul(B(d, 2)[:, (h * JT + j) * RW_N:(h * JT + j + 1) * RW_N], NG[:, d, h, j, 0, :],
                                           vt[:, j, heads[h]], start=True, stop=True)
                    mm.then_inc(S["nv_sum"], 1)
                for d in (FWD, BWD):
                    need("nv_done", d + 1)
                    for h in range(2):
                        need("y_done", 4 * (LEVELS - 1) + 2 * d + h + 1)
                        for j in range(JT):
                            mm = pe.matmul(B(d, h)[:, j * P:(j + 1) * P], Y[:, d, h, j, :], NA[:, d, h, j, :], start=True, stop=True)
                        mm.then_inc(S["ua_sum"], 1)
                for d in (FWD, BWD):
                    need("ua_done", 2 * d + 2)
                    pe.sem_inc(S["go"], 1)
                    for half in range(2):
                        rows = heads[half]
                        for j in range(JT):
                            for h in range(2):
                                mm = pe.matmul(B(d, 2 + half)[heads[h], j * RW_N:(j + 1) * RW_N], X[rows, d, h, j, RW_N:P],
                                               tok[rows, d, 1, j, heads[h]], start=True, stop=True)
                                out = B(d, 2 + half)[heads[h], 256 + j * RW_N:256 + (j + 1) * RW_N]
                                pe.matmul(out, tok[rows, d, 0, j, heads[h]], vt[rows, j, heads[h]], start=True, stop=False,
                                          skip_group_check=True)
                                mm = pe.matmul(out, tok[rows, d, 1, j, heads[h]], X[rows, d, h, j, 0:RW_N], start=False, stop=True,
                                               skip_group_check=True)
                        mm.then_inc(S["phi_sum"], 1)
                    for j in range(JT):
                        for h in range(2):
                            out = B(d, 0)[heads[h], j * P:(j + 1) * P]
                            pe.matmul(out, vt[:, j, heads[h]], NG[:, d, h, j, 1, :], start=True, stop=False, skip_group_check=True)
                            mm = pe.matmul(out, X[:, d, h, j, 0:RW_N], MH[:, d, h, j, 1, :], start=False, stop=True,
                                           skip_group_check=True)
                    mm.then_inc(S["own_sum"], 1)
                    for j in range(JT):
                        for h in range(2):
                            mm = pe.matmul(B(d, 1)[heads[h], j * P:(j + 1) * P], X[:, d, h, j, RW_N:P], MH[:, d, h, j, 1, :],
                                           start=True, stop=True)
                    mm.then_inc(S["read_sum"], 1)
                for n in range(1, N_CHUNKS - 1):
                    for d in (FWD, BWD):
                        if n == 1:
                            need("phi_done", 2 * d + 2)
                            need("psi_done", 2 * d + 2)
                        else:
                            need("state_done", 2 * (n - 2) + d + 1)
                        pe.sem_inc(S["go"], 1)
                        for h in range(2):
                            of = psi[heads[h], d, order[d][0], :] if n == 1 else state[heads[h], d, n, :]
                            mm = pe.matmul(B(d, 2 + h)[heads[h], n * RW_N:(n + 1) * RW_N], phi[heads[h], d, order[d][n], :], of,
                                           start=True, stop=True)
                        mm.then_inc(S["state_sum"], 1)
                for d in (FWD, BWD):
                    need("own_done", d + 1)
                    need("read_done", d + 1)
                    need("state_done", 2 * (N_CHUNKS - 3) + d + 1)
                    pe.sem_inc(S["go"], 1)
                    for n in range(1, N_CHUNKS):
                        c = order[d][n]
                        for h in range(2):
                            of = psi[heads[h], d, order[d][0], :] if n == 1 else state[heads[h], d, n, :]
                            mm = pe.matmul(B(d, h)[heads[h], c * RW_CHUNK:(c + 1) * RW_CHUNK], of,
                                           AR[heads[h], d, c // 2, 1, (c % 2) * RW_CHUNK:(c % 2 + 1) * RW_CHUNK], start=True, stop=True)
                    mm.then_inc(S["past_sum"], 1)

        @block.scalar
        def _(act):
            act.wait_ge(G.landed[b_slot], 16 * (G.first // SLOTS + 1))
            with act.Fori(0, KT) as i:
                need = needer(act, i)
                act.wait_ge(S["turn_done"], i + 1)
                for d in (FWD, BWD):
                    act.activation(w2[:, d, :], G.ring[0:LORA, b_slot, bass.ds(d * D + i * P, P)], ACT.Copy).then_inc(S["staged"], 1)
                for d in (FWD, BWD):
                    need("decay_sum", d + 1)
                    act.activation(ex[:, 4 * d, :], B(d, 0), ACT.Sigmoid, bias=G.col("rw_w0", d * KT + i)).then_inc(S["decay_gate"], 1)
                for d in (FWD, BWD):
                    need("exponents", d + 1)
                    lw, F, E1, E2, Fin = exponents(d)
                    act.activation(pe_end[:, d, :], F[:, RW_CHUNK - 1::RW_CHUNK], ACT.Exp).then_inc(S["sums_read"], 1)
                    act.activation(lw, Fin, ACT.Exp, scale=-1.0).then_inc(S["sums_read"], 1)
                    for e in (E1, E2):
                        act.activation(e, e, ACT.Exp)
                    need("sums_read", 2 * d + 2)
                    act.activation(Fin, Fin, ACT.Exp).then_inc(S["exps"], 1)
                need("token_sum", 1)
                act.activation(vt[:, :, :], B(0, 1).rearrange("p (j t) -> p j t", j=JT), ACT.Copy).then_inc(S["token_done"], 1)
                for d in (FWD, BWD):
                    for n in range(3):
                        need("token_sum", 1 + 3 * d + n + 1)
                        of = B(d, 1 + n).rearrange("p (j t) -> p j t", j=JT)
                        if n == 0:
                            for h in range(2):
                                ins = act.activation(NA[:, d, h, :, RW_N:P], of[:, :, heads[h]], ACT.Copy)
                        else:
                            ins = act.activation(tok[:, d, n - 1, :, :], of, ACT.Copy)
                        ins.then_inc(S["token_done"], 1)
                for l in range(LEVELS):
                    for d in (FWD, BWD):
                        if 1 <= l < LEVELS - 1:
                            for h in range(2):
                                need("x_sum", 4 * (l - 1) + 2 * d + h + 1)
                                act.activation(X[:, d, h, :, :], B(d, 2 + h).rearrange("p (j t) -> p j t", j=JT), ACT.Copy)\
                                   .then_inc(S["x_done"], 1)
                        for h in range(2):
                            need("y_sum", 4 * l + 2 * d + h + 1)
                            act.activation(Y[:, d, h, :, :], B(d, h).rearrange("p (j t) -> p j t", j=JT), ACT.Copy)\
                               .then_inc(S["y_done"], 1)
                for d in (FWD, BWD):
                    need("nv_sum", d + 1)
                    act.activation(NA[:, d, :, :, 0:RW_N], B(d, 2).rearrange("p (h j v) -> p h j v", h=2, j=JT), ACT.Copy)\
                       .then_inc(S["nv_done"], 1)
                for d in (FWD, BWD):
                    for h in range(2):
                        need("ua_sum", 2 * d + h + 1)
                        act.activation(X[:, d, h, :, :], B(d, h).rearrange("p (j t) -> p j t", j=JT), ACT.Copy, scale=-1.0)\
                           .then_inc(S["ua_done"], 1)
                for d in (FWD, BWD):
                    for half in range(2):
                        need("phi_done", 2 * d + half + 1)
                        act.activation(psi[:, d, half::2, :], B(d, 2 + half)[:, 256:512].rearrange("p (j k) -> p j k", j=JT), ACT.Copy)\
                           .then_inc(S["psi_done"], 1)

        @block.vector
        def _(dve):
            dve.sem_inc(S["turn_done"], 1)
            dve.wait_ge(S["masks_loaded"], 16)
            step = Link(dve, S["step"])
            with dve.Fori(0, KT) as i:
                need = needer(dve, i)
                step.start(i * STEPS_PER_TURN)
                need("loaded", 16)
                r, k, kk, b, v = (ld[:, n, :] for n in range(SPILLED))
                step(dve.scalar_tensor_tensor(out=bonus[:, :], in0=r, scalar=G.col("rw_r_k", i), in1=k, op0=ALU.mult, op1=ALU.mult))
                dve.sem_inc(S["bonus_in"], 1)
                for d in (FWD, BWD):
                    lw, F, E1, E2, Fin = exponents(d)
                    need("decay_gate", d + 1)
                    step(dve.tensor_scalar(lw, lw, DECAY_SCALE, None, ALU.mult))
                    step(dve.tensor_tensor_scan(F, reset, lw, 0.0, ALU.mult, ALU.add))
                    total = F[:, RW_CHUNK - 1::RW_CHUNK]
                    total = bass.AP(tensor=total.tensor, offset=total.offset, ap=[total.ap[0], total.ap[1], [0, RW_CHUNK]])
                    step.mark(dve.tensor_tensor(E1, F, lw, ALU.subtract))
                    ins = dve.tensor_tensor(E2.rearrange("p (c t) -> p c t", c=N_CHUNKS), total,
                                            F.rearrange("p (c t) -> p c t", c=N_CHUNKS), ALU.subtract)
                    if d == BWD:
                        step(ins)
                        ins = dve.tensor_tensor(Fin, E2, lw, ALU.add)
                    ins.then_inc(S["exponents"], 1)
                need("bonus_sum", 1)
                dve.scalar_tensor_tensor(out=bonus[:, :], in0=B(0, 2), scalar=float(RW_N), in1=v, op0=ALU.mult, op1=ALU.mult)\
                   .then_inc(S["bonus_done"], 1)
                for d in (FWD, BWD):
                    lw, F, E1, E2, Fin = exponents(d)
                    before, behind = (E1, E2) if d == FWD else (E2, E1)
                    need("exps", d + 1)
                    tiles = lambda a: a.rearrange("p (j t) -> p j t", j=JT)
                    dve.tensor_tensor(AR[:, d, :, 0, :], tiles(kk), tiles(before), ALU.mult)
                    dve.tensor_tensor(AR[:, d, :, 1, :], tiles(r), tiles(Fin), ALU.mult)
                    dve.tensor_tensor(KB[:, d, 0, :], k, lw, ALU.mult)
                    dve.tensor_tensor(KB[:, d, 1, :], b, lw, ALU.mult)
                    dve.tensor_tensor(hat[:, d, 0, :], k, behind, ALU.mult)
                    dve.tensor_tensor(hat[:, d, 1, :], b, behind, ALU.mult).then_inc(S["operands"], 1)
                for w, to in ((0, MH), (1, NG)):
                    for d in (FWD, BWD):
                        for h in range(2):
                            for jp in range(2):
                                need("gram_sum", 8 * w + 4 * d + 2 * h + jp + 1)
                                dve.tensor_tensor(to[:, d, h, 2 * jp:2 * jp + 2, :, :].rearrange("p j w t -> p j (w t)"),
                                                  B(d, 2 * h + jp).rearrange("p (j n) -> p j n", j=2), spread(gram_mask(d, w), 2),
                                                  ALU.mult).then_inc(S["gram_done"], 1)
                for l in range(LEVELS):
                    for d in (FWD, BWD):
                        for h in range(2):
                            need("z_sum", 4 * l + 2 * d + h + 1)
                            z = (X if l == 0 else ZF)[:, d, h, :, :]
                            step(dve.tensor_tensor(z, B(d, h).rearrange("p (j t) -> p j t", j=JT), spread(level_mask(l, d), JT), ALU.mult))
                            dve.tensor_tensor(z, z, spread(G.con("ident"), JT), ALU.add).then_inc(S["z_done"], 1)
                for d in (FWD, BWD):
                    for half in range(2):
                        need("phi_sum", 2 * d + half + 1)
                        for j in range(JT):
                            c = 2 * j + half
                            ins = dve.scalar_tensor_tensor(out=phi[:, d, c, :], in0=eye, scalar=pe_end[:, d, c:c + 1],
                                                           in1=B(d, 2 + half)[:, j * RW_N:(j + 1) * RW_N], op0=ALU.mult, op1=ALU.add)
                        ins.then_inc(S["phi_done"], 1)
                    need("own_sum", d + 1)
                    y = G.hT[:, i, :]
                    if d == FWD:
                        dve.tensor_copy(y, B(d, 0)).then_inc(S["own_done"], 1)
                        need("own_done", 1)
                    else:
                        dve.tensor_tensor(y, y, B(d, 0), ALU.add).then_inc(S["own_done"], 1)
                        need("own_done", 2)
                    need("read_sum", d + 1)
                    dve.tensor_tensor(AR[:, d, :, 1, :], AR[:, d, :, 1, :], B(d, 1).rearrange("p (j t) -> p j t", j=JT), ALU.add)\
                       .then_inc(S["read_done"], 1)
                for n in range(1, N_CHUNKS - 1):
                    for d in (FWD, BWD):
                        need("state_sum", 2 * (n - 1) + d + 1)
                        if n == 1:
                            need("psi_done", 2 * d + 2)
                        for h in range(2):
                            ins = dve.tensor_tensor(state[heads[h], d, n + 1, :], B(d, 2 + h)[heads[h], n * RW_N:(n + 1) * RW_N],
                                                    psi[heads[h], d, order[d][n], :], ALU.add)
                        ins.then_inc(S["state_done"], 1)
                for d in (FWD, BWD):
                    need("past_sum", d + 1)
                    span = slice(RW_CHUNK, SEQ) if d == FWD else slice(0, SEQ - RW_CHUNK)
                    for h in range(2):
                        y = G.hT[heads[h], i, span]
                        step.mark(dve.tensor_tensor(y, y, B(d, h)[heads[h], span], ALU.add))
                    step.settle()
                need("bonus_stored", 16)
                dve.sem_inc(S["turn_done"], 1)
                assert step.n == STEPS_PER_TURN, step.n

        G.first += 1


STEPS_PER_TURN = 36


def rwkv_output(G, T):
    nc = G.nc
    with ExitStack() as ctx:
        S = stage(G, "rwout", ctx, "loaded", "mean_sum", "centred", "squared", "var_sum", "floored", "rooted", "step", "normed",
                  "gate_sum", "gated", "out_done", "added")
        sq = G.sb("rwout_squares", [P, KT, SEQ], ctx=ctx)
        bonus = G.sb("rwout_bonus", [P, KT, SEQ], ctx=ctx)
        block = ctx.enter_context(nc.Block())

        @block.sync
        def _(sp):
            sp.dma_start(bonus[:, :, :], T.bonus_dram.ap().rearrange("t p n -> p t n")).then_inc(S["loaded"], 16)
            sp.dma_start(G.x[:, :, :], T.x_dram.ap().rearrange("t p n -> p t n")).then_inc(S["loaded"], 16)
            G.feed(sp, 2, S["out_done"], per=4)

        @block.tensor
        def _(pe):
            for m in range(KT):
                pe.matmul(G.banks[:, m, :], G.con("mean64"), G.hT[:, m, :], start=True, stop=True).then_inc(S["mean_sum"], 1)
            for m in range(KT):
                pe.wait_ge(S["squared"], m + 1)
                pe.matmul(G.banks[:, m, :], G.con("mean64"), sq[:, m, :], start=True, stop=True).then_inc(S["var_sum"], 1)
            for m in range(KT):
                pe.wait_ge(S["floored"], m + 1)
                pe.matmul(G.banks[:, m, :], T.g2[:, m * P:(m + 1) * P], T.sg[:, :], start=True, stop=True).then_inc(S["gate_sum"], 1)
            pe.wait_ge(S["gated"], KT)
            for m in range(KT):
                if m % 4 == 0:
                    G.arrived(pe, m // 4, 0)
                project(pe, G, m // 4, m % 4, m, G.hT).then_inc(S["out_done"], 1)

        @block.scalar
        def _(act):
            for m in range(KT):
                act.wait_ge(S["centred"], m + 1)
                act.activation(sq[:, m, :], G.hT[:, m, :], ACT.Square).then_inc(S["squared"], 1)
            for m in range(KT):
                act.wait_ge(S["floored"], m + 1)
                act.activation(sq[:, m, :], sq[:, m, :], ACT.Sqrt).then_inc(S["rooted"], 1)

        @block.vector
        def _(dve):
            step = Link(dve, S["step"])
            for m in range(KT):
                dve.wait_ge(S["mean_sum"], m + 1)
                dve.tensor_tensor(G.hT[:, m, :], G.hT[:, m, :], G.banks[:, m, :], ALU.subtract).then_inc(S["centred"], 1)
            for m in range(KT):
                dve.wait_ge(S["var_sum"], m + 1)
                dve.tensor_scalar(sq[:, m, :], G.banks[:, m, :], RW_GN_EPS, None, ALU.add).then_inc(S["floored"], 1)
            dve.wait_ge(S["loaded"], 32)
            for m in range(KT):
                y = G.hT[:, m, :]
                dve.wait_ge(S["rooted"], m + 1)
                step(dve.reciprocal(sq[:, m, :], sq[:, m, :]))
                step(dve.tensor_tensor(y, y, sq[:, m, :], ALU.mult))
                step(dve.tensor_scalar(y, y, G.col("rw_ln_w", m), G.col("rw_ln_b", m), ALU.mult, ALU.add))
                step(dve.tensor_tensor(y, y, bonus[:, m, :], ALU.add))
                dve.wait_ge(S["gate_sum"], m + 1)
                dve.tensor_tensor(y, y, G.banks[:, m, :], ALU.mult).then_inc(S["gated"], 1)
            for m in range(KT):
                dve.wait_ge(S["out_done"], m + 1)
                dve.tensor_tensor(G.x[:, m, :], G.x[:, m, :], G.banks[:, m, :], ALU.add).then_inc(S["added"], 1)

        G.first += 2


def rwkv(G):
    nc = G.nc
    with ExitStack() as ctx:
        T = Shared()
        T.spill = nc.dram_tensor("rwkv_operands", [KT, P, SPILLED * SEQ], F32, kind="Internal")
        T.bonus_dram = nc.dram_tensor("rwkv_bonus", [KT, P, SEQ], F32, kind="Internal")
        T.x_dram = nc.dram_tensor("rwkv_residual", [KT, P, SEQ], F32, kind="Internal")
        T.tanh = G.sb("rwkv_tanh", [LORA, 2, SEQ], ctx=ctx)
        T.sg = G.sb("rwkv_gate", [P, SEQ], ctx=ctx)
        T.g2 = G.sb("rwkv_g2", [P, D], ctx=ctx)
        rwkv_projection(G, T)
        rwkv_scan(G, T)
        rwkv_output(G, T)


def second_block(G):
    hyena(G)
    feed_forward(G, "ffn2", "ff_norm_0", "ff_taps_0", ACT.Silu, 1)
    rwkv(G)
    feed_forward(G, "ffn3", "ff_norm_1", "ff_taps_1", ACT.Silu, 1)
    norm_in_place(G, "final2", "final_norm_2")



M_HEADS, M_DIM = 4, 512
M_WIDTH = M_HEADS * M_DIM
MT_ = M_DIM // P
H_HEADS, H_DIM = 8, 128
M_TAPS = 4
ALPHA = 2 ** 0.25
LN_EPS = 1e-5
HEAD_EPS = 1e-6
N_PAIRS = JT * (JT + 1) // 2
pair = lambda i, j: j * (j + 1) // 2 + i


def third_extra(a):
    at = 4 * M_WIDTH
    w = np.ascontiguousarray(a["w_in"][0][:, at:at + 2 * M_HEADS])
    b = a["b_in"][0]
    rows = np.concatenate([b[4096:6144].reshape(4, 512), b[6144:8192].reshape(4, 512),
                           np.concatenate([b[10248:11272].reshape(2, 512), np.zeros((2, 512), np.float32)])], 1)
    return {"w_if": Layout().matrix(w), "bias_rows3": np.ascontiguousarray(rows), "third_masks": third_masks(),
            "pair_masks": pair_masks()}


def third_masks():
    s, t = np.arange(P)[:, None], np.arange(P)[None]
    pick = np.zeros((P, M_HEADS * P), np.float32)
    for h in range(M_HEADS):
        pick[h, h * P:(h + 1) * P] = 1.0
    return np.concatenate([np.broadcast_to((np.arange(SEQ) % P != 0)[None].astype(np.float32), (P, SEQ)),
                           np.where(s > t, NEG, 0.0).astype(np.float32), pick], 1)


def pair_masks():
    s, t = np.arange(P)[:, None], np.arange(P)[None]
    out = []
    for l in range(7):
        b = 1 << l
        out.append((s // (2 * b) == t // (2 * b)) & (s % (2 * b) < b) & (t % (2 * b) >= b))
    return np.concatenate(out, 1).astype(np.uint32)


def lay_third(L, a):
    w, b = a["w_in"][0], a["b_in"][0]
    for h in range(M_HEADS):
        for s in range(4):
            at = s * M_WIDTH + h * M_DIM
            L.column_chunks(w[:, at:at + M_DIM])
    hq = 4 * M_WIDTH + 2 * M_HEADS
    for g in range(2):
        for s in range(4):
            at = hq + s * D + g * 512
            L.column_chunks(w[:, at:at + 512])
    L.column_chunks(w[:, hq + 4 * D:])
    L.row_chunks(a["w_proj_a"][0])
    L.row_chunks(a["w_proj_b"][0])
    L.column_chunks(a["w_out"][0])
    L.column_chunks(np.concatenate([a["w_ffn_gate"][0], a["w_ffn_up"][0]], 1), L.up_order())
    L.row_chunks(a["w_ffn_down"][0])
    six = np.concatenate([a["conv_w"][0], a["conv_b"], b[None, :2 * M_WIDTH]]).reshape(6, 32, P)
    L.column("m_conv", six.transpose(2, 1, 0).reshape(P, 6 * 32))
    L.column("m_if_bias", np.stack([b[8192:8196], b[8196:8200]], 1))
    L.vector("m_gain", a["m_norm_g"][0])
    for n, at in (("hq", hq), ("hf", hq + D), ("hg", hq + 3 * D), ("ga", hq + 4 * D), ("gb", hq + 5 * D)):
        L.vector("b_" + n, b[at:at + D])
    L.vector("h_gain", a["h_norm_g"][0])
    for n in ("ln1_g", "ln1_b", "ln2_g", "ln2_b"):
        L.vector(n, a[n][0])


def mlstm_gates(G, T):
    nc = G.nc
    with ExitStack() as ctx:
        S = stage(G, "gate", ctx, "loaded", "if_sum", "if_done", "magnitude", "exp_done", "log_done", "step", "rows_done",
                  "floor_in", "floor_done", "turned", "spread_sum", "spread_done")
        wif = G.sb("gate_w", [P, KT * 2 * M_HEADS], ctx=ctx)
        row = G.sb("gate_rows", [M_HEADS, 8, SEQ], ctx=ctx)
        gt = G.sb("gate_pairs", [M_HEADS, JT, SEQ], ctx=ctx)
        small = G.sb("gate_small", [M_HEADS, 4 * JT], ctx=ctx)
        zero = G.sb("gate_zero", [M_HEADS, P], ctx=ctx)
        ig, fg, ab, F, gd, M, nM, fl = (row[:, n, :] for n in range(8))
        block = ctx.enter_context(nc.Block())

        @block.sync
        def _(sp):
            sp.dma_start(wif[:, :], G.aps["w_if"]).then_inc(S["loaded"], 16)
            sp.dma_start(T.masks[:, :], G.aps["third_masks"]).then_inc(S["loaded"], 16)
            sp.dma_start(T.brows[:, :, :], G.aps["bias_rows3"].rearrange("h (s n) -> h s n", s=3)).then_inc(S["loaded"], 16)
            sp.wait_ge(S["loaded"], 48)

        @block.tensor
        def _(pe):
            pe.wait_ge(S["loaded"], 48)
            for n in range(2):
                for k in range(KT):
                    at = k * 2 * M_HEADS + n * M_HEADS
                    mm = pe.matmul(G.banks[0:M_HEADS, n, :], wif[:, at:at + M_HEADS], G.x[:, k, :], start=(k == 0), stop=(k == KT - 1))
                mm.then_inc(S["if_sum"], 1)
            pe.wait_ge(S["rows_done"], 1)
            for h in range(M_HEADS):
                pe.matmul(G.banks[:, 2 + h, :], T.pick[:, h * P:(h + 1) * P], nM, start=True, stop=True).then_inc(S["spread_sum"], 1)
            for j in range(JT):
                for i in range(j + 1):
                    q = pair(i, j)
                    pe.transpose(G.banks[:, 6, 4 * q:4 * q + 4], gt[:, j, i * P:(i + 1) * P], G.con("ident")[0:M_HEADS, 0:M_HEADS])
            pe.wait_ge(S["floor_done"], 1)
            for j in range(JT):
                q = N_PAIRS + j
                mm = pe.transpose(G.banks[:, 6, 4 * q:4 * q + 4], fl[:, j * P:(j + 1) * P], G.con("ident")[0:M_HEADS, 0:M_HEADS])
            mm.then_inc(S["turned"], 1)

        @block.scalar
        def _(act):
            for n, to in enumerate((ig, fg)):
                act.wait_ge(S["if_sum"], n + 1)
                act.activation(to, G.banks[0:M_HEADS, n, :], ACT.Identity, bias=G.col("m_if_bias", n)[0:M_HEADS, :]).then_inc(S["if_done"], 1)
            act.wait_ge(S["magnitude"], 1)
            act.activation(ab, ab, ACT.Exp, scale=-1.0).then_inc(S["exp_done"], 1)
            act.wait_ge(S["exp_done"], 1)
            act.activation(ab, ab, ACT.Ln, bias=1.0).then_inc(S["log_done"], 1)
            act.wait_ge(S["floor_in"], 1)
            act.activation(fl, fl, ACT.Exp, scale=-1.0).then_inc(S["floor_done"], 1)
            for h in range(M_HEADS):
                act.wait_ge(S["spread_sum"], h + 1)
                act.activation(T.nM[:, h, :], G.banks[:, 2 + h, :], ACT.Copy).then_inc(S["spread_done"], 1)
            act.wait_ge(S["turned"], 1)
            act.activation(T.ucol[:, :, :], G.banks[:, 6, 0:4 * (N_PAIRS + JT)].rearrange("p (q h) -> p q h", h=M_HEADS), ACT.Copy)\
               .then_inc(S["spread_done"], 1)

        @block.vector
        def _(dve):
            step = Link(dve, S["step"])
            step(dve.memset(zero[:, :], 0.0))
            step(dve.memset(small[:, 0:1], 0.0))
            dve.wait_ge(S["if_done"], 2)
            dve.scalar_tensor_tensor(out=ab, in0=fg, scalar=-1.0, in1=fg, op0=ALU.mult, op1=ALU.max).then_inc(S["magnitude"], 1)
            dve.wait_ge(S["log_done"], 1)
            step(dve.scalar_tensor_tensor(out=fg, in0=fg, scalar=0.0, in1=ab, op0=ALU.min, op1=ALU.subtract))
            dve.wait_ge(S["loaded"], 48)
            step(dve.tensor_tensor_scan(F, T.masks[0:M_HEADS, 0:SEQ], fg, 0.0, ALU.mult, ALU.add))
            step(dve.tensor_tensor(gd, ig, F, ALU.subtract))
            for j in range(JT):
                own = slice(j * P, (j + 1) * P)
                before, top, start = (small[:, n * JT + j:n * JT + j + 1] for n in range(3))
                step(dve.tensor_copy(gt[:, j, own], gd[:, own]))
                if j:
                    total = F[:, j * P - 1:j * P]
                    step(dve.tensor_scalar(before, small[:, j - 1:j], total, None, ALU.add))
                    step(dve.tensor_scalar(gt[:, j, 0:j * P], gt[:, j - 1, 0:j * P], total, None, ALU.add))
                    step(dve.tensor_reduce(top, gt[:, j, 0:j * P], AX, ALU.max))
                    step(dve.tensor_tensor(start, top, before, ALU.max))
                step(dve.tensor_tensor_scan(M[:, own], zero[:, :], gd[:, own], start if j else 0.0, ALU.add, ALU.max))
            step(dve.tensor_tensor(fl, F, M, ALU.add))
            dve.sem_inc(S["floor_in"], 1)
            step(dve.tensor_scalar(nM, M, -1.0, None, ALU.mult))
            dve.sem_inc(S["rows_done"], 1)


def mlstm(G, T):
    nc = G.nc
    PER = dict(qk_sum=8, biased=8, conv_done=8, silu_done=8, picked=1, v_sum=4, v_done=4, o_sum=4, o_done=4, diag_done=4, exp_done=4,
               score_sum=4, weighed=4, den_sum=1, num_sum=4, inverted=1, y_done=4, mean_done=4, centred=4, squared=4, rooted=1, var_in=1,
               gated=4, turned=4, head_done=4, turn_done=1)
    with ExitStack() as ctx:
        S = stage(G, "mlstm", ctx, "edges", "step", *PER)
        z = G.sb("mlstm_z", [P, 4, SEQ + M_TAPS - 1], ctx=ctx)
        cv = G.sb("mlstm_conv", [P, 4, SEQ], ctx=ctx)
        qk = G.sb("mlstm_qk", [P, 2, MT_, SEQ], ctx=ctx)
        v = G.sb("mlstm_v", [P, JT, M_DIM], ctx=ctx)
        og = G.sb("mlstm_o", [P, JT, M_DIM], ctx=ctx)
        E = G.sb("mlstm_exp", [P, JT, SEQ], ctx=ctx)
        y = G.sb("mlstm_y", [P, JT, M_DIM], ctx=ctx)
        dg = G.sb("mlstm_diag", [P, JT, P], ctx=ctx)
        pick = G.sb("mlstm_pick", [M_HEADS, P], ctx=ctx)
        st = G.sb("mlstm_stats", [P, 5, JT], ctx=ctx)
        rc, total, mean, sqs, rstd = (st[:, n, :] for n in range(5))
        block = ctx.enter_context(nc.Block())

        def needer(eng, i):
            return lambda name, n: eng.wait_ge(S[name], PER[name] * i + n)

        @block.sync
        def _(sp):
            with sp.Fori(0, M_HEADS) as i:
                for c, (name, n) in enumerate((("qk_sum", 4), ("qk_sum", 8), ("v_sum", 4), ("o_sum", 4))):
                    sp.wait_ge(S[name], PER[name] * i + n)
                    sp.dma_start(G.ring[:, G.slot(c), :], G.weights[4 * i + (G.first + c + SLOTS)])\
                      .then_inc(G.landed[G.slot(c)], 16)

        @block.tensor
        def _(pe):
            with pe.Fori(0, M_HEADS) as i:
                need = needer(pe, i)
                pe.wait_ge(S["turn_done"], i + 1)
                for s in range(2):
                    pe.wait_ge(G.landed[G.slot(s)], 16 * (2 * i + (G.first + s) // SLOTS + 1))
                    for m in range(4):
                        project(pe, G, s, m, 4 * s + m, G.x).then_inc(S["qk_sum"], 1)
                need("picked", 1)
                for s, name in ((0, "v_sum"), (1, "o_sum")):
                    pe.wait_ge(G.landed[G.slot(s)], 16 * (2 * i + (G.first + 2 + s) // SLOTS + 1))
                    w = G.chunk(s, KT)
                    need("biased", 4 * s + 4)
                    for j in range(JT):
                        b = G.banks[:, 4 * s + j, :]
                        for k in range(KT):
                            pe.matmul(b, G.x[:, k, j * P:(j + 1) * P], w[:, k, :], start=(k == 0), stop=False)
                        pe.matmul(b, pick[:, :], T.brows[:, s, :], start=False, stop=True).then_inc(S[name], 1)
                need("silu_done", 8)
                for a in range(JT):
                    need("v_done", a + 1)
                    for k in range(MT_):
                        mm = pe.matmul(G.banks[:, a, a * P:SEQ], qk[:, 1, k, a * P:(a + 1) * P], qk[:, 0, k, a * P:SEQ],
                                       start=(k == 0), stop=(k == MT_ - 1))
                    mm.then_inc(S["score_sum"], 1)
                need("weighed", 4)
                need("o_done", 4)
                for j in range(JT):
                    for a in range(j + 1):
                        mm = pe.matmul(G.banks[:, 0, j:j + 1], E[:, a, j * P:(j + 1) * P], G.con("ones")[:, 0:1],
                                       start=(a == 0), stop=(a == j))
                mm.then_inc(S["den_sum"], 1)
                for j in range(JT):
                    for a in range(j + 1):
                        mm = pe.matmul(G.banks[:, 4 + j, :], E[:, a, j * P:(j + 1) * P], v[:, a, :], start=(a == 0), stop=(a == j))
                    mm.then_inc(S["num_sum"], 1)
                need("gated", 4)
                for k in range(MT_):
                    for j in range(JT):
                        mm = pe.transpose(G.banks[:, k, j * P:(j + 1) * P], y[:, j, k * P:(k + 1) * P], G.con("ident"))
                    mm.then_inc(S["turned"], 1)

        @block.scalar
        def _(act):
            act.wait_ge(S["edges"], 1)
            with act.Fori(0, M_HEADS) as i:
                need = needer(act, i)
                act.wait_ge(S["turn_done"], i + 1)
                act.activation(pick[:, :], T.pick[:, bass.ds(i * P, P)], ACT.Copy).then_inc(S["picked"], 1)
                for s in range(2):
                    for m in range(4):
                        n = 4 * s + m
                        need("qk_sum", n + 1)
                        if s:
                            need("conv_done", m + 1)
                        act.activation(z[:, m, M_TAPS - 1:], G.banks[:, n, :], ACT.Identity,
                                       bias=G.col("m_conv", 6 * (4 * i + (16 * s + m)) + 5)).then_inc(S["biased"], 1)
                    for m in range(4):
                        need("conv_done", 4 * s + m + 1)
                        act.activation(qk[:, s, m, :], cv[:, m, :], ACT.Silu).then_inc(S["silu_done"], 1)
                for j in range(JT):
                    need("v_sum", j + 1)
                    act.activation(v[:, j, :], G.banks[:, j, :], ACT.Copy).then_inc(S["v_done"], 1)
                for j in range(JT):
                    need("o_sum", j + 1)
                    act.activation(og[:, j, :], G.banks[:, 4 + j, :], ACT.Sigmoid).then_inc(S["o_done"], 1)
                need("diag_done", 4)
                for a in range(JT):
                    for j in range(a, JT):
                        of = dg[:, a, :] if j == a else T.nM[:, i, j * P:(j + 1) * P]
                        ins = act.activation(E[:, a, j * P:(j + 1) * P], of, ACT.Exp, bias=T.ucol[:, pair(a, j), bass.ds(i, 1)])
                    ins.then_inc(S["exp_done"], 1)
                need("inverted", 1)
                for j in range(JT):
                    need("num_sum", j + 1)
                    act.activation(y[:, j, :], G.banks[:, 4 + j, :], ACT.Copy, scale=rc[:, j:j + 1], accum_out=total[:, j:j + 1])\
                       .then_inc(S["y_done"], 1)
                for j in range(JT):
                    need("centred", j + 1)
                    act.activation(cv[:, j, :], y[:, j, :], ACT.Square, accum_out=sqs[:, j:j + 1]).then_inc(S["squared"], 1)
                need("var_in", 1)
                act.activation(rstd, rstd, ACT.Sqrt).then_inc(S["rooted"], 1)
                for k in range(MT_):
                    need("turned", k + 1)
                    act.activation(T.haT[:, 4 * i + k, :], G.banks[:, k, :], ACT.Copy, scale=G.col("m_gain", 4 * i + k))\
                       .then_inc(S["head_done"], 1)

        @block.vector
        def _(dve):
            dve.memset(z[:, :, 0:M_TAPS - 1], 0.0).then_inc(S["edges"], 1)
            dve.sem_inc(S["turn_done"], 1)
            step = Link(dve, S["step"])
            STEPS = 8 * (M_TAPS - 1) + 3
            with dve.Fori(0, M_HEADS) as i:
                need = needer(dve, i)
                step.start(i * STEPS)
                for s in range(2):
                    for m in range(4):
                        at = 6 * (4 * i + (16 * s + m))
                        need("biased", 4 * s + m + 1)
                        if s:
                            need("silu_done", m + 1)
                        for tap in range(M_TAPS):
                            of = z[:, m, tap:tap + SEQ]
                            if tap == 0:
                                step(dve.tensor_scalar(cv[:, m, :], of, G.col("m_conv", at), G.col("m_conv", at + 4), ALU.mult, ALU.add))
                                continue
                            ins = dve.scalar_tensor_tensor(out=cv[:, m, :], in0=of, scalar=G.col("m_conv", at + tap), in1=cv[:, m, :],
                                                           op0=ALU.mult, op1=ALU.add)
                            if tap < M_TAPS - 1:
                                step(ins)
                        ins.then_inc(S["conv_done"], 1)
                for a in range(JT):
                    dve.tensor_tensor(dg[:, a, :], T.nM[:, i, a * P:(a + 1) * P], T.masks[:, SEQ:SEQ + P], ALU.add).then_inc(S["diag_done"], 1)
                for a in range(JT):
                    need("score_sum", a + 1)
                    need("exp_done", a + 1)
                    e = E[:, a, a * P:SEQ]
                    dve.scalar_tensor_tensor(out=e, in0=G.banks[:, a, a * P:SEQ], scalar=M_DIM ** -0.5, in1=e, op0=ALU.mult, op1=ALU.mult)\
                       .then_inc(S["weighed"], 1)
                need("den_sum", 1)
                floor = T.ucol[:, N_PAIRS:N_PAIRS + JT, bass.ds(i, 1)].rearrange("p j o -> p (j o)")
                step(dve.scalar_tensor_tensor(out=rc, in0=G.banks[:, 0, 0:JT], scalar=-1.0, in1=floor, op0=ALU.mult, op1=ALU.max))
                step(dve.tensor_tensor(rc, G.banks[:, 0, 0:JT], rc, ALU.max))
                dve.reciprocal(rc, rc).then_inc(S["inverted"], 1)
                need("y_done", 4)
                dve.tensor_scalar(mean, total, 1.0 / M_DIM, None, ALU.mult).then_inc(S["mean_done"], 4)
                need("mean_done", 4)
                for j in range(JT):
                    dve.tensor_scalar(y[:, j, :], y[:, j, :], mean[:, j:j + 1], None, ALU.subtract).then_inc(S["centred"], 1)
                need("squared", 4)
                dve.tensor_scalar(rstd, sqs, 1.0 / M_DIM, HEAD_EPS, ALU.mult, ALU.add).then_inc(S["var_in"], 1)
                need("rooted", 1)
                step(dve.reciprocal(rstd, rstd))
                for j in range(JT):
                    dve.scalar_tensor_tensor(out=y[:, j, :], in0=y[:, j, :], scalar=rstd[:, j:j + 1], in1=og[:, j, :],
                                             op0=ALU.mult, op1=ALU.mult).then_inc(S["gated"], 1)
                need("head_done", 4)
                dve.sem_inc(S["turn_done"], 1)
                assert step.n == STEPS, step.n

        G.first += 4 * M_HEADS


def hgrn(G, T):
    nc = G.nc
    HH = 4
    IN = 7
    ALL = IN + 2
    PER = dict(q_sum=4, q_done=4, f_sum=4, f_done=4, f_abs=4, f_exp=4, f_log=4, f_ready=4, k_done=4, picked=1, v_sum=4, v_done=4,
               g_sum=4, g_done=4, exp_done=HH * ALL, sums=HH * ALL, operands=HH * ALL, level_sum=HH * (ALL + 1), level_done=HH * (IN + 1),
               far_done=HH * 2, o_sum=HH, o_squared=HH, sq_sum=HH, var_in=HH, rooted=HH, o_done=HH, turn_done=1)
    with ExitStack() as ctx:
        S = stage(G, "hgrn", ctx, "loaded", "step", "go", *PER)
        q = G.sb("hgrn_q", [P, HH, SEQ], ctx=ctx)
        k = G.sb("hgrn_k", [P, HH, SEQ], ctx=ctx)
        lf = G.sb("hgrn_logf", [P, HH, SEQ], ctx=ctx)
        ab = G.hT[:, 0:HH, :]
        v = G.sb("hgrn_v", [P, JT, HH * P], ctx=ctx)
        g = G.sb("hgrn_g", [P, HH, SEQ], ctx=ctx)
        behind = G.sb("hgrn_behind", [P, SEQ], ctx=ctx)
        ex = G.sb("hgrn_exp", [P, 2, 2, SEQ], ctx=ctx)
        w = G.sb("hgrn_weights", [P, JT, SEQ], ctx=ctx)
        sq = G.sb("hgrn_squares", [P, SEQ], ctx=ctx)
        rstd = G.sb("hgrn_rstd", [P, SEQ], ctx=ctx)
        pick = G.sb("hgrn_pick", [M_HEADS, P], ctx=ctx)
        masks = G.sb("hgrn_masks", [P, IN * P], U32, ctx=ctx)
        block = ctx.enter_context(nc.Block())
        diagonal = bass.AP(tensor=w[:, 0, :].tensor, offset=w[:, 0, :].offset, ap=[w[:, 0, :].ap[0], [SEQ + P, JT], [1, P]])

        def needer(eng, i):
            return lambda name, n: eng.wait_ge(S[name], PER[name] * i + n)

        @block.sync
        def _(sp):
            sp.dma_start(masks[:, :], G.aps["pair_masks"]).then_inc(S["loaded"], 16)
            for i in range(2):
                for c, name in enumerate(("q_sum", "f_sum", "v_sum", "g_sum")):
                    sp.wait_ge(S[name], 4 * i + 4)
                    sp.dma_start(G.ring[:, G.slot(c), :], G.weights[4 * i + (G.first + c + SLOTS)])\
                      .then_inc(G.landed[G.slot(c)], 16)

        @block.tensor
        def _(pe):
            with pe.Fori(0, 2) as i:
                need = needer(pe, i)
                pe.wait_ge(S["turn_done"], i + 1)
                for c, name in enumerate(("q_sum", "f_sum", "v_sum", "g_sum")):
                    pe.wait_ge(G.landed[G.slot(c)], 16 * (2 * i + (G.first + c) // SLOTS + 1))
                    wt = G.chunk(c, KT)
                    if c == 2:
                        need("picked", 1)
                        need("q_done", 4)
                    if c == 3:
                        need("k_done", 4)
                    for m in range(4):
                        b = 4 * (c % 2) + m
                        if c != 2:
                            project(pe, G, c, m, b, G.x).then_inc(S[name], 1)
                            continue
                        for kk in range(KT):
                            pe.matmul(G.banks[:, b, :], G.x[:, kk, m * P:(m + 1) * P], wt[:, kk, :], start=(kk == 0), stop=False)
                        pe.matmul(G.banks[:, b, :], pick[:, :], T.brows[:, 2, :], start=False, stop=True).then_inc(S["v_sum"], 1)
                need("v_done", 4)
                need("g_done", 4)
                need("f_ready", 4)
                for h in range(HH):
                    tiles = [slice(j * P, (j + 1) * P) for j in range(JT)]
                    for l in range(-1, ALL):
                        n = h * (ALL + 1) + l + 1
                        b = G.banks[:, n % 2, :]
                        done = h * (IN + 1) + min(l, IN)
                        if l < 0:
                            if h:
                                need("far_done", 2 * h)
                            left, right = k[:, h, :], q[:, h, :]
                        else:
                            need("operands", h * ALL + l + 1)
                            left, right = ex[:, l % 2, 1, :], ex[:, l % 2, 0, :]
                        if 1 <= l <= IN + 1:
                            need("level_done", h * (IN + 1) + l)
                        if l < IN:
                            for j in range(JT):
                                mm = pe.matmul(b[:, tiles[j]], left[:, tiles[j]], right[:, tiles[j]], start=True, stop=True)
                        elif l == IN:
                            for n2, j in enumerate((0, 2)):
                                mm = pe.matmul(b[:, tiles[n2]], left[:, tiles[j]], right[:, tiles[j + 1]], start=True, stop=True)
                        else:
                            for j in range(2):
                                mm = pe.matmul(b[:, j * 256:(j + 1) * 256], left[:, tiles[j]], right[:, 256:512], start=True, stop=True)
                        mm.then_inc(S["level_sum"], 1)
                    need("level_done", (h + 1) * (IN + 1))
                    need("far_done", 2 * h + 2)
                    if h:
                        need("o_done", h)
                    for j in range(JT):
                        mm = pe.matmul(G.banks[:, 2, j * P:SEQ], v[:, j, h * P:(h + 1) * P], w[:, j, j * P:SEQ], start=(j == 0),
                                       stop=(j == JT - 1), skip_group_check=True)
                    mm.then_inc(S["o_sum"], 1)
                    need("o_squared", h + 1)
                    pe.matmul(G.banks[:, 3, :], G.con("ones"), sq[:, :], start=True, stop=True).then_inc(S["sq_sum"], 1)

        @block.scalar
        def _(act):
            with act.Fori(0, 2) as i:
                need = needer(act, i)
                act.wait_ge(S["turn_done"], i + 1)
                act.activation(pick[:, :], T.pick[:, bass.ds(i * P, P)], ACT.Copy).then_inc(S["picked"], 1)
                for m in range(4):
                    need("q_sum", m + 1)
                    act.activation(q[:, m, :], G.banks[:, m, :], ACT.Silu, bias=G.col("b_hq", 4 * i + m)).then_inc(S["q_done"], 1)
                for m in range(4):
                    need("f_sum", m + 1)
                    act.activation(lf[:, m, :], G.banks[:, 4 + m, :], ACT.Identity, bias=G.col("b_hf", 4 * i + m)).then_inc(S["f_done"], 1)
                for m in range(4):
                    need("f_done", m + 1)
                    act.activation(k[:, m, :], lf[:, m, :], ACT.Sigmoid, scale=-1.0).then_inc(S["k_done"], 1)
                for m in range(4):
                    need("v_sum", m + 1)
                    act.activation(v[:, m, :], G.banks[:, m, :], ACT.Copy).then_inc(S["v_done"], 1)
                for m in range(4):
                    need("g_sum", m + 1)
                    act.activation(g[:, m, :], G.banks[:, 4 + m, :], ACT.Sigmoid, bias=G.col("b_hg", 4 * i + m)).then_inc(S["g_done"], 1)
                for m in range(4):
                    need("f_abs", m + 1)
                    act.activation(ab[:, m, :], ab[:, m, :], ACT.Exp, scale=-1.0).then_inc(S["f_exp"], 1)
                for m in range(4):
                    need("f_exp", m + 1)
                    act.activation(ab[:, m, :], ab[:, m, :], ACT.Ln, bias=1.0).then_inc(S["f_log"], 1)
                for h in range(HH):
                    for l in range(ALL):
                        n = h * ALL + l
                        need("sums", n + 1)
                        if l >= 2:
                            need("level_sum", h * (ALL + 1) + l)
                        act.activation(ex[:, l % 2, 0, :], lf[:, h, :], ACT.Exp)
                        act.activation(ex[:, l % 2, 1, :], behind[:, :], ACT.Exp).then_inc(S["exp_done"], 1)
                    need("level_sum", h * (ALL + 1) + IN + 1)
                    need("level_done", (h + 1) * (IN + 1))
                    for l in range(2):
                        b = G.banks[:, (h * (ALL + 1) + IN + l + 1) % 2, :]
                        need("level_sum", h * (ALL + 1) + IN + l + 2)
                        for n2 in range(2):
                            if l == 0:
                                ins = act.activation(w[:, 2 * n2, (2 * n2 + 1) * P:(2 * n2 + 2) * P], b[:, n2 * P:(n2 + 1) * P], ACT.Copy)
                            else:
                                ins = act.activation(w[:, n2, 256:512], b[:, n2 * 256:(n2 + 1) * 256], ACT.Copy)
                        ins.then_inc(S["far_done"], 1)
                    need("o_sum", h + 1)
                    act.activation(sq[:, :], G.banks[:, 2, :], ACT.Square).then_inc(S["o_squared"], 1)
                    need("var_in", h + 1)
                    act.activation(rstd[:, :], rstd[:, :], ACT.Sqrt).then_inc(S["rooted"], 1)

        @block.vector
        def _(dve):
            dve.sem_inc(S["turn_done"], 1)
            dve.wait_ge(S["loaded"], 16)
            step = Link(dve, S["step"])
            STEPS = HH * (2 * (ALL - 1) + 4) + 0
            with dve.Fori(0, 2) as i:
                need = needer(dve, i)
                step.start(i * STEPS)
                for m in range(4):
                    need("f_done", m + 1)
                    dve.scalar_tensor_tensor(out=ab[:, m, :], in0=lf[:, m, :], scalar=-1.0, in1=lf[:, m, :], op0=ALU.mult,
                                             op1=ALU.max).then_inc(S["f_abs"], 1)
                for m in range(4):
                    need("f_log", m + 1)
                    need("k_done", m + 1)
                    dve.scalar_tensor_tensor(out=lf[:, m, :], in0=lf[:, m, :], scalar=0.0, in1=ab[:, m, :], op0=ALU.min,
                                             op1=ALU.subtract).then_inc(S["f_ready"], 1)
                need("f_ready", 4)
                for h in range(HH):
                    F = lf[:, h, :]
                    if h:
                        need("exp_done", h * ALL)
                    step(dve.memset(behind[:, :], 0.0))
                    need("level_sum", h * (ALL + 1) + 1)
                    ident = spread(G.con("ident"), JT)
                    dve.tensor_tensor(diagonal, G.banks[:, (h * (ALL + 1)) % 2, :].rearrange("p (j t) -> p j t", j=JT), ident, ALU.mult)\
                       .then_inc(S["level_done"], 1)
                    need("level_done", h * (IN + 1) + 1)
                    for l in range(ALL):
                        n = h * ALL + l
                        if l:
                            b = 1 << (l - 1)
                            need("exp_done", n)
                            halves = lambda a: a.rearrange("p (n e s) -> p n e s", e=2, s=b)
                            last = lambda a, e: bass.AP(tensor=a.tensor, offset=a[:, e * b + b - 1:e * b + b].offset,
                                                        ap=[a.ap[0], [2 * b, SEQ // (2 * b)], [0, b]])
                            step(dve.tensor_tensor(halves(behind[:, :])[:, :, 0, :], halves(behind[:, :])[:, :, 0, :], last(F, 1), ALU.add))
                            step(dve.tensor_tensor(halves(F)[:, :, 1, :], halves(F)[:, :, 1, :], last(F, 0), ALU.add))
                        dve.sem_inc(S["sums"], 1)
                        need("exp_done", n + 1)
                        dve.tensor_tensor(ex[:, l % 2, 0, :], ex[:, l % 2, 0, :], q[:, h, :], ALU.mult)
                        dve.tensor_tensor(ex[:, l % 2, 1, :], ex[:, l % 2, 1, :], k[:, h, :], ALU.mult).then_inc(S["operands"], 1)
                        if l < IN:
                            m = h * (ALL + 1) + l + 1
                            need("level_sum", m + 1)
                            dve.sem_inc(S["go"], 1)
                            dve.copy_predicated(diagonal, spread(masks[:, l * P:(l + 1) * P], JT),
                                                G.banks[:, m % 2, :].rearrange("p (j t) -> p j t", j=JT)).then_inc(S["level_done"], 1)
                            need("level_done", h * (IN + 1) + l + 2)
                    need("sq_sum", h + 1)
                    dve.tensor_scalar(rstd[:, :], G.banks[:, 3, :], 1.0 / H_DIM, HEAD_EPS, ALU.mult, ALU.add).then_inc(S["var_in"], 1)
                    need("rooted", h + 1)
                    step(dve.reciprocal(rstd[:, :], rstd[:, :]))
                    out = T.hbT[:, 4 * i + h, :]
                    step(dve.scalar_tensor_tensor(out=out, in0=G.banks[:, 2, :], scalar=G.col("h_gain", 4 * i + h), in1=rstd[:, :],
                                                  op0=ALU.mult, op1=ALU.mult))
                    step(dve.tensor_tensor(out, out, g[:, h, :], ALU.mult))
                    dve.sem_inc(S["o_done"], 1)
                dve.sem_inc(S["turn_done"], 1)
                assert step.n == STEPS, (step.n, STEPS)

        G.first += 8


def gated_merge(G, T):
    nc = G.nc
    with ExitStack() as ctx:
        S = stage(G, "merge", ctx, "gate_sum", "gate_done", "used", "branch_sum", "branch_done", "mixed", "out_sum", "added")
        gate = G.sb("merge_gate", [P, 2 * KT, SEQ], ctx=ctx)
        tmp = G.sb("merge_tmp", [P, 2, SEQ], ctx=ctx)
        block = ctx.enter_context(nc.Block())

        @block.sync
        def _(sp):
            G.feed(sp, 4, S["gate_sum"], per=4)
            G.first += 4
            G.feed(sp, 6, S["used"])
            G.first += 6
            G.feed(sp, 2, S["out_sum"], per=4)
            G.first -= 10

        @block.tensor
        def _(pe):
            for c in range(4):
                G.arrived(pe, c % 2, c // 2)
                for m in range(4):
                    n = 4 * c + m
                    if n >= 8:
                        pe.wait_ge(S["gate_done"], n - 7)
                    project(pe, G, c % 2, m, n % 8, G.x).then_inc(S["gate_sum"], 1)
            pe.wait_ge(S["gate_done"], 16)
            for branch, of, chunks in ((0, T.haT, range(4, 8)), (1, T.hbT, range(8, 10))):
                if branch:
                    pe.wait_ge(S["branch_done"], KT)
                for c in chunks:
                    G.arrived(pe, c % 2, c // 2)
                    w = G.chunk(c % 2, 4)
                    for m in range(KT):
                        for k in range(4):
                            kk = 4 * (c - chunks[0]) + k
                            mm = pe.matmul(G.banks[:, m, :], w[:, k, m * P:(m + 1) * P], of[:, kk, :], start=(kk == 0),
                                           stop=(kk == 4 * len(chunks) - 1), skip_group_check=True)
                    mm.then_inc(S["used"], 1)
            pe.wait_ge(S["mixed"], KT)
            for m in range(KT):
                if m % 4 == 0:
                    G.arrived(pe, m // 4, 5)
                project(pe, G, m // 4, m % 4, m, G.hT).then_inc(S["out_sum"], 1)

        @block.scalar
        def _(act):
            for n in range(16):
                act.wait_ge(S["gate_sum"], n + 1)
                act.activation(gate[:, n, :], G.banks[:, n % 8, :], ACT.Sigmoid, bias=G.col("b_ga" if n < KT else "b_gb", n % KT))\
                   .then_inc(S["gate_done"], 1)

        @block.vector
        def _(dve):
            dve.wait_ge(S["gate_done"], 16)
            for m in range(KT):
                dve.wait_ge(S["used"], 4)
                dve.tensor_tensor(G.hT[:, m, :], G.banks[:, m, :], gate[:, m, :], ALU.mult).then_inc(S["branch_done"], 1)
            for m in range(KT):
                dve.wait_ge(S["used"], 6)
                if m >= 2:
                    dve.wait_ge(S["mixed"], m - 1)
                dve.tensor_tensor(tmp[:, m % 2, :], G.banks[:, m, :], gate[:, KT + m, :], ALU.mult).then_inc(S["branch_done"], 1)
                dve.wait_ge(S["branch_done"], KT + m + 1)
                dve.tensor_tensor(G.hT[:, m, :], G.hT[:, m, :], tmp[:, m % 2, :], ALU.add).then_inc(S["mixed"], 1)
            for m in range(KT):
                dve.wait_ge(S["out_sum"], m + 1)
                dve.scalar_tensor_tensor(out=G.x[:, m, :], in0=G.x[:, m, :], scalar=ALPHA, in1=G.banks[:, m, :],
                                         op0=ALU.mult, op1=ALU.add).then_inc(S["added"], 1)

        G.first += 12


def layer_norm(G, name, gain, bias):
    nc = G.nc
    with ExitStack() as ctx:
        S = stage(G, name, ctx, "summed", "mean_done", "centred", "squared", "squares_summed", "var_done", "root_done", "rstd_done",
                  "scaled", "shifted")
        sq = G.sb(name + "_squares", [P, KT, SEQ], ctx=ctx)
        mu = G.sb(name + "_mean", [P, SEQ], ctx=ctx)
        rstd = G.sb(name + "_rstd", [P, SEQ], ctx=ctx)
        block = ctx.enter_context(nc.Block())

        @block.tensor
        def _(pe):
            for k in range(KT):
                mm = pe.matmul(G.banks[:, 0, :], G.con("ones"), G.x[:, k, :], start=(k == 0), stop=(k == KT - 1))
            mm.then_inc(S["summed"], 1)
            for k in range(KT):
                pe.wait_ge(S["squared"], k + 1)
                mm = pe.matmul(G.banks[:, 1, :], G.con("ones"), sq[:, k, :], start=(k == 0), stop=(k == KT - 1))
            mm.then_inc(S["squares_summed"], 1)

        @block.scalar
        def _(act):
            for k in range(KT):
                act.wait_ge(S["centred"], k + 1)
                act.activation(sq[:, k, :], G.x[:, k, :], ACT.Square).then_inc(S["squared"], 1)
            act.wait_ge(S["var_done"], 1)
            act.activation(rstd[:, :], rstd[:, :], ACT.Sqrt).then_inc(S["root_done"], 1)
            for k in range(KT):
                act.wait_ge(S["scaled"], k + 1)
                act.activation(G.x[:, k, :], G.x[:, k, :], ACT.Identity, bias=G.col(bias, k)).then_inc(S["shifted"], 1)

        @block.vector
        def _(dve):
            dve.wait_ge(S["summed"], 1)
            dve.tensor_scalar(mu[:, :], G.banks[:, 0, :], 1.0 / D, None, ALU.mult).then_inc(S["mean_done"], 1)
            dve.wait_ge(S["mean_done"], 1)
            for k in range(KT):
                dve.tensor_tensor(G.x[:, k, :], G.x[:, k, :], mu[:, :], ALU.subtract).then_inc(S["centred"], 1)
            dve.wait_ge(S["squares_summed"], 1)
            dve.tensor_scalar(rstd[:, :], G.banks[:, 1, :], 1.0 / D, LN_EPS, ALU.mult, ALU.add).then_inc(S["var_done"], 1)
            dve.wait_ge(S["root_done"], 1)
            dve.reciprocal(rstd[:, :], rstd[:, :]).then_inc(S["rstd_done"], 1)
            dve.wait_ge(S["rstd_done"], 1)
            for k in range(KT):
                dve.scalar_tensor_tensor(out=G.x[:, k, :], in0=G.x[:, k, :], scalar=G.col(gain, k), in1=rstd[:, :],
                                         op0=ALU.mult, op1=ALU.mult).then_inc(S["scaled"], 1)


def third_block(G):
    with ExitStack() as ctx:
        T = Shared()
        T.haT = G.sb("mlstm_out_T", [P, M_HEADS * MT_, SEQ], ctx=ctx)
        T.hbT = G.sb("hgrn_out_T", [P, H_HEADS, SEQ], ctx=ctx)
        with ExitStack() as inner:
            T.masks = G.sb("third_masks_sb", list(G.aps["third_masks"].shape), ctx=inner)
            T.pick = T.masks[0:M_HEADS, SEQ + P:SEQ + P + M_HEADS * P]
            T.brows = G.sb("bias_rows3_sb", [M_HEADS, 3, SEQ], ctx=inner)
            T.nM = G.sb("minus_max", [P, M_HEADS, SEQ], ctx=inner)
            T.ucol = G.sb("gate_columns", [P, N_PAIRS + JT, M_HEADS], ctx=inner)
            mlstm_gates(G, T)
            mlstm(G, T)
            hgrn(G, T)
        gated_merge(G, T)
    layer_norm(G, "ln1", "ln1_g", "ln1_b")
    feed_forward(G, "ffn4", None, None, ACT.Silu, keep=ALPHA)
    layer_norm(G, "ln2", "ln2_g", "ln2_b")



def load(G):
    nc = G.nc
    with ExitStack() as ctx:
        S = stage(G, "load", ctx, "loaded")
        block = ctx.enter_context(nc.Block())

        @block.sync
        def _(sp):
            sp.dma_start(G.x[:, :, :], G.aps["x"].rearrange("(k p) n -> p k n", p=P)).then_inc(S["loaded"], 16)
            sp.dma_start(G.cols[:, :], G.aps["columns"]).then_inc(S["loaded"], 16)
            sp.dma_start(G.const[:, :], G.aps["constants"]).then_inc(S["loaded"], 16)
            for s in range(SLOTS):
                sp.dma_start(G.ring[:, s, :], G.weights[s]).then_inc(G.landed[s], 16)
            sp.wait_ge(S["loaded"], 48)


def store(G):
    nc = G.nc
    with ExitStack() as ctx:
        S = stage(G, "store", ctx, "stored")
        block = ctx.enter_context(nc.Block())

        @block.sync
        def _(sp):
            sp.dma_start(G.aps["out"].rearrange("(k p) n -> p k n", p=P), G.x[:, :, :]).then_inc(S["stored"], 16)
            sp.wait_ge(S["stored"], 16)


def three_blocks_kernel(nc, aps, layout):
    with ExitStack() as ctx:
        G = Core(nc, aps, layout, ctx)
        load(G)
        first_block(G)
        second_block(G)
        third_block(G)
        store(G)



def host_arrays(a):
    second = {n[:-2]: v for n, v in a.items() if n.endswith("_2")}
    third = {n[:-2]: v for n, v in a.items() if n.endswith("_3")}
    L = Layout()
    L.constant("ident", np.eye(P, dtype=np.float32))
    L.constant("ones", np.ones((P, P), np.float32))
    lay_first(L, a)
    lay_second(L, second)
    lay_third(L, third)
    arrays = {"weights": np.stack(L.chunks), "columns": np.concatenate(L.column_parts, 1),
              "constants": np.concatenate(L.constant_parts, 1), "x": a["x"][0].T, "pT": a["p"][0, 0].T,
              "buckets": bucket_rows(), **second_extra(), **third_extra(third)}
    return {n: np.ascontiguousarray(v) for n, v in arrays.items()}, {"columns": L.columns, "constants": L.constants}


def kernel(**inputs):
    import concourse.bacc as bacc
    from concourse.bass_utils import run_bass_kernel_spmd

    arrays, layout = host_arrays({n: np.asarray(v) for n, v in inputs.items()})
    nc = bacc.Bacc("TRN2", target_bir_lowering=False, num_devices=1)
    aps = {n: nc.dram_tensor(n, v.shape, mybir.dt.from_np(v.dtype), kind="ExternalInput").ap() for n, v in arrays.items()}
    aps["out"] = nc.dram_tensor("out", (D, SEQ), F32, kind="ExternalOutput").ap()
    three_blocks_kernel(nc, aps, layout)
    r = run_bass_kernel_spmd(nc, [arrays], core_ids=[0])
    return np.ascontiguousarray(r.results[0]["out"].T)[None]
```

```python
from contextlib import ExitStack

import numpy as np

import concourse.bass as bass
from concourse import mybir

ALU = mybir.AluOpType
ACT = mybir.ActivationFunctionType
F32 = mybir.dt.float32
F32R = mybir.dt.float32r
U32 = mybir.dt.uint32
AX = mybir.AxisListType.X

P = 128
SEQ = 512
D = 1024
KT = D // P
JT = SEQ // P
SLOTS = 2
CHUNK = 4096
FF = 2816
FT = FF // P
UP_CHUNKS = FT // 2
DOWN_CHUNKS = -(-FT // 4)
EPS = 1e-6
NEG = -1e30


class Link:

    def __init__(self, eng, sem):
        self.eng, self.sem, self.base, self.n = eng, sem, 0, 0

    def start(self, base):
        self.base, self.n = base, 0

    def mark(self, ins):
        ins.then_inc(self.sem, 1)
        self.n += 1
        return self.n

    def settle(self, upto=None):
        self.eng.wait_ge(self.sem, self.base + (self.n if upto is None else upto))

    def __call__(self, ins):
        self.mark(ins)
        self.settle()


def pairs(eng, count, body):
    if count >= 4:
        with eng.Fori(0, count // 2) as i:
            body(0, i)
            body(1, i)
    else:
        for i in range(count // 2):
            body(0, i)
            body(1, i)
    if count % 2:
        body(0, count // 2)


class Core:

    def __init__(self, nc, aps, layout, ctx):
        self.nc, self.aps, self.layout, self.ctx = nc, aps, layout, ctx
        self.weights = aps["weights"]
        self.total = self.weights.shape[0]
        self.first = 0
        self.cleared = []
        sb = self.sb
        self.ring = sb("weight_ring", [P, SLOTS, CHUNK])
        self.cols = sb("columns_sb", list(aps["columns"].shape))
        self.const = sb("constants_sb", list(aps["constants"].shape))
        self.banks = ctx.enter_context(nc.psum_tensor("banks", [P, 8, 512], F32))
        self.landed = [ctx.enter_context(nc.semaphore(f"weights_landed_{s}")) for s in range(SLOTS)]
        self.x = sb("residual", [P, KT, SEQ])
        self.hT = sb("normed", [P, KT, SEQ])

    def sb(self, name, shape, dt=F32, ctx=None):
        return (ctx or self.ctx).enter_context(self.nc.sbuf_tensor(name, shape, dt))

    def col(self, name, i=0, n=1):
        at = self.layout["columns"][name][0]
        return self.cols[:, bass.ds(i + at, n)] if not isinstance(i, int) else self.cols[:, at + i:at + i + n]

    def con(self, name):
        at, n = self.layout["constants"][name]
        return self.const[:, at:at + n]

    def slot(self, p):
        return (self.first + p) % SLOTS

    def chunk(self, p, k):
        return self.ring[:, self.slot(p), :].rearrange("p (k n) -> p k n", k=k)

    def arrived(self, pe, p, i):
        pe.wait_ge(self.landed[self.slot(p)], 16 * (i + (self.first + p) // SLOTS + 1))

    def feed(self, sp, count, used, per=1, base=0):
        def load(p, i):
            n = self.first + p + 2 * i
            if isinstance(i, int) and n + SLOTS >= self.total:
                return
            sp.wait_ge(used, base + per * (p + 2 * i + 1))
            sp.dma_start(self.ring[:, self.slot(p), :], self.weights[n + SLOTS]).then_inc(self.landed[self.slot(p)], 16)

        if self.first + count + SLOTS > self.total:
            for c in range(count):
                load(c % 2, c // 2)
        else:
            pairs(sp, count, load)


class Shared:
    pass


def stage(G, name, ctx, *semaphores):
    S = {s: G.nc.alloc_semaphore(f"{name}_{s}") for s in semaphores}

    def retire():
        for sem in G.cleared:
            G.nc.release_semaphore(sem)
        G.cleared = list(S.values())
        for sem in G.cleared:
            G.nc.gpsimd.sem_clear(sem)

    ctx.callback(retire)
    return S


def rms_act(act, G, S, sq):
    for k in range(KT):
        act.activation(sq[:, k, :], G.x[:, k, :], ACT.Square).then_inc(S["squared"], 1)


def rms_root(act, G, S, rstd):
    act.wait_ge(S["mean_done"], 1)
    act.activation(rstd[:, :], rstd[:, :], ACT.Sqrt).then_inc(S["root_done"], 1)


def rms_pe(pe, G, S, sq, bank):
    for k in range(KT):
        pe.wait_ge(S["squared"], k + 1)
        mm = pe.matmul(G.banks[:, bank, :], G.con("ones"), sq[:, k, :], start=(k == 0), stop=(k == KT - 1))
    mm.then_inc(S["summed"], 1)


def rms_dve(dve, G, S, rstd, bank, gain, out):
    dve.wait_ge(S["summed"], 1)
    dve.tensor_scalar(rstd[:, :], G.banks[:, bank, :], 1.0 / D, EPS, ALU.mult, ALU.add).then_inc(S["mean_done"], 1)
    dve.wait_ge(S["root_done"], 1)
    dve.reciprocal(rstd[:, :], rstd[:, :]).then_inc(S["rstd_done"], 1)
    dve.wait_ge(S["rstd_done"], 1)
    for k in range(KT):
        dve.scalar_tensor_tensor(out=out[:, k, :], in0=G.x[:, k, :], scalar=G.col(gain, k), in1=rstd[:, :],
                                 op0=ALU.mult, op1=ALU.mult).then_inc(S["h_ready"], 1)


RMS = ("squared", "summed", "mean_done", "root_done", "rstd_done", "h_ready")


def project(pe, G, p, m, bank, rhs, k_tiles=KT, first_wait=None):
    w = G.chunk(p, max(k_tiles, 4))
    for k in range(k_tiles):
        if first_wait is not None:
            pe.wait_ge(first_wait, k + 1)
        mm = pe.matmul(G.banks[:, bank, :], w[:, k, m * P:(m + 1) * P], rhs[:, k, :],
                       start=(k == 0), stop=(k == k_tiles - 1))
    return mm


def exact_product(pe, out, w, x, start, stop):
    pe.matmul(out, w[1], x[0], start=start, stop=False, skip_group_check=True)
    pe.matmul(out, w[0], x[1], start=False, stop=False, skip_group_check=True)
    return pe.matmul(out, w[0], x[0], start=False, stop=stop, skip_group_check=True)


def feed_forward(G, name, gain, taps, act_func, shift=0, keep=1.0):
    nc = G.nc
    conv = taps is not None
    chunks = UP_CHUNKS + DOWN_CHUNKS
    up_halves, down_halves = 2 * UP_CHUNKS, FT // 2
    half = CHUNK // 2
    with ExitStack() as ctx:
        S = stage(G, name, ctx, *RMS, "h_high", "h_split", "rounded", "split", "gate_val", "gate_free", "value_free", "centre", "tap",
                  "activated", "hidden", "tile_high", "tile_split", "down_used", "down_done", "added")
        gT = G.sb(name + "_hidden", [P, FT, SEQ], ctx=ctx)
        sq = gT[:, 0:KT, :]
        rstd = G.sb(name + "_rstd", [P, SEQ], ctx=ctx)
        gc = G.sb(name + "_gate", [P, 2, SEQ], ctx=ctx)
        vc = G.sb(name + "_value", [P, 2, SEQ], ctx=ctx)
        w_parts = [G.sb(name + "_weights_" + part, [P, 2, half], F32R, ctx=ctx) for part in ("high", "low")]
        h_parts = [G.sb(name + "_in_" + part, [P, KT, SEQ], F32R, ctx=ctx) for part in ("high", "low")]
        of = G.x if gain is None else G.hT
        block = ctx.enter_context(nc.Block())

        def landed_half(p, h, up):
            if up:
                return G.chunk(p, KT)[:, :, h * 256:(h + 1) * 256], [w[:, h, :].rearrange("p (k n) -> p k n", k=KT) for w in w_parts]
            return G.ring[:, G.slot(p), h * half:(h + 1) * half], [w[:, h, :] for w in w_parts]

        @block.sync
        def _(sp):
            G.feed(sp, chunks - 1, S["split"], per=2)
            G.first += chunks - 1
            G.feed(sp, 1, S["split"], base=2 * (chunks - 1))
            G.first -= chunks - 1

        @block.gpsimd
        def _(pool):
            def low(p, i, h, up):
                landed, parts = landed_half(p, h, up)
                pool.wait_ge(S["rounded"], 4 * i + 2 * p + h + 1)
                pool.tensor_tensor(parts[1], landed, parts[0].bitcast(F32), ALU.subtract).then_inc(S["split"], 1)

            def chunk(p, i):
                for h in range(2):
                    low(p, i, h, True)

            pairs(pool, UP_CHUNKS, chunk)
            for n in range(up_halves, up_halves + down_halves):
                low(n // 2 % 2, n // 4, n % 2, False)

        @block.tensor
        def _(pe):
            if gain is not None:
                rms_pe(pe, G, S, sq, 7)

            def up(p, i):
                for h in range(2):
                    pe.wait_ge(S["split"], 4 * i + 2 * p + h + 1)
                    w = landed_half(p, h, True)[1]
                    for m in range(2):
                        pe.wait_ge(S["value_free"] if conv and m else S["gate_free"], 4 * i + 2 * p + h + 1)
                        for k in range(KT):
                            if p == h == m == 0:
                                pe.wait_ge(S["h_split"], k + 1)
                            mm = exact_product(pe, G.banks[:, 4 * p + 2 * h + m, :], [x[:, k, m * P:(m + 1) * P] for x in w],
                                               [x[:, k, :] for x in h_parts], start=(k == 0), stop=(k == KT - 1))
                        mm.then_inc(S["gate_val"], 1)

            pairs(pe, UP_CHUNKS, up)

            for t in range(FT):
                if t % 2 == 0:
                    pe.wait_ge(S["split"], up_halves + t // 2 + 1)
                pe.wait_ge(S["tile_split"], t + 1)
                for m in (*range(4, KT), *range(4)):
                    if t == 0 and m % 4 == 0:
                        pe.wait_ge(S["gate_free"], 4 + FT - (2 if m else 0))
                        if conv:
                            pe.wait_ge(S["value_free"], 4 + FT - (2 if m else 0))
                    at = t % 2 * D + m * P
                    mm = exact_product(pe, G.banks[:, m, :], [w[:, t // 2 % 2, at:at + P] for w in w_parts],
                                       [x[:, t % KT, :] for x in h_parts], start=(t == 0), stop=(t == FT - 1))
                    if t == FT - 1:
                        mm.then_inc(S["down_done"], 1)
                if t % 2 and t < FT - 1:
                    mm.then_inc(S["down_used"], 1)

        @block.scalar
        def _(act):
            def high(p, i, h, up):
                G.arrived(act, p, i)
                landed, parts = landed_half(p, h, up)
                act.activation(parts[0], landed, ACT.Copy).then_inc(S["rounded"], 1)

            if gain is not None:
                rms_act(act, G, S, sq)
            for h in range(2):
                high(0, 0, h, True)
            if gain is not None:
                rms_root(act, G, S, rstd)
            for k in range(KT):
                if gain is not None:
                    act.wait_ge(S["h_ready"], k + 1)
                act.activation(h_parts[0][:, k, :], of[:, k, :], ACT.Copy).then_inc(S["h_high"], 1)

            def chunk(p, i):
                for h in range(2):
                    t = 4 * i + 2 * p + h
                    b = 4 * p + 2 * h
                    act.wait_ge(S["gate_val"], 8 * i + 4 * p + 2 * h + 2)
                    high(1 - p, i + p, h, isinstance(i, int) is False or 2 * i + p + 1 < UP_CHUNKS)
                    act.wait_ge(S["hidden"], t + 1)
                    if conv:
                        act.activation(gc[:, h, :], G.banks[:, b, :], ACT.Identity, bias=G.col(taps, 8 * t + 3),
                                       scale=G.col(taps, 8 * t + 2 - shift)).then_inc(S["centre"], 1)
                        act.activation(vc[:, h, :], G.banks[:, b + 1, :], ACT.Identity, bias=G.col(taps, 8 * t + 7),
                                       scale=G.col(taps, 8 * t + 6 - shift)).then_inc(S["centre"], 1)
                        act.wait_ge(S["gate_free"], 4 + t + 1)
                        act.activation(gc[:, h, :], gc[:, h, :], act_func).then_inc(S["activated"], 1)
                    else:
                        act.activation(gc[:, h, :], G.banks[:, b, :], act_func).then_inc(S["activated"], 1)

            pairs(act, UP_CHUNKS, chunk)
            for t in range(FT):
                if t >= KT and t % 2 == 0:
                    act.wait_ge(S["down_used"], t // 2 - 3)
                    n = up_halves + t // 2 - 2
                    high(n // 2 % 2, n // 4, n % 2, False)
                act.wait_ge(S["hidden"], 2 + t + 1)
                act.activation(h_parts[0][:, t % KT, :], gT[:, t, :], ACT.Copy).then_inc(S["tile_high"], 1)
            for j in range(FT // 2 - 2, down_halves):
                act.wait_ge(S["down_used"], j - 1)
                n = up_halves + j
                high(n // 2 % 2, n // 4, n % 2, False)

        @block.vector
        def _(dve):
            dve.sem_inc(S["gate_free"], 4)
            dve.sem_inc(S["value_free"], 4)
            dve.sem_inc(S["hidden"], 2)
            if gain is not None:
                rms_dve(dve, G, S, rstd, 7, gain, G.hT)
            for k in range(KT):
                dve.wait_ge(S["h_high"], k + 1)
                dve.tensor_tensor(h_parts[1][:, k, :], of[:, k, :], h_parts[0][:, k, :].bitcast(F32), ALU.subtract).then_inc(S["h_split"], 1)
            n = SEQ
            if shift == 0:
                sides = [(0, slice(2, n), slice(0, n - 2)), (1, slice(1, n), slice(0, n - 1))]
            else:
                sides = [(0, slice(1, n), slice(0, n - 1)), (2, slice(0, n - 1), slice(1, n))]

            def chunk(p, i):
                for h in range(2):
                    t = 4 * i + 2 * p + h
                    b = 4 * p + 2 * h
                    if conv:
                        dve.wait_ge(S["centre"], 2 * t + 2)
                        for s, (tap, to, of) in enumerate(sides):
                            for q, buf in enumerate((gc, vc)):
                                if s == 1:
                                    dve.wait_ge(S["tap"], 2 * t + q + 1)
                                ins = dve.scalar_tensor_tensor(
                                    out=buf[:, h, to], in0=G.banks[:, b + q, of], scalar=G.col(taps, 8 * t + 4 * q + tap),
                                    in1=buf[:, h, to], op0=ALU.mult, op1=ALU.add)
                                if s == 0:
                                    ins.then_inc(S["tap"], 1)
                                else:
                                    ins.then_inc((S["gate_free"], S["value_free"])[q], 1)
                        dve.wait_ge(S["activated"], t + 1)
                        dve.wait_ge(S["value_free"], 4 + t + 1)
                        value = vc[:, h, :]
                    else:
                        dve.wait_ge(S["gate_val"], 2 * t + 2)
                        dve.wait_ge(S["activated"], t + 1)
                        value = G.banks[:, b + 1, :]
                    dve.tensor_tensor(gT[:, t, :], gc[:, h, :], value, ALU.mult).then_inc(S["hidden"], 1)
                    if not conv:
                        dve.wait_ge(S["hidden"], 2 + t + 1)
                        dve.sem_inc(S["gate_free"], 1)

            pairs(dve, UP_CHUNKS, chunk)
            for t in range(FT):
                dve.wait_ge(S["tile_high"], t + 1)
                dve.tensor_tensor(h_parts[1][:, t % KT, :], gT[:, t, :], h_parts[0][:, t % KT, :].bitcast(F32), ALU.subtract)\
                   .then_inc(S["tile_split"], 1)
            for n, m in enumerate((*range(4, KT), *range(4))):
                dve.wait_ge(S["down_done"], n + 1)
                dve.scalar_tensor_tensor(out=G.x[:, m, :], in0=G.x[:, m, :], scalar=keep, in1=G.banks[:, m, :],
                                         op0=ALU.mult, op1=ALU.add).then_inc(S["added"], 1)

        G.first += UP_CHUNKS + DOWN_CHUNKS



class Layout:
    def __init__(self):
        self.chunks, self.column_parts, self.columns, self.n_columns = [], [], {}, 0
        self.constant_parts, self.constants, self.n_constants = [], {}, 0

    def chunk(self, *parts):
        c = np.zeros((P, CHUNK), np.float32)
        at = 0
        for part in parts:
            c[:part.shape[0], at:at + part.shape[1]] = part
            at += part.shape[1]
        assert at <= CHUNK
        self.chunks.append(c)

    def matrix(self, w):
        k = w.shape[0] // P
        return w.reshape(k, P, w.shape[1]).transpose(1, 0, 2).reshape(P, k * w.shape[1])

    def column_chunks(self, w, order=None):
        if order is not None:
            w = w[:, order]
        for c in range(0, w.shape[1], 512):
            self.chunk(self.matrix(w[:, c:c + 512]))

    def row_chunks(self, w):
        for r in range(0, w.shape[0], 512):
            self.chunk(self.matrix(w[r:r + 512]))

    def column(self, name, value):
        self.columns[name] = (self.n_columns, value.shape[1])
        c = np.zeros((P, value.shape[1]), np.float32)
        c[:value.shape[0]] = value
        self.column_parts.append(c)
        self.n_columns += value.shape[1]

    def vector(self, name, v):
        self.column(name, v.reshape(-1, P).T)

    def constant(self, name, value):
        self.constants[name] = (self.n_constants, value.shape[1])
        c = np.zeros((P, value.shape[1]), np.float32)
        c[:value.shape[0]] = value
        self.constant_parts.append(c)
        self.n_constants += value.shape[1]

    def up_order(self):
        t = np.arange(FT)
        return (np.stack([t, t + FT], 1).reshape(-1, 1) * P + np.arange(P)).reshape(-1)

    def ff_taps(self, name, w, b):
        four = np.concatenate([w, b[None]], 0).reshape(4, 2, FT, P)
        self.column(name, four.transpose(3, 2, 1, 0).reshape(P, FT * 8))



HEADS, GROUPS, DH = 8, 2, 64
PER_GROUP = HEADS // GROUPS
L_CMP, D_STRIDE = 32, 16
N_CMP = (SEQ - L_CMP) // D_STRIDE + 1
TAPS = 31
CT = 4
BIAS_W = 896
BIAS_ROW = 1024


def lay_first(L, a):
    w_in = a["w_in"][0]
    tile = lambda at, t: at + t * P + np.arange(P)
    q0, kv0, ng0, mg0 = 1024, 1536, 2304, 2328
    for c in range(2):
        L.column_chunks(w_in, np.concatenate([tile(0, 2 * c), tile(512, 2 * c), tile(0, 2 * c + 1), tile(512, 2 * c + 1)]))
    d = np.arange(DH)
    L.column_chunks(w_in, np.concatenate([q0 + (g * PER_GROUP + t) * DH + d for t in range(PER_GROUP) for g in range(GROUPS)]))
    L.column_chunks(w_in, np.concatenate([kv0 + (s * GROUPS + g) * DH + d for s in (0, 1) for g in range(GROUPS) for _ in range(2)]))
    L.column_chunks(w_in, np.concatenate([kv0 + s * P + np.arange(P) for s in (2, 4, 3, 5)]))
    L.column_chunks(w_in[:, mg0:mg0 + 2 * D])
    L.chunk(L.matrix(np.ascontiguousarray(w_in[:, ng0:ng0 + 24])), L.matrix(a["w_ck2"][0]), L.matrix(a["w_cv2"][0]))
    L.chunk(L.matrix(a["w_ck1"][0]))
    L.chunk(L.matrix(a["w_cv1"][0]))
    L.row_chunks(a["w_conv_out"][0])
    L.row_chunks(a["w_attn_out"][0])
    L.column_chunks(a["w_out"][0])
    L.column_chunks(a["w_up"][0], L.up_order())
    L.row_chunks(a["w_down"][0])
    L.column_chunks(a["w_ple_gate"][0])
    L.chunk(L.matrix(a["w_ple"][0]))
    L.vector("norm_mix", a["norm_mix"][0])
    L.column("conv_w", a["conv_dw_w"][0].reshape(TAPS, CT, P).transpose(2, 1, 0).reshape(P, CT * TAPS))
    for n in ("conv_dw_b", "conv_ln_g", "conv_ln_b", "norm_ffn", "norm_ple"):
        L.vector(n, a[n][0])
    L.vector("pe_k", a["cmp_pe_k"][0].reshape(-1))
    L.vector("pe_v", a["cmp_pe_v"][0].reshape(-1))
    L.ff_taps("ffn_taps", a["ffn_dw_w"][0], a["ffn_dw_b"][0])
    L.vector("norm_final", a["norm_final"])
    L.column("rel_bias", np.concatenate([a["rel_bias"], np.full((1, HEADS), NEG, np.float32)]))
    L.constant("seen_cmp", (np.arange(P) >= L_CMP - 1).astype(np.float32)[:, None])


def bucket_rows():
    n = 511 - np.arange(BIAS_ROW)
    m = np.maximum(n, 0)
    far = 16 + (np.log(np.maximum(m, 16).astype(np.float32) / np.float32(16)) / np.float32(np.log(8.0)) * np.float32(16)).astype(np.int32)
    b = np.where(m < 16, m, np.minimum(far, 31))
    b = np.where(n < 0, 32, b)
    return (np.arange(33)[:, None] == b[None]).astype(np.float32)


def bias_tiles(G, W):
    nc = G.nc
    rows_dram = nc.dram_tensor("bias_rows", [HEADS, 2, BIAS_ROW], F32, kind="Internal")
    with ExitStack() as ctx:
        S = stage(G, "bias", ctx, "loaded", "looked_up", "copied", "stored", "spread")
        onehot = G.sb("bucket_onehot", [33, BIAS_ROW], ctx=ctx)
        rows = G.sb("bias_rows_sb", [HEADS, BIAS_ROW], ctx=ctx)
        block = ctx.enter_context(nc.Block())

        @block.sync
        def _(sp):
            sp.dma_start(onehot[:, :], G.aps["buckets"]).then_inc(S["loaded"], 16)
            sp.wait_ge(S["copied"], 2)
            for c in range(2):
                sp.dma_start(rows_dram.ap()[:, c, :], rows[:, :]).then_inc(S["stored"], 16)
            sp.wait_ge(S["stored"], 32)
            for h in range(HEADS):
                sp.dma_start(W[:, h, :], bass.AP(tensor=rows_dram, offset=h * 2 * BIAS_ROW + P - 1,
                                                 ap=[[BIAS_ROW - P // 2, 2], [-1, P // 2], [1, BIAS_W]])).then_inc(S["spread"], 16)
            sp.wait_ge(S["spread"], 16 * HEADS)

        @block.tensor
        def _(pe):
            pe.wait_ge(S["loaded"], 16)
            for n in range(2):
                pe.matmul(G.banks[0:HEADS, n, :], G.col("rel_bias", 0, HEADS)[0:33, :], onehot[:, n * 512:(n + 1) * 512],
                          start=True, stop=True).then_inc(S["looked_up"], 1)

        @block.scalar
        def _(act):
            for n in range(2):
                act.wait_ge(S["looked_up"], n + 1)
                act.activation(rows[:, n * 512:(n + 1) * 512], G.banks[0:HEADS, n, :], ACT.Copy).then_inc(S["copied"], 1)


def in_projection(G, T):
    nc = G.nc
    with ExitStack() as ctx:
        S = stage(G, "in", ctx, *RMS, "tile_done", "gate_done", "glu_done", "evacuated", "padded", "tap_done")
        sq = T.mgT[:, 0:KT, :]
        rstd = G.sb("in_rstd", [P, SEQ], ctx=ctx)
        sg = G.sb("in_glu_gate", [P, 2, SEQ], ctx=ctx)
        block = ctx.enter_context(nc.Block())
        STRAIGHT, MERGE = 5, 4

        @block.sync
        def _(sp):
            G.feed(sp, STRAIGHT, S["tile_done"], per=4)
            G.first += STRAIGHT
            G.feed(sp, MERGE, S["tile_done"], per=4, base=4 * STRAIGHT)
            G.first -= STRAIGHT

        @block.tensor
        def _(pe):
            rms_pe(pe, G, S, sq, 7)
            for c in range(STRAIGHT):
                p, i = c % 2, c // 2
                G.arrived(pe, p, i)
                if c in (2, 3):
                    pe.wait_ge(S["glu_done"], 2 * (c - 1))
                if c == 4:
                    pe.wait_ge(S["evacuated"], 4)
                for m in range(4 if c < 4 else 2):
                    project(pe, G, p, m, 4 * p + m, G.hT, first_wait=S["h_ready"] if c == 0 and m == 0 else None)\
                        .then_inc(S["tile_done"], 1)
            w = G.chunk(p, KT)
            for j in range(JT):
                for k in range(KT):
                    mm = pe.matmul(G.banks[:, 4 * p + 2 + j // 2, (j % 2) * 256:(j % 2) * 256 + 256],
                                   G.hT[:, k, j * P:(j + 1) * P], w[:, k, 256:512], start=(k == 0), stop=(k == KT - 1))
                if j % 2:
                    mm.then_inc(S["tile_done"], 1)
            G.first += STRAIGHT

            def merge(p, i):
                G.arrived(pe, p, i)
                pe.wait_ge(S["evacuated"], 8 * i + 4 * p + 8)
                for m in range(4):
                    project(pe, G, p, m, 4 * ((STRAIGHT + p) % 2) + m, G.hT).then_inc(S["tile_done"], 1)

            pairs(pe, MERGE, merge)
            G.first -= STRAIGHT

        @block.scalar
        def _(act):
            rms_act(act, G, S, sq)
            rms_root(act, G, S, rstd)
            for c in range(2):
                for h in range(2):
                    act.wait_ge(S["tile_done"], 4 * c + 2 * h + 2)
                    if c:
                        act.wait_ge(S["glu_done"], h + 1)
                    act.activation(sg[:, h, :], G.banks[:, 4 * c + 2 * h + 1, :], ACT.Sigmoid).then_inc(S["gate_done"], 1)
            for m in range(4):
                act.wait_ge(S["tile_done"], 8 + m + 1)
                act.activation(T.qT[:, m, :], G.banks[:, m, :], ACT.Copy).then_inc(S["evacuated"], 1)
            for m in range(4):
                act.wait_ge(S["tile_done"], 12 + m + 1)
                for odd in range(2):
                    rows = slice(64 * odd, 64 * odd + 64)
                    of = bass.AP(tensor=G.banks[rows, 4 + m, odd:odd + 1].tensor, offset=G.banks[rows, 4 + m, odd:odd + 1].offset,
                                 ap=[G.banks[rows, 4 + m, :].ap[0], [2, L_CMP // 2], [D_STRIDE, N_CMP]])
                    ins = act.activation(T.kcol[rows, m // 2, :, m % 2, 0:N_CMP], of, ACT.Copy)
                ins.then_inc(S["evacuated"], 1)
            for m in range(2):
                act.wait_ge(S["tile_done"], 16 + m + 1)
                act.activation(T.ksw[:, m, :], G.banks[:, m, :], ACT.Copy).then_inc(S["evacuated"], 1)
            for m in range(2):
                act.wait_ge(S["tile_done"], 18 + m + 1)
                act.activation(T.vtok[:, 2 * m:2 * m + 2, :], G.banks[:, 2 + m, :].rearrange("p (j n) -> p j n", j=2),
                               ACT.Copy).then_inc(S["evacuated"], 1)

            def merge(p, i):
                for m in range(4):
                    act.wait_ge(S["tile_done"], 20 + 8 * i + 4 * p + m + 1)
                    act.activation(T.mgT[:, 8 * i + 4 * p + m, :], G.banks[:, 4 * ((STRAIGHT + p) % 2) + m, :], ACT.Sigmoid)\
                       .then_inc(S["evacuated"], 1)

            pairs(act, MERGE, merge)

        @block.vector
        def _(dve):
            dve.memset(T.apad[:, :, 0:TAPS - 1], 0.0).then_inc(S["padded"], 1)
            rms_dve(dve, G, S, rstd, 7, "norm_mix", G.hT)
            for c in range(2):
                for h in range(2):
                    dve.wait_ge(S["gate_done"], 2 * c + h + 1)
                    dve.tensor_tensor(T.apad[:, 2 * c + h, TAPS - 1:], G.banks[:, 4 * c + 2 * h, :], sg[:, h, :], ALU.mult)\
                       .then_inc(S["glu_done"], 1)
            for s, name in enumerate(("pe_k", "pe_v")):
                for g in range(GROUPS):
                    dve.tensor_copy(T.kcol[:, s, :, g, N_CMP], G.col(name, 0, L_CMP // 2)).then_inc(S["padded"], 1)
            dve.wait_ge(S["padded"], 1)
            dve.wait_ge(S["glu_done"], 4)
            done = Link(dve, S["tap_done"])
            for tap in range(TAPS):
                for t in range(CT):
                    of, w = T.apad[:, t, tap:tap + SEQ], G.col("conv_w", t * TAPS + tap)
                    if tap == 0:
                        done.mark(dve.tensor_scalar(T.conv[:, t, :], of, w, G.col("conv_dw_b", t), ALU.mult, ALU.add))
                    else:
                        done.settle(done.n - CT + 1)
                        done.mark(dve.scalar_tensor_tensor(out=T.conv[:, t, :], in0=of, scalar=w, in1=T.conv[:, t, :],
                                                           op0=ALU.mult, op1=ALU.add))

        G.first += STRAIGHT + MERGE


def compress_and_convolution(G, T):
    nc = G.nc
    with ExitStack() as ctx:
        S = stage(G, "cmp", ctx, "gates_sum", "gates_done", "w2_copied", "hidden_sum", "hidden_bias",
                  "hidden_done", "kv_sum", "kv_done", "summed", "mean_done", "centred", "squared", "squares_summed", "var_done",
                  "root_done", "rstd_done", "scaled", "silu_done", "out_done", "mixed")
        w2 = G.sb("cmp_w2", [P, 2, 2, DH], ctx=ctx)
        bias = G.sb("cmp_bias", [P, 2, 4], ctx=ctx)
        hid = G.sb("cmp_hidden", [P, 2, 2, GROUPS, N_CMP], ctx=ctx)
        sq = G.sb("conv_squares", [P, CT, SEQ], ctx=ctx)
        mu = G.sb("conv_mean", [P, SEQ], ctx=ctx)
        rstd = G.sb("conv_rstd", [P, SEQ], ctx=ctx)
        block = ctx.enter_context(nc.Block())
        half = [G.banks[:, 1 + s, 0:4 * 32].rearrange("p (m g c) -> p m g c", m=2, g=GROUPS) for s in range(2)]

        @block.sync
        def _(sp):
            sp.wait_ge(S["w2_copied"], 2)
            G.feed(sp, 1, S["gates_sum"])
            G.first += 1
            G.feed(sp, 2, S["hidden_sum"])
            G.first += 2
            G.feed(sp, 1, S["out_done"], per=KT)
            G.first -= 3

        @block.tensor
        def _(pe):
            for t in range(CT):
                mm = pe.matmul(G.banks[:, 5, :], G.con("ones"), T.conv[:, t, :], start=(t == 0), stop=(t == CT - 1))
            mm.then_inc(S["summed"], 1)
            G.arrived(pe, 0, 0)
            w = G.ring[:, G.slot(0), 0:KT * 24].rearrange("p (k n) -> p k n", k=KT)
            for j in range(JT):
                for k in range(KT):
                    mm = pe.matmul(G.banks[:, 0, j * 24:(j + 1) * 24], G.hT[:, k, j * P:(j + 1) * P], w[:, k, :],
                                   start=(k == 0), stop=(k == KT - 1))
            mm.then_inc(S["gates_sum"], 1)
            for s in range(2):
                G.arrived(pe, (1 + s) % 2, (1 + s) // 2)
                w = G.chunk((1 + s) % 2, 16)
                for m in range(2):
                    for l in range(16):
                        mm = pe.matmul(G.banks[:, 1 + s, m * 64:(m + 1) * 64], w[:, l, m * P:(m + 1) * P],
                                       T.kcol[:, s, l, :, :], start=(l == 0), stop=(l == 15))
                    if m:
                        mm.then_inc(S["hidden_sum"], 1)
            pe.wait_ge(S["centred"], CT)
            for t in range(CT):
                pe.wait_ge(S["squared"], t + 1)
                mm = pe.matmul(G.banks[:, 6, :], G.con("ones"), sq[:, t, :], start=(t == 0), stop=(t == CT - 1))
            mm.then_inc(S["squares_summed"], 1)
            pe.wait_ge(S["hidden_done"], 8)
            pe.wait_ge(S["w2_copied"], 2)
            for g in range(GROUPS):
                for m in range(2):
                    pe.matmul(G.banks[g * DH:(g + 1) * DH, 3, 0:N_CMP], w2[:, 0, m, :], hid[:, 0, m, g, :],
                              start=(m == 0), stop=(m == 1))
                for m in range(2):
                    mm = pe.matmul(G.banks[0:N_CMP, 4, g * DH:(g + 1) * DH], hid[:, 1, m, g, :], w2[:, 1, m, :],
                                   start=(m == 0), stop=(m == 1))
            mm.then_inc(S["kv_sum"], 1)
            G.arrived(pe, 1, 1)
            pe.wait_ge(S["silu_done"], CT)
            pe.wait_ge(S["kv_done"], 2)
            for m in range(KT):
                project(pe, G, 1, m, m, sq, k_tiles=CT).then_inc(S["out_done"], 1)

        @block.scalar
        def _(act):
            act.wait_ge(G.landed[G.slot(0)], 16 * (G.first // SLOTS + 1))
            for s in range(2):
                at = KT * 24 + s * 2 * DH
                act.activation(w2[:, s, :, :], G.ring[:, G.slot(0), at:at + 2 * DH].rearrange("p (m n) -> p m n", m=2), ACT.Copy)\
                   .then_inc(S["w2_copied"], 1)
            act.wait_ge(S["gates_sum"], 1)
            act.activation(T.gates[:, :, :], G.banks[:, 0, 0:JT * 24].rearrange("p (j n) -> p j n", j=JT), ACT.Sigmoid)\
               .then_inc(S["gates_done"], 1)
            act.wait_ge(S["centred"], CT)
            for t in range(CT):
                act.activation(sq[:, t, :], T.conv[:, t, :], ACT.Square).then_inc(S["squared"], 1)
            for s in range(2):
                act.wait_ge(S["hidden_sum"], s + 1)
                act.activation(bias[:, s, :].rearrange("p (m g) -> p m g", m=2), half[s][:, :, :, N_CMP], ACT.Copy)\
                   .then_inc(S["hidden_bias"], 1)
                act.wait_ge(S["hidden_bias"], s + 1)
                for m in range(2):
                    for g in range(GROUPS):
                        act.activation(hid[:, s, m, g, :], half[s][:, m, g, 0:N_CMP], ACT.Gelu_apprx_tanh,
                                       bias=bias[:, s, 2 * m + g:2 * m + g + 1]).then_inc(S["hidden_done"], 1)
            act.wait_ge(S["var_done"], 1)
            act.activation(rstd[:, :], rstd[:, :], ACT.Sqrt).then_inc(S["root_done"], 1)
            act.wait_ge(S["kv_sum"], 1)
            act.activation(T.kcT[:, :], G.banks[:, 3, 0:N_CMP], ACT.Copy).then_inc(S["kv_done"], 1)
            act.activation(T.vc[0:N_CMP, :], G.banks[0:N_CMP, 4, 0:GROUPS * DH], ACT.Copy).then_inc(S["kv_done"], 1)
            for t in range(CT):
                act.wait_ge(S["scaled"], t + 1)
                act.activation(sq[:, t, :], T.conv[:, t, :], ACT.Silu, bias=G.col("conv_ln_b", t), scale=G.col("conv_ln_g", t))\
                   .then_inc(S["silu_done"], 1)

        @block.vector
        def _(dve):
            dve.wait_ge(S["summed"], 1)
            dve.tensor_scalar(mu[:, :], G.banks[:, 5, :], 1.0 / (CT * P), None, ALU.mult).then_inc(S["mean_done"], 1)
            dve.wait_ge(S["mean_done"], 1)
            for t in range(CT):
                dve.tensor_tensor(T.conv[:, t, :], T.conv[:, t, :], mu[:, :], ALU.subtract).then_inc(S["centred"], 1)
            dve.wait_ge(S["gates_done"], 1)
            seen = T.gates[:, 0, :].rearrange("p (h b) -> p h b", b=3)[:, :, 0]
            dve.tensor_scalar(seen, seen, G.con("seen_cmp"), None, ALU.mult).then_inc(S["gates_done"], 1)
            dve.wait_ge(S["squares_summed"], 1)
            dve.tensor_scalar(rstd[:, :], G.banks[:, 6, :], 1.0 / (CT * P), EPS, ALU.mult, ALU.add).then_inc(S["var_done"], 1)
            dve.wait_ge(S["root_done"], 1)
            dve.reciprocal(rstd[:, :], rstd[:, :]).then_inc(S["rstd_done"], 1)
            dve.wait_ge(S["rstd_done"], 1)
            for t in range(CT):
                dve.tensor_tensor(T.conv[:, t, :], T.conv[:, t, :], rstd[:, :], ALU.mult).then_inc(S["scaled"], 1)
            for m in range(KT):
                dve.wait_ge(S["out_done"], m + 1)
                dve.tensor_tensor(G.hT[:, m, :], G.banks[:, m, :], T.mgT[:, m, :], ALU.mult).then_inc(S["mixed"], 1)

        G.first += 4


def attention(G, T):
    nc = G.nc
    CMP, SLC, WIN = range(3)
    units = [(j, b, g) for j in range(JT) for b in (SLC, WIN, CMP) for g in range(GROUPS)]
    U = len(units)
    width = lambda u: N_CMP if units[u][1] == CMP else P * (units[u][0] + 1)
    with ExitStack() as ctx:
        S = stage(G, "attn", ctx, "staged", "scored", "biased", "max_done", "negated", "expd", "turned", "copied", "weighed",
                  "inverted", "coefficient", "combined")
        qs = G.sb("attn_q", [P, SEQ], ctx=ctx)
        sc = G.sb("attn_scores", [P, 2, SEQ], ctx=ctx)
        pT = G.sb("attn_probs_T", [P, 2, SEQ], ctx=ctx)
        stat = G.sb("attn_stats", [P, 4, U], ctx=ctx)
        top, bottom, total, coef = (stat[:, n, :] for n in range(4))
        block = ctx.enter_context(nc.Block())
        SCORE, TURN, OUT = 0, 2, 4

        @block.tensor
        def _(pe):
            def scores(u, i):
                j, b, g = units[u]
                rows = slice(g * DH, (g + 1) * DH)
                if u == 0:
                    pe.wait_ge(S["staged"], i + 1)
                if u >= 2:
                    pe.wait_ge(S["biased"], U * i + u - 1)
                keys = T.kcT[rows, :] if b == CMP else T.ksw[rows, b - 1, 0:width(u)]
                pe.matmul(G.banks[:, SCORE + u % 2, 0:width(u)], qs[rows, j * P:(j + 1) * P], keys, start=True, stop=True)\
                  .then_inc(S["scored"], 1)

            def turn(u, i):
                pe.wait_ge(S["expd"], U * i + u + 1)
                if u >= 2:
                    pe.wait_ge(S["copied"], U * i + u - 1)
                n = width(u)
                for at in range(0, n, P):
                    w = min(P, n - at)
                    mm = pe.transpose(G.banks[0:w, TURN + u % 2, at:at + P], sc[:, u % 2, at:at + w], G.con("ident"))
                mm.then_inc(S["turned"], 1)

            def values(u, i):
                j, b, g = units[u]
                pe.wait_ge(S["copied"], U * i + u + 1)
                if u >= 2:
                    pe.wait_ge(S["combined"], U * i + u)
                out = G.banks[:, OUT + u % 2, 0:DH]
                cols = slice(g * DH, (g + 1) * DH)
                if b == CMP:
                    pe.matmul(out, pT[0:N_CMP, u % 2, 0:P], T.vc[0:N_CMP, cols], start=True, stop=True).then_inc(S["weighed"], 1)
                else:
                    for s in range(j + 1):
                        at = (b - 1) * P + g * DH
                        mm = pe.matmul(out, pT[:, u % 2, s * P:(s + 1) * P], T.vtok[:, s, at:at + DH],
                                       start=(s == 0), stop=(s == j))
                    mm.then_inc(S["weighed"], 1)

            with pe.Fori(0, PER_GROUP) as i:
                for u in range(U + 2):
                    if u < U:
                        scores(u, i)
                    if 1 <= u <= U:
                        turn(u - 1, i)
                    if u >= 2:
                        values(u - 2, i)

        @block.scalar
        def _(act):
            def exps(u, i):
                act.wait_ge(S["negated"], U * i + u + 1)
                s = sc[:, u % 2, 0:width(u)]
                act.activation(s, s, ACT.Exp, bias=bottom[:, u:u + 1], accum_out=total[:, u:u + 1]).then_inc(S["expd"], 1)

            def copy(u, i):
                act.wait_ge(S["turned"], U * i + u + 1)
                if u >= 2:
                    act.wait_ge(S["weighed"], U * i + u - 1)
                j, b, g = units[u]
                rows, n = (N_CMP, P) if b == CMP else (P, width(u))
                act.activation(pT[0:rows, u % 2, 0:n], G.banks[0:rows, TURN + u % 2, 0:n], ACT.Copy).then_inc(S["copied"], 1)

            with act.Fori(0, PER_GROUP) as i:
                act.wait_ge(S["combined"], U * i + 1)
                act.activation(qs[:, :], T.qT[:, i, :], ACT.Copy).then_inc(S["staged"], 1)
                for u in range(U + 1):
                    if u < U:
                        exps(u, i)
                    if u >= 1:
                        copy(u - 1, i)

        @block.vector
        def _(dve):
            dve.sem_inc(S["combined"], 1)

            def bias(u, i):
                j, b, g = units[u]
                dve.wait_ge(S["scored"], U * i + u + 1)
                if u >= 2:
                    dve.wait_ge(S["turned"], U * i + u - 1)
                if b == CMP:
                    y = 3 * P + L_CMP - 1 - j * P
                    w = T.W[:, g * PER_GROUP + i, y:y + D_STRIDE * (N_CMP - 1) + 1:D_STRIDE]
                else:
                    w = T.W[:, g * PER_GROUP + i, (JT - 1 - j) * P:SEQ]
                s = sc[:, u % 2, 0:width(u)]
                dve.scalar_tensor_tensor(out=s, in0=G.banks[:, SCORE + u % 2, 0:width(u)], scalar=DH ** -0.5, in1=w,
                                         op0=ALU.mult, op1=ALU.add).then_inc(S["biased"], 1)
                dve.wait_ge(S["biased"], U * i + u + 1)
                dve.tensor_reduce(top[:, u:u + 1], s, AX, ALU.max).then_inc(S["max_done"], 1)
                dve.wait_ge(S["max_done"], U * i + u + 1)
                dve.tensor_scalar(bottom[:, u:u + 1], top[:, u:u + 1], -1.0, None, ALU.mult).then_inc(S["negated"], 1)

            def combine(u, i):
                j, b, g = units[u]
                head = g * PER_GROUP + i
                dve.wait_ge(S["weighed"], U * i + u + 1)
                dve.reciprocal(coef[:, u:u + 1], total[:, u:u + 1]).then_inc(S["inverted"], 1)
                dve.wait_ge(S["inverted"], U * i + u + 1)
                dve.tensor_scalar(coef[:, u:u + 1], coef[:, u:u + 1], T.gates[:, j, bass.ds(3 * head + b, 1)], None, ALU.mult)\
                   .then_inc(S["coefficient"], 1)
                dve.wait_ge(S["coefficient"], U * i + u + 1)
                o = T.o[:, j, bass.ds(head * DH, DH)]
                out = G.banks[:, OUT + u % 2, 0:DH]
                if b == SLC:
                    ins = dve.tensor_scalar(o, out, coef[:, u:u + 1], None, ALU.mult)
                else:
                    dve.wait_ge(S["combined"], U * i + u)
                    ins = dve.scalar_tensor_tensor(out=o, in0=out, scalar=coef[:, u:u + 1], in1=o, op0=ALU.mult, op1=ALU.add)
                ins.then_inc(S["combined"], 1)

            with dve.Fori(0, PER_GROUP) as i:
                for u in range(U + 2):
                    if u < U:
                        bias(u, i)
                    if u >= 2:
                        combine(u - 2, i)


def merge_branches(G, T):
    nc = G.nc
    with ExitStack() as ctx:
        S = stage(G, "mix", ctx, "turned", "copied", "attn_done", "gated", "mixed", "out_done", "added")
        oT = G.sb("mix_oT", [P, CT, SEQ], ctx=ctx)
        yg = G.sb("mix_gated", [P, 2, SEQ], ctx=ctx)
        block = ctx.enter_context(nc.Block())

        @block.sync
        def _(sp):
            G.feed(sp, 1, S["attn_done"], per=KT)
            G.first += 1
            G.feed(sp, 2, S["out_done"], per=4)
            G.first -= 1

        @block.tensor
        def _(pe):
            for t in range(CT):
                for j in range(JT):
                    mm = pe.transpose(G.banks[:, t, j * P:(j + 1) * P], T.o[:, j, t * P:(t + 1) * P], G.con("ident"))
                mm.then_inc(S["turned"], 1)
            G.arrived(pe, 0, 0)
            pe.wait_ge(S["copied"], CT)
            for m in range(KT):
                project(pe, G, 0, m, m, oT, k_tiles=CT).then_inc(S["attn_done"], 1)
            pe.wait_ge(S["mixed"], KT)
            for m in range(KT):
                if m % 4 == 0:
                    G.arrived(pe, 1 + m // 4, 0) if m == 0 else G.arrived(pe, 0, 1)
                project(pe, G, 1 if m < 4 else 0, m % 4, m, G.hT).then_inc(S["out_done"], 1)

        @block.scalar
        def _(act):
            for t in range(CT):
                act.wait_ge(S["turned"], t + 1)
                act.activation(oT[:, t, :], G.banks[:, t, :], ACT.Copy).then_inc(S["copied"], 1)

        @block.vector
        def _(dve):
            for m in range(KT):
                dve.wait_ge(S["attn_done"], m + 1)
                if m >= 2:
                    dve.wait_ge(S["mixed"], m - 1)
                dve.tensor_tensor(yg[:, m % 2, :], G.banks[:, m, :], T.mgT[:, KT + m, :], ALU.mult).then_inc(S["gated"], 1)
                dve.wait_ge(S["gated"], m + 1)
                dve.tensor_tensor(G.hT[:, m, :], G.hT[:, m, :], yg[:, m % 2, :], ALU.add).then_inc(S["mixed"], 1)
            for m in range(KT):
                dve.wait_ge(S["out_done"], m + 1)
                dve.tensor_tensor(G.x[:, m, :], G.x[:, m, :], G.banks[:, m, :], ALU.add).then_inc(S["added"], 1)

        G.first += 3


def layer_embedding(G):
    nc = G.nc
    with ExitStack() as ctx:
        S = stage(G, "ple", ctx, *RMS, "p_loaded", "gate_sum", "gate_done", "embedded", "gated", "added")
        pT = G.sb("ple_pT", [P, 2, SEQ], ctx=ctx)
        sg = G.sb("ple_gate", [P, KT, SEQ], ctx=ctx)
        rstd = G.sb("ple_rstd", [P, SEQ], ctx=ctx)
        block = ctx.enter_context(nc.Block())

        @block.sync
        def _(sp):
            sp.dma_start(pT[:, :, :], G.aps["pT"].rearrange("(k p) n -> p k n", p=P)).then_inc(S["p_loaded"], 16)
            G.feed(sp, 2, S["gate_sum"], per=4)
            G.first += 2
            G.feed(sp, 1, S["embedded"], per=KT)
            G.first -= 2

        @block.tensor
        def _(pe):
            rms_pe(pe, G, S, sg, 7)
            for m in range(KT):
                if m % 4 == 0:
                    G.arrived(pe, m // 4, 0)
                if m == 7:
                    pe.wait_ge(S["h_ready"], KT)
                project(pe, G, m // 4, m % 4, m, G.hT, first_wait=S["h_ready"] if m == 0 else None).then_inc(S["gate_sum"], 1)
            pe.wait_ge(S["p_loaded"], 16)
            G.arrived(pe, 0, 1)
            for m in range(KT):
                pe.wait_ge(S["gate_done"], m + 1)
                project(pe, G, 0, m, m, pT, k_tiles=2).then_inc(S["embedded"], 1)

        @block.scalar
        def _(act):
            rms_act(act, G, S, sg)
            rms_root(act, G, S, rstd)
            for m in range(KT):
                act.wait_ge(S["gate_sum"], m + 1)
                act.activation(sg[:, m, :], G.banks[:, m, :], ACT.Sigmoid).then_inc(S["gate_done"], 1)

        @block.vector
        def _(dve):
            rms_dve(dve, G, S, rstd, 7, "norm_ple", G.hT)
            for m in range(KT):
                dve.wait_ge(S["embedded"], m + 1)
                dve.tensor_tensor(sg[:, m, :], sg[:, m, :], G.banks[:, m, :], ALU.mult).then_inc(S["gated"], 1)
                dve.wait_ge(S["gated"], m + 1)
                dve.tensor_tensor(G.x[:, m, :], G.x[:, m, :], sg[:, m, :], ALU.add).then_inc(S["added"], 1)

        G.first += 3


def norm_in_place(G, name, gain):
    nc = G.nc
    with ExitStack() as ctx:
        S = stage(G, name, ctx, *RMS)
        sq = G.sb(name + "_squares", [P, KT, SEQ], ctx=ctx)
        rstd = G.sb(name + "_rstd", [P, SEQ], ctx=ctx)
        block = ctx.enter_context(nc.Block())

        @block.tensor
        def _(pe):
            rms_pe(pe, G, S, sq, 7)

        @block.scalar
        def _(act):
            rms_act(act, G, S, sq)
            rms_root(act, G, S, rstd)

        @block.vector
        def _(dve):
            rms_dve(dve, G, S, rstd, 7, gain, G.x)


def first_block(G):
    with ExitStack() as ctx:
        T = Shared()
        T.W = G.sb("bias_tiles", [P, HEADS, BIAS_W], ctx=ctx)
        T.qT = G.sb("qT", [P, PER_GROUP, SEQ], ctx=ctx)
        T.kcol = G.sb("compress_columns", [P, 2, L_CMP // 2, GROUPS, N_CMP + 1], ctx=ctx)
        T.ksw = G.sb("keys_T", [P, 2, SEQ], ctx=ctx)
        T.vtok = G.sb("values", [P, JT, 256], ctx=ctx)
        T.mgT = G.sb("merge_gates", [P, 2 * KT, SEQ], ctx=ctx)
        T.gates = G.sb("branch_gates", [P, JT, 3 * HEADS], ctx=ctx)
        T.kcT = G.sb("compressed_keys_T", [P, N_CMP], ctx=ctx)
        T.vc = G.sb("compressed_values", [P, GROUPS * DH], ctx=ctx)
        bias_tiles(G, T.W)
        with ExitStack() as conv:
            T.apad = G.sb("glu_padded", [P, CT, SEQ + TAPS - 1], ctx=conv)
            T.conv = G.sb("convolved", [P, CT, SEQ], ctx=conv)
            in_projection(G, T)
            compress_and_convolution(G, T)
        T.o = G.sb("attn_out", [P, JT, SEQ], ctx=ctx)
        attention(G, T)
        merge_branches(G, T)
    feed_forward(G, "ffn1", "norm_ffn", "ffn_taps", ACT.Gelu_apprx_tanh, 0)
    layer_embedding(G)
    norm_in_place(G, "final1", "norm_final")



FILTER = 64
EMB = 33
TWO_PI = 6.283185307179586
TURN_HI = 6.28125
TURN_LO = TWO_PI - TURN_HI
ROUND = 1.5 * 2.0 ** 23


def dft_tables():
    n, f = np.arange(SEQ), np.arange(SEQ)
    ang = 2 * np.pi * ((n[:, None] * f[None]) % (2 * SEQ)) / (2 * SEQ)
    last = np.where(n % 2 == 0, 1.0, -1.0)
    re, im = np.cos(ang), -np.sin(ang)
    im[:, 0] = last
    share = np.where(f == 0, 1.0, 2.0)[:, None] / (2 * SEQ)
    inv_re, inv_im = share * np.cos(ang).T, -share * np.sin(ang).T
    inv_im[0] = last / (2 * SEQ)
    return np.concatenate([re, im], 1).astype(np.float32), np.concatenate([inv_re, inv_im], 1).astype(np.float32)


def filter_tables():
    f = np.float32
    n = np.arange(SEQ, dtype=f)
    t = n / f(SEQ - 1)
    fr = np.linspace(1e-4, 15, 16, dtype=f)
    ang = f(2.0 * np.pi / SEQ) * n[:, None] * fr[None]
    z = np.concatenate([t[:, None], np.cos(ang), -np.sin(ang)], 1)
    deltas = np.abs(np.linspace(np.log(1e-2) / 1.5, np.log(1e-2) / 0.3, D, dtype=f))
    return np.ascontiguousarray(z.T), np.exp(-t[:, None] * deltas[None]).astype(f)


def second_extra():
    return {"decay": filter_tables()[1], "scan_masks": scan_masks()}


def lay_second(L, a):
    tile = lambda at, t: at + t * P + np.arange(P)
    wide = lambda v: np.concatenate([v, np.zeros((P - v.shape[0], v.shape[1]), np.float32)]) if v.shape[0] < P else v
    L.chunk(*(wide(v) for v in (filter_tables()[0], a["hy_f_w1"][0], a["hy_f_w2"][0], a["hy_f_w3"][0], a["hy_f_w4"][0])))
    order = np.concatenate([tile(at, t) for t in range(KT) for at in (D, 2 * D)])
    L.column_chunks(a["hy_w_in"][0], order)
    L.column_chunks(a["hy_w_in"][0][:, :D])
    for table in dft_tables():
        L.chunk(L.matrix(table))
    L.column_chunks(a["hy_w_out"][0])
    L.vector("hy_norm", a["norm_mix_g"][0])
    five = np.concatenate([a["hy_conv_w"][0], a["hy_conv_b"], a["hy_b_in"]]).reshape(5, 3 * KT, P)
    seq = [s * KT + t for t in range(KT) for s in (1, 2)] + list(range(KT))
    L.column("hy_conv", five[:, seq].transpose(2, 1, 0).reshape(P, 15 * KT))
    L.column("hy_filter", np.stack([a["hy_f_b1"][0], a["hy_f_b2"][0], a["hy_f_b3"][0], a["hy_f_freq"][0]], 1))
    L.vector("hy_skip", a["hy_skip"][0])
    L.vector("hy_b_out", a["hy_b_out"][0])
    lay_ff2(L, a, 0)
    lay_rwkv(L, a)
    lay_ff2(L, a, 1)
    L.vector("final_norm_2", a["final_norm_g"])


def lay_ff2(L, a, i):
    L.column_chunks(a["ff_w_up"][i], L.up_order())
    L.row_chunks(a["ff_w_down"][i])
    L.vector(f"ff_norm_{i}", a["norm_ffn_g"][i])
    L.ff_taps(f"ff_taps_{i}", a["ff_conv_w"][i], a["ff_conv_b"][i])


def hyena_filters(G, T):
    nc = G.nc
    with ExitStack() as ctx:
        S = stage(G, "filt", ctx, "decay_loaded", "layer_sum", "step", "sine_in", "sine_done", "filter_sum", "scaled", "added")
        decay = G.sb("filt_decay", [P, JT, D], ctx=ctx)
        arg = G.sb("filt_arg", [FILTER, 3, SEQ], ctx=ctx)
        scaled = G.sb("filt_scaled", [P, 2, 2, SEQ], ctx=ctx)
        block = ctx.enter_context(nc.Block())
        w = G.ring[:, G.slot(0), :]
        zT, w123, w4 = w[0:EMB, 0:SEQ], SEQ, SEQ + 3 * FILTER
        ROUNDS = [(j, half) for j in range(JT) for half in range(2)]

        @block.sync
        def _(sp):
            sp.dma_start(decay[:, :, :], G.aps["decay"].rearrange("(j p) n -> p j n", p=P)).then_inc(S["decay_loaded"], 16)
            G.feed(sp, 1, S["filter_sum"], per=2 * len(ROUNDS))

        @block.tensor
        def _(pe):
            G.arrived(pe, 0, 0)
            for n in range(3):
                if n:
                    pe.wait_ge(S["sine_done"], n)
                rows = EMB if n == 0 else FILTER
                pe.matmul(G.banks[0:FILTER, n, :], w[0:rows, w123 + n * FILTER:w123 + (n + 1) * FILTER],
                          zT if n == 0 else arg[:, 2, :], start=True, stop=True).then_inc(S["layer_sum"], 1)
            pe.wait_ge(S["sine_done"], 3)
            for n, (j, half) in enumerate(ROUNDS):
                if n >= 4:
                    pe.wait_ge(S["scaled"], 2 * (n - 3))
                for s in range(2):
                    at = w4 + s * D + half * 512
                    pe.matmul(G.banks[:, 2 * (n % 4) + s, :], arg[:, 2, j * P:(j + 1) * P], w[0:FILTER, at:at + 512],
                              start=True, stop=True).then_inc(S["filter_sum"], 1)

        @block.scalar
        def _(act):
            for n in range(3):
                act.wait_ge(S["sine_in"], n + 1)
                act.activation(arg[:, 2, :], arg[:, 0, :], ACT.Sin).then_inc(S["sine_done"], 1)

        @block.vector
        def _(dve):
            step = Link(dve, S["step"])
            freq = G.col("hy_filter", 3)[0:FILTER, :]
            a, turns = arg[:, 0, :], arg[:, 1, :]
            for n in range(3):
                dve.wait_ge(S["layer_sum"], n + 1)
                step(dve.tensor_scalar(a, G.banks[0:FILTER, n, :], G.col("hy_filter", n)[0:FILTER, :], freq, ALU.add, ALU.mult))
                step(dve.tensor_scalar(turns, a, 1.0 / TWO_PI, ROUND, ALU.mult, ALU.add))
                step(dve.tensor_scalar(turns, turns, -ROUND, None, ALU.add))
                step(dve.scalar_tensor_tensor(out=a, in0=turns, scalar=-TURN_HI, in1=a, op0=ALU.mult, op1=ALU.add))
                step(dve.scalar_tensor_tensor(out=a, in0=turns, scalar=-TURN_LO, in1=a, op0=ALU.mult, op1=ALU.add))
                dve.tensor_scalar(a, a, 3.1415925, -3.1415925, ALU.min, ALU.max).then_inc(S["sine_in"], 1)
            dve.wait_ge(S["decay_loaded"], 16)
            for n, (j, half) in enumerate(ROUNDS):
                cols = slice(half * 512, half * 512 + 512)
                if n >= 2:
                    dve.wait_ge(S["added"], 2 * n - 2)
                for s in range(2):
                    dve.wait_ge(S["filter_sum"], 2 * n + s + 1)
                    dve.tensor_tensor(scaled[:, n % 2, s, :], G.banks[:, 2 * (n % 4) + s, :], decay[:, j, cols], ALU.mult)\
                       .then_inc(S["scaled"], 1)
                dve.wait_ge(S["scaled"], 2 * n + 2)
                dve.tensor_tensor(T.ksum[:, j, cols], scaled[:, n % 2, 0, :], scaled[:, n % 2, 1, :], ALU.add).then_inc(S["added"], 1)
                dve.tensor_tensor(T.kdiff[:, j, cols], scaled[:, n % 2, 0, :], scaled[:, n % 2, 1, :], ALU.subtract)\
                   .then_inc(S["added"], 1)

        G.first += 1


def hyena_projection(G, T):
    nc = G.nc
    U_CHUNKS, X_CHUNKS = 4, 2
    with ExitStack() as ctx:
        S = stage(G, "hyin", ctx, *RMS, "edges", "tile_sum", "biased", "centre", "left", "right", "product", "h_high", "h_split", "rounded", "split")
        sq = T.uT
        z = G.sb("hyin_z", [P, 4, SEQ + 2], ctx=ctx)
        rstd, c = T.x0T[:, 0, :], T.x0T[:, 4:8, :]
        w_parts = [G.sb("hyin_weights_" + part, [P, 2, CHUNK // 2], F32R, ctx=ctx) for part in ("high", "low")]
        h_parts = [G.sb("hyin_normed_" + part, [P, KT, SEQ], F32R, ctx=ctx) for part in ("high", "low")]
        halves = 2 * (U_CHUNKS + X_CHUNKS)
        block = ctx.enter_context(nc.Block())

        @block.sync
        def _(sp):
            G.feed(sp, U_CHUNKS + X_CHUNKS, S["split"], per=2)

        def landed_half(n):
            columns = slice(n % 2 * 256, n % 2 * 256 + 256)
            return G.chunk(n // 2, KT)[:, :, columns], [w[:, n % 2, :].rearrange("p (k n) -> p k n", k=KT) for w in w_parts]

        @block.gpsimd
        def _(pool):
            for n in range(halves):
                landed, parts = landed_half(n)
                pool.wait_ge(S["rounded"], n + 1)
                pool.tensor_tensor(parts[1], landed, parts[0].bitcast(F32), ALU.subtract).then_inc(S["split"], 1)

        @block.tensor
        def _(pe):
            rms_pe(pe, G, S, sq, 7)

            def chunk(p, i):
                for m in range(4):
                    pe.wait_ge(S["biased"], 8 * i + 4 * p + m + 1)
                    pe.wait_ge(S["split"], 4 * i + 2 * p + m // 2 + 1)
                    w = landed_half(m // 2)[1]
                    for k in range(KT):
                        if p == m == 0:
                            pe.wait_ge(S["h_split"], k + 1)
                        mm = exact_product(pe, G.banks[:, 4 * p + m, :], [x[:, k, m % 2 * P:(m % 2 + 1) * P] for x in w],
                                           [x[:, k, :] for x in h_parts], start=(k == 0), stop=(k == KT - 1))
                    mm.then_inc(S["tile_sum"], 1)

            pairs(pe, U_CHUNKS + X_CHUNKS, chunk)

        @block.scalar
        def _(act):
            act.sem_inc(S["biased"], 8)
            def high(n):
                G.arrived(act, n // 2 % 2, n // 4)
                landed, parts = landed_half(n)
                act.activation(parts[0], landed, ACT.Copy).then_inc(S["rounded"], 1)

            rms_act(act, G, S, sq)
            for n in range(2):
                high(n)
            rms_root(act, G, S, rstd)
            for k in range(KT):
                act.wait_ge(S["h_ready"], k + 1)
                act.activation(h_parts[0][:, k, :], G.hT[:, k, :], ACT.Copy).then_inc(S["h_high"], 1)
            act.wait_ge(S["edges"], 1)

            for n in range(2 * halves):
                act.wait_ge(S["tile_sum"], n + 1)
                if n % 2 and n // 2 + 2 < halves:
                    high(n // 2 + 2)
                act.wait_ge(S["right"], n + 5)
                act.activation(z[:, n % 4, 1:SEQ + 1], G.banks[:, n % 8, :], ACT.Identity, bias=G.col("hy_conv", 5 * n + 4))\
                   .then_inc(S["biased"], 1)

        @block.vector
        def _(dve):
            dve.memset(z[:, :, 0:SEQ + 2:SEQ + 1], 0.0).then_inc(S["edges"], 1)
            dve.sem_inc(S["right"], 8)
            rms_dve(dve, G, S, rstd, 7, "hy_norm", G.hT)
            for k in range(KT):
                dve.wait_ge(S["h_high"], k + 1)
                dve.tensor_tensor(h_parts[1][:, k, :], G.hT[:, k, :], h_parts[0][:, k, :].bitcast(F32), ALU.subtract).then_inc(S["h_split"], 1)

            def convolve(p, i, m, n, to):
                b = z[:, m, :]
                dve.wait_ge(S["biased"], 8 + n + 1)
                dve.tensor_scalar(to, b[:, 1:SEQ + 1], G.col("hy_conv", 5 * n + 1), G.col("hy_conv", 5 * n + 3),
                                  ALU.mult, ALU.add).then_inc(S["centre"], 1)
                dve.wait_ge(S["centre"], n + 1)
                dve.scalar_tensor_tensor(out=to, in0=b[:, 0:SEQ], scalar=G.col("hy_conv", 5 * n), in1=to,
                                         op0=ALU.mult, op1=ALU.add).then_inc(S["left"], 1)
                dve.wait_ge(S["left"], n + 1)
                dve.scalar_tensor_tensor(out=to, in0=b[:, 2:SEQ + 2], scalar=G.col("hy_conv", 5 * n + 2), in1=to,
                                         op0=ALU.mult, op1=ALU.add).then_inc(S["right"], 1)

            def u_chunk(p, i):
                for m in range(4):
                    n = 8 * i + 4 * p + m
                    convolve(p, i, m, n, c[:, m, :])
                    if m % 2:
                        dve.wait_ge(S["right"], 8 + n + 1)
                        dve.tensor_tensor(T.uT[:, 4 * i + 2 * p + m // 2, :], c[:, m - 1, :], c[:, m, :], ALU.mult)\
                           .then_inc(S["product"], 1)
                        dve.wait_ge(S["product"], 4 * i + 2 * p + m // 2 + 1)

            pairs(dve, U_CHUNKS, u_chunk)
            for m in range(4 * X_CHUNKS):
                n = 4 * U_CHUNKS + m
                convolve(m // 4, U_CHUNKS // 2, m % 4, n, T.x0T[:, m, :])

        G.first += U_CHUNKS + X_CHUNKS


def hyena_convolution(G, T):
    nc = G.nc
    with ExitStack() as ctx:
        S = stage(G, "long", ctx, "turned", "copied", "last_sum", "last_done", "spectra", "u_copied", "step", "bank_free",
                  "back", "skipped", "gated", "out_done", "added")
        ut = G.sb("long_u", [P, JT, D], ctx=ctx)
        yr = G.sb("long_re", [P, 4, D], ctx=ctx)
        yi = G.sb("long_im", [P, 4, D], ctx=ctx)
        us = G.sb("long_us", [P, 2, 2, SEQ], ctx=ctx)
        tmp = G.sb("long_tmp", [P, 4, SEQ], ctx=ctx)
        last = G.sb("long_last", [1, D], ctx=ctx)
        block = ctx.enter_context(nc.Block())
        ROUNDS = [(f, half) for f in range(4) for half in range(2)]

        @block.sync
        def _(sp):
            G.feed(sp, 1, S["spectra"], per=len(ROUNDS))
            G.first += 1
            G.feed(sp, 1, S["back"], per=KT)
            G.first += 1
            G.feed(sp, 2, S["out_done"], per=4)
            G.first -= 2

        @block.tensor
        def _(pe):
            for t in range(KT):
                for j in range(JT):
                    mm = pe.transpose(G.banks[:, t, j * P:(j + 1) * P], T.uT[:, t, j * P:(j + 1) * P], G.con("ident"))
                mm.then_inc(S["turned"], 1)
            G.arrived(pe, 0, 0)
            w = G.chunk(0, 4)
            pe.wait_ge(S["copied"], KT)
            for half in range(2):
                for s in range(4):
                    mm = pe.matmul(G.banks[0:1, half, :], w[:, s, SEQ:SEQ + 1], T.ksum[:, s, half * 512:half * 512 + 512],
                                   start=(s == 0), stop=(s == 3))
                mm.then_inc(S["last_sum"], 1)
            pe.wait_ge(S["last_done"], 2)
            for n, (f, half) in enumerate(ROUNDS):
                if n >= 2:
                    pe.wait_ge(S["bank_free"], n - 1)
                cols = slice(half * 512, half * 512 + 512)
                for b, (at, of) in enumerate(((0, ut), (SEQ, ut), (0, T.ksum), (SEQ, T.kdiff))):
                    for s in range(4):
                        mm = pe.matmul(G.banks[:, 4 * (n % 2) + b, :], w[:, s, at + f * P:at + (f + 1) * P], of[:, s, cols],
                                       start=(s == 0), stop=(s == 3))
                mm.then_inc(S["spectra"], 1)
            G.arrived(pe, 1, 0)
            w = G.chunk(1, 4)
            pe.wait_ge(S["bank_free"], len(ROUNDS))
            for m in range(KT):
                for n in range(8):
                    of = yr if n < 4 else yi
                    mm = pe.matmul(G.banks[:, m, :], of[:, n % 4, m * P:(m + 1) * P], w[:, n % 4, (n // 4) * 512:(n // 4) * 512 + 512],
                                   start=(n == 0), stop=(n == 7))
                mm.then_inc(S["back"], 1)
            pe.wait_ge(S["gated"], KT)
            for m in range(KT):
                if m % 4 == 0:
                    G.arrived(pe, m // 4, 1)
                project(pe, G, m // 4, m % 4, m, G.hT).then_inc(S["out_done"], 1)

        @block.scalar
        def _(act):
            for t in range(KT):
                act.wait_ge(S["turned"], t + 1)
                act.activation(ut[:, :, t * P:(t + 1) * P], G.banks[:, t, :].rearrange("p (j n) -> p j n", j=JT), ACT.Copy)\
                   .then_inc(S["copied"], 1)
            for half in range(2):
                act.wait_ge(S["last_sum"], half + 1)
                act.activation(last[:, half * 512:half * 512 + 512], G.banks[0:1, half, :], ACT.Copy).then_inc(S["last_done"], 1)
            for n in range(len(ROUNDS)):
                act.wait_ge(S["spectra"], n + 1)
                if n >= 2:
                    act.wait_ge(S["bank_free"], n - 1)
                for s in range(2):
                    act.activation(us[:, n % 2, s, :], G.banks[:, 4 * (n % 2) + s, :], ACT.Copy).then_inc(S["u_copied"], 1)

        @block.vector
        def _(dve):
            step = Link(dve, S["step"])
            for n, (f, half) in enumerate(ROUNDS):
                cols = slice(half * 512, half * 512 + 512)
                dve.wait_ge(S["u_copied"], 2 * n + 2)
                kr, ki = G.banks[:, 4 * (n % 2) + 2, :], G.banks[:, 4 * (n % 2) + 3, :]
                ur, ui = us[:, n % 2, 0, :], us[:, n % 2, 1, :]
                step.mark(dve.tensor_tensor(tmp[:, 0, :], ur, kr, ALU.mult))
                step.mark(dve.tensor_tensor(tmp[:, 1, :], ui, ki, ALU.mult))
                step.mark(dve.tensor_tensor(tmp[:, 2, :], ur, ki, ALU.mult))
                step(dve.tensor_tensor(tmp[:, 3, :], ui, kr, ALU.mult))
                step.mark(dve.tensor_tensor(yr[:, f, cols], tmp[:, 0, :], tmp[:, 1, :], ALU.subtract))
                step(dve.tensor_tensor(yi[:, f, cols], tmp[:, 2, :], tmp[:, 3, :], ALU.add))
                if f == 0:
                    dve.wait_ge(S["last_done"], 2)
                    step.mark(dve.tensor_copy(yr[0:1, 0, cols], tmp[0:1, 0, :]))
                    step(dve.tensor_tensor(yi[0:1, 0, cols], ui[0:1, :], last[0:1, cols], ALU.mult))
                dve.sem_inc(S["bank_free"], 1)
            for m in range(KT):
                dve.wait_ge(S["back"], m + 1)
                dve.scalar_tensor_tensor(out=tmp[:, m % 4, :], in0=T.uT[:, m, :], scalar=G.col("hy_skip", m), in1=G.banks[:, m, :],
                                         op0=ALU.mult, op1=ALU.add).then_inc(S["skipped"], 1)
                dve.wait_ge(S["skipped"], m + 1)
                dve.tensor_tensor(G.hT[:, m, :], tmp[:, m % 4, :], T.x0T[:, m, :], ALU.mult).then_inc(S["gated"], 1)
                dve.wait_ge(S["gated"], m + 1)
            for m in range(KT):
                dve.wait_ge(S["out_done"], m + 1)
                dve.scalar_tensor_tensor(out=G.x[:, m, :], in0=G.banks[:, m, :], scalar=G.col("hy_b_out", m), in1=G.x[:, m, :],
                                         op0=ALU.add, op1=ALU.add).then_inc(S["added"], 1)

        G.first += 4


def hyena(G):
    with ExitStack() as ctx:
        T = Shared()
        T.ksum = G.sb("filter_sum", [P, JT, D], ctx=ctx)
        T.kdiff = G.sb("filter_difference", [P, JT, D], ctx=ctx)
        T.uT = G.sb("hyena_u_T", [P, KT, SEQ], ctx=ctx)
        T.x0T = G.sb("hyena_x0_T", [P, KT, SEQ], ctx=ctx)
        hyena_filters(G, T)
        hyena_projection(G, T)
        hyena_convolution(G, T)



RW_CHUNK = 64
RW_N = 64
N_CHUNKS = SEQ // RW_CHUNK
LEVELS = 6
LORA, GATE_LORA = 64, 128
RW_GN_EPS = RW_N * 1e-5
DECAY_SCALE = -float(np.exp(-0.5))
FWD, BWD = 0, 1
SPILLED = 5


def scan_masks():
    s, t = np.arange(P)[:, None], np.arange(P)[None]
    same = (s // RW_CHUNK) == (t // RW_CHUNK)
    out = []
    for l in range(LEVELS):
        b = 1 << l
        m = ((s // (2 * b)) == (t // (2 * b))) & (s % (2 * b) >= b) & (t % (2 * b) < b)
        out += [m, m.T]
    for before, upto in ((same & (s < t), same & (s <= t)), (same & (s > t), same & (s >= t))):
        before, upto = before.astype(np.float32), upto.astype(np.float32)
        out += [-before, upto, before, upto]
    out.append(np.broadcast_to((np.arange(SEQ) % RW_CHUNK != 0)[None], (P, SEQ)))
    out.append(np.tile(np.eye(RW_N), (2, 1)))
    return np.concatenate([o.astype(np.float32) for o in out], 1)


def lay_rwkv(L, a):
    wide = lambda v: np.concatenate([v, np.zeros((P - v.shape[0], v.shape[1]), np.float32)])
    for n in ("r", "k", "v"):
        L.column_chunks(a[f"rw_w_{n}"][0])
    L.chunk(L.matrix(a["rw_w1"][0, 0]), L.matrix(a["rw_w1"][0, 1]), L.matrix(a["rw_a1"][0]), L.matrix(a["rw_g1"][0]), a["rw_g2"][0])
    L.chunk(wide(a["rw_w2"][0, 0]), wide(a["rw_w2"][0, 1]), wide(a["rw_a2"][0]))
    L.column_chunks(a["rw_w_o"][0])
    L.vector("rw_norm", a["norm_mix_g"][1])
    L.vector("rw_mu", a["rw_mu"][0].reshape(-1))
    L.vector("rw_w0", a["rw_w0"][0].reshape(-1))
    for n in ("a0", "k_k", "k_a", "ln_w", "ln_b"):
        L.vector("rw_" + n, a["rw_" + n][0])
    L.vector("rw_r_k", a["rw_r_k"][0].reshape(-1))
    same = np.arange(P)[:, None] // RW_N == np.arange(P)[None] // RW_N
    L.constant("mean64", same.astype(np.float32) / RW_N)


def spread(ap, n):
    return bass.AP(tensor=ap.tensor, offset=ap.offset, ap=[ap.ap[0], [0, n], ap.ap[1]])


def rwkv_projection(G, T):
    nc = G.nc
    R, K, V, W0, W1, A1, G1, A2 = 0, 8, 16, 24, 25, 26, 27, 28
    N_OUT = A2 + KT
    LERPS = ("r", "k", "v", "w", "a", "g")
    MU = (0, 2, 3, 1, 4, 5)
    with ExitStack() as ctx:
        S = stage(G, "rwin", ctx, *RMS, "delta", "lerped", "out_sum", "out_done", "g2_copied", "raw", "keys_squared", "norm_sum",
                  "floored", "rooted", "step", "mixed", "unit", "spilled")
        big = {n: G.sb("rwin_" + n, [P, KT, SEQ], ctx=ctx) for n in ("xx", "x0", "x1", "r", "k", "v", "a")}
        xx = big["xx"]
        rstd = G.sb("rwin_rstd", [P, SEQ], ctx=ctx)
        al = G.sb("rwin_a_lora", [LORA, SEQ], ctx=ctx)
        block = ctx.enter_context(nc.Block())
        lora_at = {W0: (0, LORA), W1: (KT * LORA, LORA), A1: (2 * KT * LORA, LORA), G1: (3 * KT * LORA, GATE_LORA)}
        last_use = {0: R + KT, 1: K + KT, 2: V + KT, 3: W1 + 1, 4: A1 + 1}

        @block.sync
        def _(sp):
            sp.dma_start(T.x_dram.ap().rearrange("t p n -> p t n"), G.x[:, :, :]).then_inc(S["spilled"], 16)
            G.feed(sp, 6, S["out_sum"], per=4)
            sp.wait_ge(S["out_done"], N_OUT)
            sp.wait_ge(S["g2_copied"], 1)
            G.first += 6
            G.feed(sp, 1, S["out_sum"], base=G1)
            G.first -= 6
            sp.wait_ge(S["mixed"], KT)
            sp.wait_ge(S["unit"], 2 * KT)
            for n, name in enumerate(("r", "x1", "x0", "a", "v")):
                sp.dma_start(T.spill.ap()[:, :, n * SEQ:(n + 1) * SEQ].rearrange("t p n -> p t n"), big[name][:, :, :])\
                  .then_inc(S["spilled"], 16)
            sp.wait_ge(S["spilled"], 16 * (SPILLED + 1))

        @block.tensor
        def _(pe):
            rms_pe(pe, G, S, xx, 7)
            n = 0

            def bank():
                if n >= 8:
                    pe.wait_ge(S["out_done"], n - 7)
                return n % 8

            for l in range(3):
                for m in range(KT):
                    c = 2 * l + m // 4
                    if m % 4 == 0:
                        G.arrived(pe, c % 2, c // 2)
                    if m == 0:
                        pe.wait_ge(S["lerped"], KT * (l + 1))
                    project(pe, G, c % 2, m % 4, bank(), big[f"x{l % 2}"]).then_inc(S["out_sum"], 1)
                    n += 1
            G.arrived(pe, 0, 3)
            w = G.ring[:, G.slot(0), :]
            for l, outs in ((3, (W0, W1)), (4, (A1,)), (5, (G1,))):
                pe.wait_ge(S["lerped"], KT * (l + 1))
                for o in outs:
                    at, width = lora_at[o]
                    b = bank()
                    for k in range(KT):
                        mm = pe.matmul(G.banks[0:width, b, :], w[:, at + k * width:at + (k + 1) * width], big[f"x{l % 2}"][:, k, :],
                                       start=(k == 0), stop=(k == KT - 1))
                    mm.then_inc(S["out_sum"], 1)
                    n += 1
            G.arrived(pe, 1, 3)
            w2 = G.ring[0:LORA, G.slot(1), :]
            pe.wait_ge(S["out_done"], A1 + 1)
            for m in range(KT):
                b = bank()
                pe.matmul(G.banks[:, b, :], w2[:, 2 * D + m * P:2 * D + (m + 1) * P], al[:, :], start=True, stop=True)\
                  .then_inc(S["out_sum"], 1)
                n += 1
            pe.wait_ge(S["out_done"], N_OUT)
            for m in range(KT):
                pe.wait_ge(S["keys_squared"], m + 1)
                pe.matmul(G.banks[:, m, :], G.con("mean64"), xx[:, m, :], start=True, stop=True).then_inc(S["norm_sum"], 1)

        @block.scalar
        def _(act):
            rms_act(act, G, S, xx)
            rms_root(act, G, S, rstd)
            for n in range(N_OUT):
                act.wait_ge(S["out_sum"], n + 1)
                of = G.banks[:, n % 8, :]
                if n < W0:
                    ins = act.activation(big["rkv"[n // KT]][:, n % KT, :], of, ACT.Copy)
                elif n < A1:
                    ins = act.activation(T.tanh[:, n - W0, :], of[0:LORA, :], ACT.Tanh)
                elif n == A1:
                    ins = act.activation(al[:, :], of[0:LORA, :], ACT.Copy)
                elif n == G1:
                    ins = act.activation(T.sg[:, :], of, ACT.Sigmoid)
                else:
                    ins = act.activation(big["a"][:, n - A2, :], of, ACT.Sigmoid, bias=G.col("rw_a0", n - A2))
                ins.then_inc(S["out_done"], 1)
            at = 3 * KT * LORA + KT * GATE_LORA
            act.activation(T.g2[:, :], G.ring[:, G.slot(0), at:at + D], ACT.Copy).then_inc(S["g2_copied"], 1)
            for m in range(KT):
                act.wait_ge(S["raw"], m + 1)
                act.activation(xx[:, m, :], big["x0"][:, m, :], ACT.Square).then_inc(S["keys_squared"], 1)
            for m in range(KT):
                act.wait_ge(S["floored"], m + 1)
                act.activation(xx[:, m, :], xx[:, m, :], ACT.Sqrt).then_inc(S["rooted"], 1)

        @block.vector
        def _(dve):
            rms_dve(dve, G, S, rstd, 7, "rw_norm", G.hT)
            h, n = G.hT, SEQ
            dve.wait_ge(S["h_ready"], KT)
            dve.tensor_tensor(xx[:, :, 1:n - 1], h[:, :, 0:n - 2], h[:, :, 2:n], ALU.add).then_inc(S["delta"], 1)
            dve.tensor_copy(xx[:, :, 0:1], h[:, :, 1:2]).then_inc(S["delta"], 1)
            dve.tensor_copy(xx[:, :, n - 1:n], h[:, :, n - 2:n - 1]).then_inc(S["delta"], 1)
            dve.wait_ge(S["delta"], 3)
            for k in range(KT):
                dve.scalar_tensor_tensor(out=xx[:, k, :], in0=xx[:, k, :], scalar=0.5, in1=h[:, k, :],
                                         op0=ALU.mult, op1=ALU.subtract).then_inc(S["delta"], 1)
            dve.wait_ge(S["delta"], 3 + KT)
            for l in range(len(LERPS)):
                if l >= 2:
                    dve.wait_ge(S["out_sum"], last_use[l - 2])
                for k in range(KT):
                    dve.scalar_tensor_tensor(out=big[f"x{l % 2}"][:, k, :], in0=xx[:, k, :], scalar=G.col("rw_mu", MU[l] * KT + k),
                                             in1=h[:, k, :], op0=ALU.mult, op1=ALU.add).then_inc(S["lerped"], 1)
            dve.wait_ge(S["out_done"], N_OUT)
            dve.wait_ge(S["lerped"], KT * len(LERPS))
            kk, mixed, b = big["x0"], big["x1"], big["a"]
            step = Link(dve, S["step"])
            for m in range(KT):
                dve.tensor_scalar(kk[:, m, :], big["k"][:, m, :], G.col("rw_k_k", m), None, ALU.mult).then_inc(S["raw"], 1)
                step(dve.tensor_scalar(mixed[:, m, :], b[:, m, :], -1.0, G.col("rw_k_a", m), ALU.add, ALU.mult))
                dve.scalar_tensor_tensor(out=mixed[:, m, :], in0=mixed[:, m, :], scalar=1.0, in1=big["k"][:, m, :],
                                         op0=ALU.add, op1=ALU.mult).then_inc(S["mixed"], 1)
            for m in range(KT):
                dve.wait_ge(S["norm_sum"], m + 1)
                dve.tensor_scalar(xx[:, m, :], G.banks[:, m, :], float(RW_N), 1e-24, ALU.mult, ALU.max).then_inc(S["floored"], 1)
            for m in range(KT):
                dve.wait_ge(S["rooted"], m + 1)
                step(dve.reciprocal(xx[:, m, :], xx[:, m, :]))
                dve.tensor_tensor(kk[:, m, :], kk[:, m, :], xx[:, m, :], ALU.mult).then_inc(S["unit"], 1)
                dve.wait_ge(S["unit"], 2 * m + 1)
                dve.tensor_tensor(b[:, m, :], b[:, m, :], kk[:, m, :], ALU.mult).then_inc(S["unit"], 1)

        G.first += 7


def rwkv_scan(G, T):
    nc = G.nc
    PER = dict(loaded=16, staged=2, decay_sum=2, decay_gate=2, exponents=2, sums_read=4, exps=2, operands=2, bonus_in=1, bonus_sum=1, bonus_done=1,
               token_sum=7, token_done=7, gram_sum=16, gram_done=16, z_sum=24, z_done=20, x_sum=20, x_done=24, y_sum=24, y_done=24,
               nv_sum=2, nv_done=2, ua_sum=4, ua_done=4, phi_sum=4, phi_done=4, psi_done=4, own_sum=2, own_done=2, read_sum=2,
               read_done=2, state_sum=12, state_done=12, past_sum=2, turn_done=1, bonus_stored=16)
    with ExitStack() as ctx:
        S = stage(G, "scan", ctx, "masks_loaded", "step", "go", *PER)
        ld = G.sb("scan_in", [P, SPILLED, SEQ], ctx=ctx)
        early = G.sb("scan_early", [P, 9 * SEQ], ctx=ctx)
        ex = early[:, :].rearrange("p (n t) -> p n t", n=9)
        MH = early[:, 0:8 * SEQ].rearrange("p (d h j w t) -> p d h j w t", d=2, h=2, j=JT, w=2)
        NG = G.sb("scan_NG", [P, 2, 2, JT, 2, P], ctx=ctx)
        AR = G.sb("scan_AR", [P, 2, JT, 2, P], ctx=ctx)
        KB = G.sb("scan_KB", [P, 2, 2, SEQ], ctx=ctx)
        hat = G.sb("scan_hat", [P, 2, 2, SEQ], ctx=ctx)
        phi = hat[:, :, 0, :].rearrange("p d (c k) -> p d c k", c=N_CHUNKS)
        psi = hat[:, :, 1, :].rearrange("p d (c k) -> p d c k", c=N_CHUNKS)
        X = G.sb("scan_X", [P, 2, 2, JT, P], ctx=ctx)
        Y = G.sb("scan_Y", [P, 2, 2, JT, P], ctx=ctx)
        NA = G.sb("scan_NA", [P, 2, 2, JT, P], ctx=ctx)
        tok = G.sb("scan_tok", [P, 2, 2, JT, P], ctx=ctx)
        vt = G.sb("scan_v", [P, JT, P], ctx=ctx)
        pe_end = G.sb("scan_decay", [P, 2, N_CHUNKS], ctx=ctx)
        state = G.sb("scan_state", [P, 2, N_CHUNKS, RW_N], ctx=ctx)
        bonus = G.sb("scan_bonus", [P, SEQ], ctx=ctx)
        w2 = G.sb("scan_w2", [LORA, 2, P], ctx=ctx)
        masks = G.sb("scan_masks_sb", list(G.aps["scan_masks"].shape), ctx=ctx)
        block = ctx.enter_context(nc.Block())
        B = lambda d, n: G.banks[:, 4 * d + n, :]
        Z = lambda d, h: KB[:, d, h, 0:JT * RW_CHUNK]

        added = lambda b: b[:, JT * RW_CHUNK:]

        def opened(x, l, d):
            return x.rearrange("p j (n e s) -> p j n e s", e=2, s=1 << l)[:, :, :, d, :]

        def joined(z, l):
            return z[:, 0:JT * RW_CHUNK].rearrange("p (j n s) -> p j n s", j=JT, s=1 << l)

        at = 2 * LEVELS * P
        level_mask = lambda l, d: masks[:, (2 * l + d) * P:(2 * l + d + 1) * P]
        gram_mask = lambda d, w: masks[:, at + (2 * d + w) * 2 * P:at + (2 * d + w + 1) * 2 * P]
        reset = masks[:, at + 8 * P:at + 8 * P + SEQ]
        eye = masks[:, at + 8 * P + SEQ:at + 8 * P + SEQ + RW_N]
        order = [list(range(N_CHUNKS)), list(range(N_CHUNKS))[::-1]]
        heads = [slice(0, RW_N), slice(RW_N, P)]
        b_slot = G.slot(0)

        def exponents(d):
            lw, F, E1, E2 = (ex[:, 4 * d + n, :] for n in range(4))
            return lw, F, E1, E2, F if d == FWD else ex[:, 8, :]

        def needer(eng, i):
            return lambda name, n: eng.wait_ge(S[name], PER[name] * i + n)

        @block.sync
        def _(sp):
            sp.dma_start(masks[:, :], G.aps["scan_masks"]).then_inc(S["masks_loaded"], 16)
            with sp.Fori(0, KT) as i:
                sp.wait_ge(S["turn_done"], i + 1)
                sp.dma_start(ld[:, :, :], T.spill.ap()[i].rearrange("p (a n) -> p a n", a=SPILLED)).then_inc(S["loaded"], 16)
                sp.wait_ge(S["bonus_done"], i + 1)
                sp.dma_start(T.bonus_dram.ap()[i], bonus[:, :]).then_inc(S["bonus_stored"], 16)
            sp.wait_ge(S["bonus_stored"], 16 * KT)
            G.feed(sp, 1, S["turn_done"], per=KT + 1)

        @block.tensor
        def _(pe):
            G.arrived(pe, 0, 0)
            pe.wait_ge(S["masks_loaded"], 16)
            with pe.Fori(0, KT) as i:
                need = needer(pe, i)
                for d in (FWD, BWD):
                    need("staged", d + 1)
                    pe.matmul(B(d, 0), w2[:, d, :], T.tanh[:, d, :], start=True, stop=True).then_inc(S["decay_sum"], 1)
                need("bonus_in", 1)
                pe.matmul(B(0, 2), G.con("mean64"), bonus[:, :], start=True, stop=True).then_inc(S["bonus_sum"], 1)
                need("loaded", 16)
                for j in range(JT):
                    mm = pe.transpose(B(0, 1)[:, j * P:(j + 1) * P], ld[:, 4, j * P:(j + 1) * P], G.con("ident"))
                mm.then_inc(S["token_sum"], 1)
                need("token_done", 1)
                need("bonus_done", 1)
                for d in (FWD, BWD):
                    need("operands", d + 1)
                    for n, of in enumerate((AR[:, d, :, 0, :], hat[:, d, 0, :], hat[:, d, 1, :])):
                        for j in range(JT):
                            src = of[:, j, :] if n == 0 else of[:, j * P:(j + 1) * P]
                            mm = pe.transpose(B(d, 1 + n)[:, j * P:(j + 1) * P], src, G.con("ident"))
                        mm.then_inc(S["token_sum"], 1)
                for w, left in ((0, 1), (1, 0)):
                    for d in (FWD, BWD):
                        if w == 0:
                            need("token_done", 1 + 3 * (d + 1))
                        for h in range(2):
                            for j in range(JT):
                                if w == 1 and j % 2 == 0:
                                    need("gram_done", 4 * d + 2 * h + j // 2 + 1)
                                mm = pe.matmul(B(d, 2 * h + j // 2)[:, (j % 2) * 256:(j % 2) * 256 + 256],
                                               KB[heads[h], d, left, j * P:(j + 1) * P], AR[heads[h], d, j, :, :],
                                               start=True, stop=True)
                                if j % 2:
                                    mm.then_inc(S["gram_sum"], 1)
                def transposes(l):
                    for d in (FWD, BWD):
                        for h in range(2):
                            need("x_done", 4 * l + 2 * d + h + 1)
                            for j in range(JT):
                                mm = pe.transpose(B(d, 2 + h)[:, j * P:(j + 1) * P], X[:, d, h, j, :], G.con("ident"))
                            mm.then_inc(S["y_sum"], 1)

                for l in range(LEVELS):
                    for d in (FWD, BWD):
                        for h in range(2):
                            need("gram_done" if l == 0 else "x_done", 8 + 4 * d + 4 if l == 0 else 4 * (l - 1) + 2 * d + h + 1)
                            for j in range(JT):
                                if l == 0:
                                    mm = pe.transpose(B(d, h)[:, j * P:(j + 1) * P], MH[:, d, h, j, 0, :], G.con("ident"))
                                else:
                                    mm = pe.matmul(joined(B(d, h), l)[:, j], MH[:, d, h, j, 0, :],
                                                   opened(X[:, d, h, :, :], l, d)[:, j], start=True, stop=True)
                            mm.then_inc(S["z_sum"], 1)
                    if l:
                        transposes(l - 1)
                        for d in (FWD, BWD):
                            for h in range(2):
                                need("z_done", 4 * (l - 1) + 2 * d + h + 1)
                                need("y_done", 4 * (l - 1) + 2 * d + h + 1)
                                for j in range(JT):
                                    mm = pe.matmul(added(B(d, h))[:, j * RW_CHUNK:(j + 1) * RW_CHUNK], Y[:, d, h, j, :],
                                                   Z(d, h)[:, j * RW_CHUNK:(j + 1) * RW_CHUNK], start=True, stop=True)
                                mm.then_inc(S["x_sum"], 1)
                transposes(LEVELS - 1)
                for d in (FWD, BWD):
                    need("y_done", 4 * (LEVELS - 1) + 2 * d + 1)
                    for h in range(2):
                        for j in range(JT):
                            mm = pe.matmul(B(d, 2)[:, (h * JT + j) * RW_N:(h * JT + j + 1) * RW_N], NG[:, d, h, j, 0, :],
                                           vt[:, j, heads[h]], start=True, stop=True)
                    mm.then_inc(S["nv_sum"], 1)
                for d in (FWD, BWD):
                    need("nv_done", d + 1)
                    for h in range(2):
                        need("y_done", 4 * (LEVELS - 1) + 2 * d + h + 1)
                        for j in range(JT):
                            mm = pe.matmul(B(d, h)[:, j * P:(j + 1) * P], Y[:, d, h, j, :], NA[:, d, h, j, :], start=True, stop=True)
                        mm.then_inc(S["ua_sum"], 1)
                for d in (FWD, BWD):
                    need("ua_done", 2 * d + 2)
                    pe.sem_inc(S["go"], 1)
                    for half in range(2):
                        rows = heads[half]
                        for j in range(JT):
                            for h in range(2):
                                mm = pe.matmul(B(d, 2 + half)[heads[h], j * RW_N:(j + 1) * RW_N], X[rows, d, h, j, RW_N:P],
                                               tok[rows, d, 1, j, heads[h]], start=True, stop=True)
                                out = B(d, 2 + half)[heads[h], 256 + j * RW_N:256 + (j + 1) * RW_N]
                                pe.matmul(out, tok[rows, d, 0, j, heads[h]], vt[rows, j, heads[h]], start=True, stop=False,
                                          skip_group_check=True)
                                mm = pe.matmul(out, tok[rows, d, 1, j, heads[h]], X[rows, d, h, j, 0:RW_N], start=False, stop=True,
                                               skip_group_check=True)
                        mm.then_inc(S["phi_sum"], 1)
                    for j in range(JT):
                        for h in range(2):
                            out = B(d, 0)[heads[h], j * P:(j + 1) * P]
                            pe.matmul(out, vt[:, j, heads[h]], NG[:, d, h, j, 1, :], start=True, stop=False, skip_group_check=True)
                            mm = pe.matmul(out, X[:, d, h, j, 0:RW_N], MH[:, d, h, j, 1, :], start=False, stop=True,
                                           skip_group_check=True)
                    mm.then_inc(S["own_sum"], 1)
                    for j in range(JT):
                        for h in range(2):
                            mm = pe.matmul(B(d, 1)[heads[h], j * P:(j + 1) * P], X[:, d, h, j, RW_N:P], MH[:, d, h, j, 1, :],
                                           start=True, stop=True)
                    mm.then_inc(S["read_sum"], 1)
                for n in range(1, N_CHUNKS - 1):
                    for d in (FWD, BWD):
                        if n == 1:
                            need("phi_done", 2 * d + 2)
                            need("psi_done", 2 * d + 2)
                        else:
                            need("state_done", 2 * (n - 2) + d + 1)
                        pe.sem_inc(S["go"], 1)
                        for h in range(2):
                            of = psi[heads[h], d, order[d][0], :] if n == 1 else state[heads[h], d, n, :]
                            mm = pe.matmul(B(d, 2 + h)[heads[h], n * RW_N:(n + 1) * RW_N], phi[heads[h], d, order[d][n], :], of,
                                           start=True, stop=True)
                        mm.then_inc(S["state_sum"], 1)
                for d in (FWD, BWD):
                    need("own_done", d + 1)
                    need("read_done", d + 1)
                    need("state_done", 2 * (N_CHUNKS - 3) + d + 1)
                    pe.sem_inc(S["go"], 1)
                    for n in range(1, N_CHUNKS):
                        c = order[d][n]
                        for h in range(2):
                            of = psi[heads[h], d, order[d][0], :] if n == 1 else state[heads[h], d, n, :]
                            mm = pe.matmul(B(d, h)[heads[h], c * RW_CHUNK:(c + 1) * RW_CHUNK], of,
                                           AR[heads[h], d, c // 2, 1, (c % 2) * RW_CHUNK:(c % 2 + 1) * RW_CHUNK], start=True, stop=True)
                    mm.then_inc(S["past_sum"], 1)

        @block.scalar
        def _(act):
            act.wait_ge(G.landed[b_slot], 16 * (G.first // SLOTS + 1))
            with act.Fori(0, KT) as i:
                need = needer(act, i)
                act.wait_ge(S["turn_done"], i + 1)
                for d in (FWD, BWD):
                    act.activation(w2[:, d, :], G.ring[0:LORA, b_slot, bass.ds(d * D + i * P, P)], ACT.Copy).then_inc(S["staged"], 1)
                for d in (FWD, BWD):
                    need("decay_sum", d + 1)
                    act.activation(ex[:, 4 * d, :], B(d, 0), ACT.Sigmoid, bias=G.col("rw_w0", d * KT + i)).then_inc(S["decay_gate"], 1)
                for d in (FWD, BWD):
                    need("exponents", d + 1)
                    lw, F, E1, E2, Fin = exponents(d)
                    act.activation(pe_end[:, d, :], F[:, RW_CHUNK - 1::RW_CHUNK], ACT.Exp).then_inc(S["sums_read"], 1)
                    act.activation(lw, Fin, ACT.Exp, scale=-1.0).then_inc(S["sums_read"], 1)
                    for e in (E1, E2):
                        act.activation(e, e, ACT.Exp)
                    need("sums_read", 2 * d + 2)
                    act.activation(Fin, Fin, ACT.Exp).then_inc(S["exps"], 1)
                need("token_sum", 1)
                act.activation(vt[:, :, :], B(0, 1).rearrange("p (j t) -> p j t", j=JT), ACT.Copy).then_inc(S["token_done"], 1)
                for d in (FWD, BWD):
                    for n in range(3):
                        need("token_sum", 1 + 3 * d + n + 1)
                        of = B(d, 1 + n).rearrange("p (j t) -> p j t", j=JT)
                        if n == 0:
                            for h in range(2):
                                ins = act.activation(NA[:, d, h, :, RW_N:P], of[:, :, heads[h]], ACT.Copy)
                        else:
                            ins = act.activation(tok[:, d, n - 1, :, :], of, ACT.Copy)
                        ins.then_inc(S["token_done"], 1)
                for l in range(LEVELS):
                    for d in (FWD, BWD):
                        for h in range(2):
                            need("y_sum", 4 * l + 2 * d + h + 1)
                            act.activation(Y[:, d, h, :, :], B(d, 2 + h).rearrange("p (j t) -> p j t", j=JT), ACT.Copy)\
                               .then_inc(S["y_done"], 1)
                for d in (FWD, BWD):
                    need("nv_sum", d + 1)
                    act.activation(NA[:, d, :, :, 0:RW_N], B(d, 2).rearrange("p (h j v) -> p h j v", h=2, j=JT), ACT.Copy)\
                       .then_inc(S["nv_done"], 1)
                for d in (FWD, BWD):
                    for h in range(2):
                        need("ua_sum", 2 * d + h + 1)
                        act.activation(X[:, d, h, :, :], B(d, h).rearrange("p (j t) -> p j t", j=JT), ACT.Copy, scale=-1.0)\
                           .then_inc(S["ua_done"], 1)
                for d in (FWD, BWD):
                    for half in range(2):
                        need("phi_done", 2 * d + half + 1)
                        act.activation(psi[:, d, half::2, :], B(d, 2 + half)[:, 256:512].rearrange("p (j k) -> p j k", j=JT), ACT.Copy)\
                           .then_inc(S["psi_done"], 1)

        @block.vector
        def _(dve):
            dve.sem_inc(S["turn_done"], 1)
            dve.wait_ge(S["masks_loaded"], 16)
            step = Link(dve, S["step"])
            with dve.Fori(0, KT) as i:
                need = needer(dve, i)
                step.start(i * STEPS_PER_TURN)
                need("loaded", 16)
                r, k, kk, b, v = (ld[:, n, :] for n in range(SPILLED))
                step(dve.scalar_tensor_tensor(out=bonus[:, :], in0=r, scalar=G.col("rw_r_k", i), in1=k, op0=ALU.mult, op1=ALU.mult))
                dve.sem_inc(S["bonus_in"], 1)
                for d in (FWD, BWD):
                    lw, F, E1, E2, Fin = exponents(d)
                    need("decay_gate", d + 1)
                    step(dve.tensor_scalar(lw, lw, DECAY_SCALE, None, ALU.mult))
                    step(dve.tensor_tensor_scan(F, reset, lw, 0.0, ALU.mult, ALU.add))
                    total = F[:, RW_CHUNK - 1::RW_CHUNK]
                    total = bass.AP(tensor=total.tensor, offset=total.offset, ap=[total.ap[0], total.ap[1], [0, RW_CHUNK]])
                    step.mark(dve.tensor_tensor(E1, F, lw, ALU.subtract))
                    ins = dve.tensor_tensor(E2.rearrange("p (c t) -> p c t", c=N_CHUNKS), total,
                                            F.rearrange("p (c t) -> p c t", c=N_CHUNKS), ALU.subtract)
                    if d == BWD:
                        step(ins)
                        ins = dve.tensor_tensor(Fin, E2, lw, ALU.add)
                    ins.then_inc(S["exponents"], 1)
                need("bonus_sum", 1)
                dve.scalar_tensor_tensor(out=bonus[:, :], in0=B(0, 2), scalar=float(RW_N), in1=v, op0=ALU.mult, op1=ALU.mult)\
                   .then_inc(S["bonus_done"], 1)
                for d in (FWD, BWD):
                    lw, F, E1, E2, Fin = exponents(d)
                    before, behind = (E1, E2) if d == FWD else (E2, E1)
                    need("exps", d + 1)
                    tiles = lambda a: a.rearrange("p (j t) -> p j t", j=JT)
                    dve.tensor_tensor(AR[:, d, :, 0, :], tiles(kk), tiles(before), ALU.mult)
                    dve.tensor_tensor(AR[:, d, :, 1, :], tiles(r), tiles(Fin), ALU.mult)
                    dve.tensor_tensor(KB[:, d, 0, :], k, lw, ALU.mult)
                    dve.tensor_tensor(KB[:, d, 1, :], b, lw, ALU.mult)
                    dve.tensor_tensor(hat[:, d, 0, :], k, behind, ALU.mult)
                    dve.tensor_tensor(hat[:, d, 1, :], b, behind, ALU.mult).then_inc(S["operands"], 1)
                for w, to in ((0, MH), (1, NG)):
                    for d in (FWD, BWD):
                        for h in range(2):
                            for jp in range(2):
                                need("gram_sum", 8 * w + 4 * d + 2 * h + jp + 1)
                                dve.tensor_tensor(to[:, d, h, 2 * jp:2 * jp + 2, :, :].rearrange("p j w t -> p j (w t)"),
                                                  B(d, 2 * h + jp).rearrange("p (j n) -> p j n", j=2), spread(gram_mask(d, w), 2),
                                                  ALU.mult).then_inc(S["gram_done"], 1)
                for d in (FWD, BWD):
                    for h in range(2):
                        need("z_sum", 2 * d + h + 1)
                        x = X[:, d, h, :, :]
                        step(dve.tensor_tensor(x, B(d, h).rearrange("p (j t) -> p j t", j=JT), spread(level_mask(0, d), JT), ALU.mult))
                        dve.tensor_tensor(x, x, spread(G.con("ident"), JT), ALU.add).then_inc(S["x_done"], 1)
                for l in range(1, LEVELS):
                    for d in (FWD, BWD):
                        for h in range(2):
                            need("z_sum", 4 * l + 2 * d + h + 1)
                            mask = level_mask(l, d).rearrange("p (n e s) -> p n e s", e=2, s=1 << l)[:, :, d, :]
                            mask = bass.AP(tensor=mask.tensor, offset=mask.offset, ap=[mask.ap[0], [0, JT], *list(mask.ap)[1:]])
                            dve.tensor_tensor(joined(Z(d, h), l), joined(B(d, h), l), mask, ALU.mult).then_inc(S["z_done"], 1)
                    for d in (FWD, BWD):
                        for h in range(2):
                            need("x_sum", 4 * (l - 1) + 2 * d + h + 1)
                            x = opened(X[:, d, h, :, :], l, d)
                            dve.tensor_tensor(x, x, joined(added(B(d, h)), l), ALU.add).then_inc(S["x_done"], 1)
                for d in (FWD, BWD):
                    for half in range(2):
                        need("phi_sum", 2 * d + half + 1)
                        for j in range(JT):
                            c = 2 * j + half
                            ins = dve.scalar_tensor_tensor(out=phi[:, d, c, :], in0=eye, scalar=pe_end[:, d, c:c + 1],
                                                           in1=B(d, 2 + half)[:, j * RW_N:(j + 1) * RW_N], op0=ALU.mult, op1=ALU.add)
                        ins.then_inc(S["phi_done"], 1)
                    need("own_sum", d + 1)
                    y = G.hT[:, i, :]
                    if d == FWD:
                        dve.tensor_copy(y, B(d, 0)).then_inc(S["own_done"], 1)
                        need("own_done", 1)
                    else:
                        dve.tensor_tensor(y, y, B(d, 0), ALU.add).then_inc(S["own_done"], 1)
                        need("own_done", 2)
                    need("read_sum", d + 1)
                    dve.tensor_tensor(AR[:, d, :, 1, :], AR[:, d, :, 1, :], B(d, 1).rearrange("p (j t) -> p j t", j=JT), ALU.add)\
                       .then_inc(S["read_done"], 1)
                for n in range(1, N_CHUNKS - 1):
                    for d in (FWD, BWD):
                        need("state_sum", 2 * (n - 1) + d + 1)
                        if n == 1:
                            need("psi_done", 2 * d + 2)
                        for h in range(2):
                            ins = dve.tensor_tensor(state[heads[h], d, n + 1, :], B(d, 2 + h)[heads[h], n * RW_N:(n + 1) * RW_N],
                                                    psi[heads[h], d, order[d][n], :], ALU.add)
                        ins.then_inc(S["state_done"], 1)
                for d in (FWD, BWD):
                    need("past_sum", d + 1)
                    span = slice(RW_CHUNK, SEQ) if d == FWD else slice(0, SEQ - RW_CHUNK)
                    for h in range(2):
                        y = G.hT[heads[h], i, span]
                        step.mark(dve.tensor_tensor(y, y, B(d, h)[heads[h], span], ALU.add))
                    step.settle()
                need("bonus_stored", 16)
                dve.sem_inc(S["turn_done"], 1)
                assert step.n == STEPS_PER_TURN, step.n

        G.first += 1


STEPS_PER_TURN = 16


def rwkv_output(G, T):
    nc = G.nc
    with ExitStack() as ctx:
        S = stage(G, "rwout", ctx, "loaded", "mean_sum", "centred", "squared", "var_sum", "floored", "rooted", "step", "normed",
                  "gate_sum", "gated", "out_done", "added")
        sq = G.sb("rwout_squares", [P, KT, SEQ], ctx=ctx)
        bonus = G.sb("rwout_bonus", [P, KT, SEQ], ctx=ctx)
        block = ctx.enter_context(nc.Block())

        @block.sync
        def _(sp):
            sp.dma_start(bonus[:, :, :], T.bonus_dram.ap().rearrange("t p n -> p t n")).then_inc(S["loaded"], 16)
            sp.dma_start(G.x[:, :, :], T.x_dram.ap().rearrange("t p n -> p t n")).then_inc(S["loaded"], 16)
            G.feed(sp, 2, S["out_done"], per=4)

        @block.tensor
        def _(pe):
            for m in range(KT):
                pe.matmul(G.banks[:, m, :], G.con("mean64"), G.hT[:, m, :], start=True, stop=True).then_inc(S["mean_sum"], 1)
            for m in range(KT):
                pe.wait_ge(S["squared"], m + 1)
                pe.matmul(G.banks[:, m, :], G.con("mean64"), sq[:, m, :], start=True, stop=True).then_inc(S["var_sum"], 1)
            for m in range(KT):
                pe.wait_ge(S["floored"], m + 1)
                pe.matmul(G.banks[:, m, :], T.g2[:, m * P:(m + 1) * P], T.sg[:, :], start=True, stop=True).then_inc(S["gate_sum"], 1)
            pe.wait_ge(S["gated"], KT)
            for m in range(KT):
                if m % 4 == 0:
                    G.arrived(pe, m // 4, 0)
                project(pe, G, m // 4, m % 4, m, G.hT).then_inc(S["out_done"], 1)

        @block.scalar
        def _(act):
            for m in range(KT):
                act.wait_ge(S["centred"], m + 1)
                act.activation(sq[:, m, :], G.hT[:, m, :], ACT.Square).then_inc(S["squared"], 1)
            for m in range(KT):
                act.wait_ge(S["floored"], m + 1)
                act.activation(sq[:, m, :], sq[:, m, :], ACT.Sqrt).then_inc(S["rooted"], 1)

        @block.vector
        def _(dve):
            step = Link(dve, S["step"])
            for m in range(KT):
                dve.wait_ge(S["mean_sum"], m + 1)
                dve.tensor_tensor(G.hT[:, m, :], G.hT[:, m, :], G.banks[:, m, :], ALU.subtract).then_inc(S["centred"], 1)
            for m in range(KT):
                dve.wait_ge(S["var_sum"], m + 1)
                dve.tensor_scalar(sq[:, m, :], G.banks[:, m, :], RW_GN_EPS, None, ALU.add).then_inc(S["floored"], 1)
            dve.wait_ge(S["loaded"], 32)
            for m in range(KT):
                y = G.hT[:, m, :]
                dve.wait_ge(S["rooted"], m + 1)
                step(dve.reciprocal(sq[:, m, :], sq[:, m, :]))
                step(dve.tensor_tensor(y, y, sq[:, m, :], ALU.mult))
                step(dve.tensor_scalar(y, y, G.col("rw_ln_w", m), G.col("rw_ln_b", m), ALU.mult, ALU.add))
                step(dve.tensor_tensor(y, y, bonus[:, m, :], ALU.add))
                dve.wait_ge(S["gate_sum"], m + 1)
                dve.tensor_tensor(y, y, G.banks[:, m, :], ALU.mult).then_inc(S["gated"], 1)
            for m in range(KT):
                dve.wait_ge(S["out_done"], m + 1)
                dve.tensor_tensor(G.x[:, m, :], G.x[:, m, :], G.banks[:, m, :], ALU.add).then_inc(S["added"], 1)

        G.first += 2


def rwkv(G):
    nc = G.nc
    with ExitStack() as ctx:
        T = Shared()
        T.spill = nc.dram_tensor("rwkv_operands", [KT, P, SPILLED * SEQ], F32, kind="Internal")
        T.bonus_dram = nc.dram_tensor("rwkv_bonus", [KT, P, SEQ], F32, kind="Internal")
        T.x_dram = nc.dram_tensor("rwkv_residual", [KT, P, SEQ], F32, kind="Internal")
        T.tanh = G.sb("rwkv_tanh", [LORA, 2, SEQ], ctx=ctx)
        T.sg = G.sb("rwkv_gate", [P, SEQ], ctx=ctx)
        T.g2 = G.sb("rwkv_g2", [P, D], ctx=ctx)
        rwkv_projection(G, T)
        rwkv_scan(G, T)
        rwkv_output(G, T)


def second_block(G):
    hyena(G)
    feed_forward(G, "ffn2", "ff_norm_0", "ff_taps_0", ACT.Silu, 1)
    rwkv(G)
    feed_forward(G, "ffn3", "ff_norm_1", "ff_taps_1", ACT.Silu, 1)
    norm_in_place(G, "final2", "final_norm_2")



M_HEADS, M_DIM = 4, 512
M_WIDTH = M_HEADS * M_DIM
MT_ = M_DIM // P
H_HEADS, H_DIM = 8, 128
M_TAPS = 4
ALPHA = 2 ** 0.25
LN_EPS = 1e-5
HEAD_EPS = 1e-6
N_PAIRS = JT * (JT + 1) // 2
pair = lambda i, j: j * (j + 1) // 2 + i


def third_extra(a):
    at = 4 * M_WIDTH
    w = np.ascontiguousarray(a["w_in"][0][:, at:at + 2 * M_HEADS])
    b = a["b_in"][0]
    rows = np.concatenate([b[4096:6144].reshape(4, 512), b[6144:8192].reshape(4, 512),
                           np.concatenate([b[10248:11272].reshape(2, 512), np.zeros((2, 512), np.float32)])], 1)
    return {"w_if": Layout().matrix(w), "bias_rows3": np.ascontiguousarray(rows), "third_masks": third_masks(),
            "pair_masks": pair_masks()}


def third_masks():
    s, t = np.arange(P)[:, None], np.arange(P)[None]
    pick = np.zeros((P, M_HEADS * P), np.float32)
    for h in range(M_HEADS):
        pick[h, h * P:(h + 1) * P] = 1.0
    return np.concatenate([np.broadcast_to((np.arange(SEQ) % P != 0)[None].astype(np.float32), (P, SEQ)),
                           np.where(s > t, NEG, 0.0).astype(np.float32), pick], 1)


def pair_masks():
    s, t = np.arange(P)[:, None], np.arange(P)[None]
    out = []
    for l in range(7):
        b = 1 << l
        out.append((s // (2 * b) == t // (2 * b)) & (s % (2 * b) < b) & (t % (2 * b) >= b))
    return np.concatenate(out, 1).astype(np.uint32)


def lay_third(L, a):
    w, b = a["w_in"][0], a["b_in"][0]
    for h in range(M_HEADS):
        for s in range(4):
            at = s * M_WIDTH + h * M_DIM
            L.column_chunks(w[:, at:at + M_DIM])
    hq = 4 * M_WIDTH + 2 * M_HEADS
    for g in range(2):
        for s in range(4):
            at = hq + s * D + g * 512
            L.column_chunks(w[:, at:at + 512])
    L.column_chunks(w[:, hq + 4 * D:])
    L.row_chunks(a["w_proj_a"][0])
    L.row_chunks(a["w_proj_b"][0])
    L.column_chunks(a["w_out"][0])
    L.column_chunks(np.concatenate([a["w_ffn_gate"][0], a["w_ffn_up"][0]], 1), L.up_order())
    L.row_chunks(a["w_ffn_down"][0])
    six = np.concatenate([a["conv_w"][0], a["conv_b"], b[None, :2 * M_WIDTH]]).reshape(6, 32, P)
    L.column("m_conv", six.transpose(2, 1, 0).reshape(P, 6 * 32))
    L.column("m_if_bias", np.stack([b[8192:8196], b[8196:8200]], 1))
    L.vector("m_gain", a["m_norm_g"][0])
    for n, at in (("hq", hq), ("hf", hq + D), ("hg", hq + 3 * D), ("ga", hq + 4 * D), ("gb", hq + 5 * D)):
        L.vector("b_" + n, b[at:at + D])
    L.vector("h_gain", a["h_norm_g"][0])
    for n in ("ln1_g", "ln1_b", "ln2_g", "ln2_b"):
        L.vector(n, a[n][0])


def mlstm_gates(G, T):
    nc = G.nc
    with ExitStack() as ctx:
        S = stage(G, "gate", ctx, "loaded", "if_sum", "if_done", "magnitude", "exp_done", "log_done", "step", "rows_done",
                  "floor_in", "floor_done", "turned", "spread_sum", "spread_done")
        wif = G.sb("gate_w", [P, KT * 2 * M_HEADS], ctx=ctx)
        row = G.sb("gate_rows", [M_HEADS, 8, SEQ], ctx=ctx)
        gt = G.sb("gate_pairs", [M_HEADS, JT, SEQ], ctx=ctx)
        small = G.sb("gate_small", [M_HEADS, 4 * JT], ctx=ctx)
        zero = G.sb("gate_zero", [M_HEADS, P], ctx=ctx)
        ig, fg, ab, F, gd, M, nM, fl = (row[:, n, :] for n in range(8))
        block = ctx.enter_context(nc.Block())

        @block.sync
        def _(sp):
            sp.dma_start(wif[:, :], G.aps["w_if"]).then_inc(S["loaded"], 16)
            sp.dma_start(T.masks[:, :], G.aps["third_masks"]).then_inc(S["loaded"], 16)
            sp.dma_start(T.brows[:, :, :], G.aps["bias_rows3"].rearrange("h (s n) -> h s n", s=3)).then_inc(S["loaded"], 16)
            sp.wait_ge(S["loaded"], 48)

        @block.tensor
        def _(pe):
            pe.wait_ge(S["loaded"], 48)
            for n in range(2):
                for k in range(KT):
                    at = k * 2 * M_HEADS + n * M_HEADS
                    mm = pe.matmul(G.banks[0:M_HEADS, n, :], wif[:, at:at + M_HEADS], G.x[:, k, :], start=(k == 0), stop=(k == KT - 1))
                mm.then_inc(S["if_sum"], 1)
            pe.wait_ge(S["rows_done"], 1)
            for h in range(M_HEADS):
                pe.matmul(G.banks[:, 2 + h, :], T.pick[:, h * P:(h + 1) * P], nM, start=True, stop=True).then_inc(S["spread_sum"], 1)
            for j in range(JT):
                for i in range(j + 1):
                    q = pair(i, j)
                    pe.transpose(G.banks[:, 6, 4 * q:4 * q + 4], gt[:, j, i * P:(i + 1) * P], G.con("ident")[0:M_HEADS, 0:M_HEADS])
            pe.wait_ge(S["floor_done"], 1)
            for j in range(JT):
                q = N_PAIRS + j
                mm = pe.transpose(G.banks[:, 6, 4 * q:4 * q + 4], fl[:, j * P:(j + 1) * P], G.con("ident")[0:M_HEADS, 0:M_HEADS])
            mm.then_inc(S["turned"], 1)

        @block.scalar
        def _(act):
            for n, to in enumerate((ig, fg)):
                act.wait_ge(S["if_sum"], n + 1)
                act.activation(to, G.banks[0:M_HEADS, n, :], ACT.Identity, bias=G.col("m_if_bias", n)[0:M_HEADS, :]).then_inc(S["if_done"], 1)
            act.wait_ge(S["magnitude"], 1)
            act.activation(ab, ab, ACT.Exp, scale=-1.0).then_inc(S["exp_done"], 1)
            act.wait_ge(S["exp_done"], 1)
            act.activation(ab, ab, ACT.Ln, bias=1.0).then_inc(S["log_done"], 1)
            act.wait_ge(S["floor_in"], 1)
            act.activation(fl, fl, ACT.Exp, scale=-1.0).then_inc(S["floor_done"], 1)
            for h in range(M_HEADS):
                act.wait_ge(S["spread_sum"], h + 1)
                act.activation(T.nM[:, h, :], G.banks[:, 2 + h, :], ACT.Copy).then_inc(S["spread_done"], 1)
            act.wait_ge(S["turned"], 1)
            act.activation(T.ucol[:, :, :], G.banks[:, 6, 0:4 * (N_PAIRS + JT)].rearrange("p (q h) -> p q h", h=M_HEADS), ACT.Copy)\
               .then_inc(S["spread_done"], 1)

        @block.vector
        def _(dve):
            step = Link(dve, S["step"])
            step(dve.memset(zero[:, :], 0.0))
            step(dve.memset(small[:, 0:1], 0.0))
            dve.wait_ge(S["if_done"], 2)
            dve.scalar_tensor_tensor(out=ab, in0=fg, scalar=-1.0, in1=fg, op0=ALU.mult, op1=ALU.max).then_inc(S["magnitude"], 1)
            dve.wait_ge(S["log_done"], 1)
            step(dve.scalar_tensor_tensor(out=fg, in0=fg, scalar=0.0, in1=ab, op0=ALU.min, op1=ALU.subtract))
            dve.wait_ge(S["loaded"], 48)
            step(dve.tensor_tensor_scan(F, T.masks[0:M_HEADS, 0:SEQ], fg, 0.0, ALU.mult, ALU.add))
            step(dve.tensor_tensor(gd, ig, F, ALU.subtract))
            for j in range(JT):
                own = slice(j * P, (j + 1) * P)
                before, top, start = (small[:, n * JT + j:n * JT + j + 1] for n in range(3))
                step(dve.tensor_copy(gt[:, j, own], gd[:, own]))
                if j:
                    total = F[:, j * P - 1:j * P]
                    step(dve.tensor_scalar(before, small[:, j - 1:j], total, None, ALU.add))
                    step(dve.tensor_scalar(gt[:, j, 0:j * P], gt[:, j - 1, 0:j * P], total, None, ALU.add))
                    step(dve.tensor_reduce(top, gt[:, j, 0:j * P], AX, ALU.max))
                    step(dve.tensor_tensor(start, top, before, ALU.max))
                step(dve.tensor_tensor_scan(M[:, own], zero[:, :], gd[:, own], start if j else 0.0, ALU.add, ALU.max))
            step(dve.tensor_tensor(fl, F, M, ALU.add))
            dve.sem_inc(S["floor_in"], 1)
            step(dve.tensor_scalar(nM, M, -1.0, None, ALU.mult))
            dve.sem_inc(S["rows_done"], 1)


def mlstm(G, T):
    nc = G.nc
    PER = dict(qk_sum=8, biased=8, conv_done=8, silu_done=8, picked=1, v_sum=4, v_done=4, o_sum=4, o_done=4, diag_done=4, exp_done=4,
               score_sum=4, weighed=4, den_sum=1, num_sum=4, inverted=1, y_done=4, mean_done=4, centred=4, squared=4, rooted=1, var_in=1,
               gated=4, turned=4, head_done=4, turn_done=1)
    with ExitStack() as ctx:
        S = stage(G, "mlstm", ctx, "edges", "step", *PER)
        z = G.sb("mlstm_z", [P, 4, SEQ + M_TAPS - 1], ctx=ctx)
        cv = G.sb("mlstm_conv", [P, 4, SEQ], ctx=ctx)
        qk = G.sb("mlstm_qk", [P, 2, MT_, SEQ], ctx=ctx)
        v = G.sb("mlstm_v", [P, JT, M_DIM], ctx=ctx)
        og = G.sb("mlstm_o", [P, JT, M_DIM], ctx=ctx)
        E = G.sb("mlstm_exp", [P, JT, SEQ], ctx=ctx)
        y = G.sb("mlstm_y", [P, JT, M_DIM], ctx=ctx)
        dg = G.sb("mlstm_diag", [P, JT, P], ctx=ctx)
        pick = G.sb("mlstm_pick", [M_HEADS, P], ctx=ctx)
        st = G.sb("mlstm_stats", [P, 5, JT], ctx=ctx)
        rc, total, mean, sqs, rstd = (st[:, n, :] for n in range(5))
        block = ctx.enter_context(nc.Block())

        def needer(eng, i):
            return lambda name, n: eng.wait_ge(S[name], PER[name] * i + n)

        @block.sync
        def _(sp):
            with sp.Fori(0, M_HEADS) as i:
                for c, (name, n) in enumerate((("qk_sum", 4), ("qk_sum", 8), ("v_sum", 4), ("o_sum", 4))):
                    sp.wait_ge(S[name], PER[name] * i + n)
                    sp.dma_start(G.ring[:, G.slot(c), :], G.weights[4 * i + (G.first + c + SLOTS)])\
                      .then_inc(G.landed[G.slot(c)], 16)

        @block.tensor
        def _(pe):
            with pe.Fori(0, M_HEADS) as i:
                need = needer(pe, i)
                pe.wait_ge(S["turn_done"], i + 1)
                for s in range(2):
                    pe.wait_ge(G.landed[G.slot(s)], 16 * (2 * i + (G.first + s) // SLOTS + 1))
                    for m in range(4):
                        project(pe, G, s, m, 4 * s + m, G.x).then_inc(S["qk_sum"], 1)
                need("picked", 1)
                for s, name in ((0, "v_sum"), (1, "o_sum")):
                    pe.wait_ge(G.landed[G.slot(s)], 16 * (2 * i + (G.first + 2 + s) // SLOTS + 1))
                    w = G.chunk(s, KT)
                    need("biased", 4 * s + 4)
                    for j in range(JT):
                        b = G.banks[:, 4 * s + j, :]
                        for k in range(KT):
                            pe.matmul(b, G.x[:, k, j * P:(j + 1) * P], w[:, k, :], start=(k == 0), stop=False)
                        pe.matmul(b, pick[:, :], T.brows[:, s, :], start=False, stop=True).then_inc(S[name], 1)
                need("silu_done", 8)
                for a in range(JT):
                    need("v_done", a + 1)
                    for k in range(MT_):
                        mm = pe.matmul(G.banks[:, a, a * P:SEQ], qk[:, 1, k, a * P:(a + 1) * P], qk[:, 0, k, a * P:SEQ],
                                       start=(k == 0), stop=(k == MT_ - 1))
                    mm.then_inc(S["score_sum"], 1)
                need("weighed", 4)
                need("o_done", 4)
                for j in range(JT):
                    for a in range(j + 1):
                        mm = pe.matmul(G.banks[:, 0, j:j + 1], E[:, a, j * P:(j + 1) * P], G.con("ones")[:, 0:1],
                                       start=(a == 0), stop=(a == j))
                mm.then_inc(S["den_sum"], 1)
                for j in range(JT):
                    for a in range(j + 1):
                        mm = pe.matmul(G.banks[:, 4 + j, :], E[:, a, j * P:(j + 1) * P], v[:, a, :], start=(a == 0), stop=(a == j))
                    mm.then_inc(S["num_sum"], 1)
                need("gated", 4)
                for k in range(MT_):
                    for j in range(JT):
                        mm = pe.transpose(G.banks[:, k, j * P:(j + 1) * P], y[:, j, k * P:(k + 1) * P], G.con("ident"))
                    mm.then_inc(S["turned"], 1)

        @block.scalar
        def _(act):
            act.wait_ge(S["edges"], 1)
            with act.Fori(0, M_HEADS) as i:
                need = needer(act, i)
                act.wait_ge(S["turn_done"], i + 1)
                act.activation(pick[:, :], T.pick[:, bass.ds(i * P, P)], ACT.Copy).then_inc(S["picked"], 1)
                for s in range(2):
                    for m in range(4):
                        n = 4 * s + m
                        need("qk_sum", n + 1)
                        if s:
                            need("conv_done", m + 1)
                        act.activation(z[:, m, M_TAPS - 1:], G.banks[:, n, :], ACT.Identity,
                                       bias=G.col("m_conv", 6 * (4 * i + (16 * s + m)) + 5)).then_inc(S["biased"], 1)
                    for m in range(4):
                        need("conv_done", 4 * s + m + 1)
                        act.activation(qk[:, s, m, :], cv[:, m, :], ACT.Silu).then_inc(S["silu_done"], 1)
                for j in range(JT):
                    need("v_sum", j + 1)
                    act.activation(v[:, j, :], G.banks[:, j, :], ACT.Copy).then_inc(S["v_done"], 1)
                for j in range(JT):
                    need("o_sum", j + 1)
                    act.activation(og[:, j, :], G.banks[:, 4 + j, :], ACT.Sigmoid).then_inc(S["o_done"], 1)
                need("diag_done", 4)
                for a in range(JT):
                    for j in range(a, JT):
                        of = dg[:, a, :] if j == a else T.nM[:, i, j * P:(j + 1) * P]
                        ins = act.activation(E[:, a, j * P:(j + 1) * P], of, ACT.Exp, bias=T.ucol[:, pair(a, j), bass.ds(i, 1)])
                    ins.then_inc(S["exp_done"], 1)
                need("inverted", 1)
                for j in range(JT):
                    need("num_sum", j + 1)
                    act.activation(y[:, j, :], G.banks[:, 4 + j, :], ACT.Copy, scale=rc[:, j:j + 1], accum_out=total[:, j:j + 1])\
                       .then_inc(S["y_done"], 1)
                for j in range(JT):
                    need("centred", j + 1)
                    act.activation(cv[:, j, :], y[:, j, :], ACT.Square, accum_out=sqs[:, j:j + 1]).then_inc(S["squared"], 1)
                need("var_in", 1)
                act.activation(rstd, rstd, ACT.Sqrt).then_inc(S["rooted"], 1)
                for k in range(MT_):
                    need("turned", k + 1)
                    act.activation(T.haT[:, 4 * i + k, :], G.banks[:, k, :], ACT.Copy, scale=G.col("m_gain", 4 * i + k))\
                       .then_inc(S["head_done"], 1)

        @block.vector
        def _(dve):
            dve.memset(z[:, :, 0:M_TAPS - 1], 0.0).then_inc(S["edges"], 1)
            dve.sem_inc(S["turn_done"], 1)
            step = Link(dve, S["step"])
            STEPS = 8 * (M_TAPS - 1) + 3
            with dve.Fori(0, M_HEADS) as i:
                need = needer(dve, i)
                step.start(i * STEPS)
                for s in range(2):
                    for m in range(4):
                        at = 6 * (4 * i + (16 * s + m))
                        need("biased", 4 * s + m + 1)
                        if s:
                            need("silu_done", m + 1)
                        for tap in range(M_TAPS):
                            of = z[:, m, tap:tap + SEQ]
                            if tap == 0:
                                step(dve.tensor_scalar(cv[:, m, :], of, G.col("m_conv", at), G.col("m_conv", at + 4), ALU.mult, ALU.add))
                                continue
                            ins = dve.scalar_tensor_tensor(out=cv[:, m, :], in0=of, scalar=G.col("m_conv", at + tap), in1=cv[:, m, :],
                                                           op0=ALU.mult, op1=ALU.add)
                            if tap < M_TAPS - 1:
                                step(ins)
                        ins.then_inc(S["conv_done"], 1)
                for a in range(JT):
                    dve.tensor_tensor(dg[:, a, :], T.nM[:, i, a * P:(a + 1) * P], T.masks[:, SEQ:SEQ + P], ALU.add).then_inc(S["diag_done"], 1)
                for a in range(JT):
                    need("score_sum", a + 1)
                    need("exp_done", a + 1)
                    e = E[:, a, a * P:SEQ]
                    dve.scalar_tensor_tensor(out=e, in0=G.banks[:, a, a * P:SEQ], scalar=M_DIM ** -0.5, in1=e, op0=ALU.mult, op1=ALU.mult)\
                       .then_inc(S["weighed"], 1)
                need("den_sum", 1)
                floor = T.ucol[:, N_PAIRS:N_PAIRS + JT, bass.ds(i, 1)].rearrange("p j o -> p (j o)")
                step(dve.scalar_tensor_tensor(out=rc, in0=G.banks[:, 0, 0:JT], scalar=-1.0, in1=floor, op0=ALU.mult, op1=ALU.max))
                step(dve.tensor_tensor(rc, G.banks[:, 0, 0:JT], rc, ALU.max))
                dve.reciprocal(rc, rc).then_inc(S["inverted"], 1)
                need("y_done", 4)
                dve.tensor_scalar(mean, total, 1.0 / M_DIM, None, ALU.mult).then_inc(S["mean_done"], 4)
                need("mean_done", 4)
                for j in range(JT):
                    dve.tensor_scalar(y[:, j, :], y[:, j, :], mean[:, j:j + 1], None, ALU.subtract).then_inc(S["centred"], 1)
                need("squared", 4)
                dve.tensor_scalar(rstd, sqs, 1.0 / M_DIM, HEAD_EPS, ALU.mult, ALU.add).then_inc(S["var_in"], 1)
                need("rooted", 1)
                step(dve.reciprocal(rstd, rstd))
                for j in range(JT):
                    dve.scalar_tensor_tensor(out=y[:, j, :], in0=y[:, j, :], scalar=rstd[:, j:j + 1], in1=og[:, j, :],
                                             op0=ALU.mult, op1=ALU.mult).then_inc(S["gated"], 1)
                need("head_done", 4)
                dve.sem_inc(S["turn_done"], 1)
                assert step.n == STEPS, step.n

        G.first += 4 * M_HEADS


def hgrn(G, T):
    nc = G.nc
    HH = 4
    IN = 7
    ALL = IN + 2
    PER = dict(q_sum=4, q_done=4, f_sum=4, f_done=4, f_ready=4, k_done=4, picked=1, v_sum=4, v_done=4, g_sum=4, g_done=4,
               operands=HH * ALL, level_sum=HH * (ALL + 1), level_done=HH * (IN + 1), far_done=HH * 2, o_sum=HH, o_squared=HH,
               sq_sum=HH, var_in=HH, rooted=HH, inverted=HH, normed=HH, o_done=HH, turn_done=1)
    operand_count = lambda n, l, e: n * 2 * ALL + 2 * l + e + 1
    sum_count = lambda n, l, e: n * 2 * (ALL + 1) + 2 * (l + 1) + e + 1
    drain_count = lambda n, l, e: n * 2 * (IN + 1) + 2 * (l + 1) + e + 1
    with ExitStack() as ctx:
        S = stage(G, "hgrn", ctx, "loaded", "go", *PER)
        q = G.sb("hgrn_q", [P, HH, SEQ], ctx=ctx)
        k = G.sb("hgrn_k", [P, HH, SEQ], ctx=ctx)
        f = G.sb("hgrn_f", [P, HH, SEQ], ctx=ctx)
        v = G.sb("hgrn_v", [P, JT, HH * P], ctx=ctx)
        g = G.sb("hgrn_g", [P, HH, SEQ], ctx=ctx)
        totals = G.sb("hgrn_totals", [P, 2, SEQ], ctx=ctx)
        w = G.sb("hgrn_weights", [P, 2, JT, SEQ], ctx=ctx)
        sq, rstd = G.hT[:, 0:2, :], G.hT[:, 2:4, :]
        pick = G.sb("hgrn_pick", [M_HEADS, P], ctx=ctx)
        masks = G.sb("hgrn_masks", [P, IN * P], U32, ctx=ctx)
        block = ctx.enter_context(nc.Block())
        tiles = [slice(j * P, (j + 1) * P) for j in range(JT)]
        bank = lambda l, e: G.banks[:, 2 * e + (l + 1) % 2, :]

        def diagonal(e):
            of = w[:, e, 0, :]
            return bass.AP(tensor=of.tensor, offset=of.offset, ap=[of.ap[0], [SEQ + P, JT], [1, P]])

        def total(l, h, e):
            at = SEQ - (SEQ >> (l - 1)) if l else 0
            return totals[:, e, at:at + (SEQ >> l)] if l else f[:, h, :]

        def needer(eng, i):
            return lambda name, n: eng.wait_ge(S[name], PER[name] * i + n)

        @block.sync
        def _(sp):
            sp.dma_start(masks[:, :], G.aps["pair_masks"]).then_inc(S["loaded"], 16)
            for i in range(2):
                for c, name in enumerate(("q_sum", "f_sum", "v_sum", "g_sum")):
                    sp.wait_ge(S[name], 4 * i + 4)
                    sp.dma_start(G.ring[:, G.slot(c), :], G.weights[4 * i + (G.first + c + SLOTS)])\
                      .then_inc(G.landed[G.slot(c)], 16)

        @block.tensor
        def _(pe):
            with pe.Fori(0, 2) as i:
                need = needer(pe, i)
                pe.wait_ge(S["turn_done"], i + 1)
                arrived = lambda c: pe.wait_ge(G.landed[G.slot(c)], 16 * (2 * i + (G.first + c) // SLOTS + 1))
                for c, name in enumerate(("q_sum", "f_sum", "v_sum")):
                    arrived(c)
                    wt = G.chunk(c, KT)
                    if c == 2:
                        need("picked", 1)
                        need("q_done", 4)
                    for m in range(4):
                        b = 4 * (c % 2) + m
                        if c != 2:
                            project(pe, G, c, m, b, G.x).then_inc(S[name], 1)
                            continue
                        for kk in range(KT):
                            pe.matmul(G.banks[:, b, :], G.x[:, kk, tiles[m]], wt[:, kk, :], start=(kk == 0), stop=False)
                        pe.matmul(G.banks[:, b, :], pick[:, :], T.brows[:, 2, :], start=False, stop=True).then_inc(S["v_sum"], 1)
                need("v_done", 4)
                need("k_done", 4)
                arrived(3)
                for n in range(2):
                    for l in range(-1, ALL):
                        for e in range(2):
                            h = 2 * n + e
                            if l >= 0:
                                need("operands", operand_count(n, l, e))
                            if 1 <= l <= IN + 1:
                                need("level_done", drain_count(n, l - 2, e))
                            elif n:
                                need("far_done", 4 * n)
                            left, right, b = k[:, h, :], q[:, h, :], bank(l, e)
                            if l < IN:
                                for j in range(JT):
                                    mm = pe.matmul(b[:, tiles[j]], left[:, tiles[j]], right[:, tiles[j]], start=True, stop=True)
                            elif l == IN:
                                for to, j in enumerate((0, 2)):
                                    mm = pe.matmul(b[:, tiles[to]], left[:, tiles[j]], right[:, tiles[j + 1]], start=True, stop=True)
                            else:
                                for j in range(2):
                                    mm = pe.matmul(b[:, j * 256:(j + 1) * 256], left[:, tiles[j]], right[:, 256:512], start=True, stop=True)
                            mm.then_inc(S["level_sum"], 1)
                        if n == 0 and 0 <= l < 4:
                            project(pe, G, 3, l, 4 + l, G.x).then_inc(S["g_sum"], 1)
                    if n == 0:
                        need("g_done", 4)
                    for e in range(2):
                        need("level_done", drain_count(n, IN - 1, e))
                        need("far_done", 4 * n + 2 * e + 2)
                        if n:
                            need("o_done", 2 * (n - 1) + e + 1)
                        for j in range(JT):
                            mm = pe.matmul(G.banks[:, 4 + e, j * P:SEQ], v[:, j, (2 * n + e) * P:(2 * n + e + 1) * P],
                                           w[:, e, j, j * P:SEQ], start=(j == 0), stop=(j == JT - 1), skip_group_check=True)
                        mm.then_inc(S["o_sum"], 1)
                    for e in range(2):
                        need("o_squared", 2 * n + e + 1)
                        pe.matmul(G.banks[:, 6 + e, :], G.con("ones"), sq[:, e, :], start=True, stop=True).then_inc(S["sq_sum"], 1)

        @block.scalar
        def _(act):
            with act.Fori(0, 2) as i:
                need = needer(act, i)
                act.wait_ge(S["turn_done"], i + 1)
                act.activation(pick[:, :], T.pick[:, bass.ds(i * P, P)], ACT.Copy).then_inc(S["picked"], 1)
                for m in range(4):
                    need("q_sum", m + 1)
                    act.activation(q[:, m, :], G.banks[:, m, :], ACT.Silu, bias=G.col("b_hq", 4 * i + m)).then_inc(S["q_done"], 1)
                for m in range(4):
                    need("f_sum", m + 1)
                    act.activation(f[:, m, :], G.banks[:, 4 + m, :], ACT.Identity, bias=G.col("b_hf", 4 * i + m)).then_inc(S["f_done"], 1)
                for m in range(4):
                    need("f_done", m + 1)
                    act.activation(k[:, m, :], f[:, m, :], ACT.Sigmoid, scale=-1.0).then_inc(S["k_done"], 1)
                for m in range(4):
                    need("k_done", m + 1)
                    act.activation(f[:, m, :], f[:, m, :], ACT.Sigmoid).then_inc(S["f_ready"], 1)
                for m in range(4):
                    need("g_sum", m + 1)
                    act.activation(g[:, m, :], G.banks[:, 4 + m, :], ACT.Sigmoid, bias=G.col("b_hg", 4 * i + m)).then_inc(S["g_done"], 1)
                for n in range(2):
                    for e in range(2):
                        for l in (IN, IN + 1):
                            b = bank(l, e)
                            need("level_sum", sum_count(n, l, e))
                            for to in range(2):
                                if l == IN:
                                    ins = act.activation(w[:, e, 2 * to, (2 * to + 1) * P:(2 * to + 2) * P], b[:, tiles[to]], ACT.Copy)
                                else:
                                    ins = act.activation(w[:, e, to, 256:512], b[:, to * 256:(to + 1) * 256], ACT.Copy)
                            ins.then_inc(S["far_done"], 1)
                    for e in range(2):
                        need("o_sum", 2 * n + e + 1)
                        act.activation(sq[:, e, :], G.banks[:, 4 + e, :], ACT.Square).then_inc(S["o_squared"], 1)
                    for e in range(2):
                        need("var_in", 2 * n + e + 1)
                        act.activation(rstd[:, e, :], rstd[:, e, :], ACT.Sqrt).then_inc(S["rooted"], 1)

        @block.vector
        def _(dve):
            dve.sem_inc(S["turn_done"], 1)
            dve.wait_ge(S["loaded"], 16)
            with dve.Fori(0, 2) as i:
                need = needer(dve, i)
                for m in range(4):
                    need("v_sum", m + 1)
                    dve.tensor_copy(v[:, m, :], G.banks[:, m, :]).then_inc(S["v_done"], 1)
                need("f_ready", 4)
                for n in range(2):
                    for l in range(ALL + 1):
                        for e in range(2):
                            h = 2 * n + e
                            need("level_sum", sum_count(n, l - 1, e))
                            if l == 0:
                                dve.tensor_tensor(q[:, h, :], q[:, h, :], f[:, h, :], ALU.mult).then_inc(S["operands"], 1)
                            elif l < ALL:
                                need("operands", operand_count(n, l - 1, e))
                                b = 1 << (l - 1)
                                halves = lambda a: a.rearrange("p (n e s) -> p n e s", e=2, s=b)
                                before = total(l - 1, h, e)
                                over = lambda x: bass.AP(tensor=before.tensor, offset=before[:, x:x + 1].offset,
                                                         ap=[before.ap[0], [2, SEQ // (2 * b)], [0, b]])
                                if l < ALL - 1:
                                    dve.tensor_tensor(total(l, h, e), before[:, 0::2], before[:, 1::2], ALU.mult)
                                first, second = halves(k[:, h, :])[:, :, 0, :], halves(q[:, h, :])[:, :, 1, :]
                                dve.tensor_tensor(first, first, over(1), ALU.mult)
                                dve.tensor_tensor(second, second, over(0), ALU.mult).then_inc(S["operands"], 1)
                            if l == 0:
                                if n:
                                    need("o_sum", 2 * (n - 1) + e + 1)
                                dve.tensor_tensor(diagonal(e), bank(-1, e).rearrange("p (j t) -> p j t", j=JT),
                                                  spread(G.con("ident"), JT), ALU.mult).then_inc(S["level_done"], 1)
                            elif l <= IN:
                                need("level_done", drain_count(n, l - 2, e))
                                dve.sem_inc(S["go"], 1)
                                dve.copy_predicated(diagonal(e), spread(masks[:, (l - 1) * P:l * P], JT),
                                                    bank(l - 1, e).rearrange("p (j t) -> p j t", j=JT)).then_inc(S["level_done"], 1)
                    for e in range(2):
                        need("sq_sum", 2 * n + e + 1)
                        dve.tensor_scalar(rstd[:, e, :], G.banks[:, 6 + e, :], 1.0 / H_DIM, HEAD_EPS, ALU.mult, ALU.add)\
                           .then_inc(S["var_in"], 1)
                    for e in range(2):
                        need("rooted", 2 * n + e + 1)
                        dve.reciprocal(rstd[:, e, :], rstd[:, e, :]).then_inc(S["inverted"], 1)
                        need("inverted", 2 * n + e + 1)
                        out = T.hbT[:, 4 * i + (2 * n + e), :]
                        dve.scalar_tensor_tensor(out=out, in0=G.banks[:, 4 + e, :], scalar=G.col("h_gain", 4 * i + (2 * n + e)),
                                                 in1=rstd[:, e, :], op0=ALU.mult, op1=ALU.mult).then_inc(S["normed"], 1)
                        need("normed", 2 * n + e + 1)
                        dve.tensor_tensor(out, out, g[:, 2 * n + e, :], ALU.mult).then_inc(S["o_done"], 1)
                need("o_done", HH)
                dve.sem_inc(S["turn_done"], 1)

        G.first += 8


def gated_merge(G, T):
    nc = G.nc
    tiles_a, tiles_b = M_HEADS * MT_, H_HEADS
    tiles = tiles_a + tiles_b
    gate_halves, branch_halves = 8, tiles // 2
    halves = gate_halves + branch_halves + 4
    part_words = CHUNK // 2
    with ExitStack() as ctx:
        S = stage(G, "merge", ctx, "x_high", "x_split", "rounded", "split", "tile_high", "tile_split", "gate_sum", "gate_done", "used",
                  "branch_done", "mixed", "out_sum", "added")
        gates = [G.sb("merge_gate", [P, KT, SEQ], ctx=ctx), G.hT]
        w_parts = [G.sb("merge_weights_" + part, [P, 2, part_words], F32R, ctx=ctx) for part in ("high", "low")]
        x_parts = [G.sb("merge_in_" + part, [P, KT, SEQ], F32R, ctx=ctx) for part in ("high", "low")]
        block = ctx.enter_context(nc.Block())

        def landed_half(n):
            c, h = n // 2, n % 2
            if gate_halves <= n < gate_halves + branch_halves:
                return G.ring[:, G.slot(c), h * part_words:(h + 1) * part_words], [w[:, h, :] for w in w_parts]
            return G.chunk(c, KT)[:, :, h * 256:(h + 1) * 256], [w[:, h, :].rearrange("p (k n) -> p k n", k=KT) for w in w_parts]

        def source(t):
            return T.haT[:, t, :] if t < tiles_a else T.hbT[:, t - tiles_a, :] if t < tiles else G.hT[:, t - tiles, :]

        @block.sync
        def _(sp):
            G.feed(sp, halves // 2, S["split"], per=2)

        @block.gpsimd
        def _(pool):
            for n in range(halves):
                landed, parts = landed_half(n)
                pool.wait_ge(S["rounded"], n + 1)
                pool.tensor_tensor(parts[1], landed, parts[0].bitcast(F32), ALU.subtract).then_inc(S["split"], 1)

        @block.tensor
        def _(pe):
            def output(n, m, bank):
                w = landed_half(n)[1]
                for k in range(KT):
                    if n == 0 and m == 0:
                        pe.wait_ge(S["x_split"], k + 1)
                    mm = exact_product(pe, G.banks[:, bank, :], [x[:, k, m * P:(m + 1) * P] for x in w], [x[:, k, :] for x in x_parts],
                                       start=(k == 0), stop=(k == KT - 1))
                return mm

            for t in range(2 * KT):
                if t % 2 == 0:
                    pe.wait_ge(S["split"], t // 2 + 1)
                if t >= 8:
                    pe.wait_ge(S["gate_done"], t - 7)
                output(t // 2, t % 2, t % 8).then_inc(S["gate_sum"], 1)
            pe.wait_ge(S["gate_done"], 2 * KT)
            for t in range(tiles):
                if t == tiles_a:
                    pe.wait_ge(S["branch_done"], KT)
                if t % 2 == 0:
                    pe.wait_ge(S["split"], gate_halves + t // 2 + 1)
                pe.wait_ge(S["tile_split"], t + 1)
                for m in range(KT):
                    at = t % 2 * D + m * P
                    mm = exact_product(pe, G.banks[:, m, :], [w[:, t // 2 % 2, at:at + P] for w in w_parts], [x[:, t % KT, :] for x in x_parts],
                                       start=t in (0, tiles_a), stop=t in (tiles_a - 1, tiles - 1))
                if t % 2:
                    mm.then_inc(S["used"], 1)
            pe.wait_ge(S["tile_split"], tiles + KT)
            for m in range(KT):
                if m % 2 == 0:
                    pe.wait_ge(S["split"], gate_halves + branch_halves + m // 2 + 1)
                output(gate_halves + branch_halves + m // 2, m % 2, m).then_inc(S["out_sum"], 1)

        @block.scalar
        def _(act):
            def high(n):
                G.arrived(act, n // 2 % 2, n // 4)
                landed, parts = landed_half(n)
                act.activation(parts[0], landed, ACT.Copy).then_inc(S["rounded"], 1)

            def tile_high(t):
                act.activation(x_parts[0][:, t % KT, :], source(t), ACT.Copy).then_inc(S["tile_high"], 1)

            for n in range(2):
                high(n)
            for k in range(KT):
                act.activation(x_parts[0][:, k, :], G.x[:, k, :], ACT.Copy).then_inc(S["x_high"], 1)
            for t in range(2 * KT):
                act.wait_ge(S["gate_sum"], t + 1)
                if t % 2:
                    high(t // 2 + 2)
                act.activation(gates[t // KT][:, t % KT, :], G.banks[:, t % 8, :], ACT.Sigmoid, bias=G.col("b_ga" if t < KT else "b_gb", t % KT))\
                   .then_inc(S["gate_done"], 1)
            for t in range(tiles):
                if t >= KT and t % 2 == 0:
                    act.wait_ge(S["used"], t // 2 - 3)
                    high(gate_halves + t // 2 - 2)
                tile_high(t)
            for u in range(branch_halves - 3, branch_halves + 1):
                act.wait_ge(S["used"], u)
                high(gate_halves + u + 1)
            for k in range(KT):
                act.wait_ge(S["mixed"], k + 1)
                tile_high(tiles + k)
            for n in range(halves - 2, halves):
                act.wait_ge(S["out_sum"], 2 * (n - halves + 3))
                high(n)

        @block.vector
        def _(dve):
            def tile_low(t):
                dve.wait_ge(S["tile_high"], t + 1)
                dve.tensor_tensor(x_parts[1][:, t % KT, :], source(t), x_parts[0][:, t % KT, :].bitcast(F32), ALU.subtract)\
                   .then_inc(S["tile_split"], 1)

            for k in range(KT):
                dve.wait_ge(S["x_high"], k + 1)
                dve.tensor_tensor(x_parts[1][:, k, :], G.x[:, k, :], x_parts[0][:, k, :].bitcast(F32), ALU.subtract).then_inc(S["x_split"], 1)
            dve.wait_ge(S["gate_done"], 2 * KT)
            for t in range(tiles - 2):
                tile_low(t)
            for m in range(KT):
                dve.wait_ge(S["used"], tiles_a // 2)
                dve.tensor_tensor(gates[0][:, m, :], G.banks[:, m, :], gates[0][:, m, :], ALU.mult).then_inc(S["branch_done"], 1)
            for t in range(tiles - 2, tiles):
                tile_low(t)
            for m in range(KT):
                dve.wait_ge(S["used"], branch_halves)
                dve.tensor_tensor(G.hT[:, m, :], G.banks[:, m, :], G.hT[:, m, :], ALU.mult).then_inc(S["branch_done"], 1)
                dve.wait_ge(S["branch_done"], KT + m + 1)
                dve.tensor_tensor(G.hT[:, m, :], G.hT[:, m, :], gates[0][:, m, :], ALU.add).then_inc(S["mixed"], 1)
            for k in range(KT):
                tile_low(tiles + k)
            for m in range(KT):
                dve.wait_ge(S["out_sum"], m + 1)
                dve.scalar_tensor_tensor(out=G.x[:, m, :], in0=G.x[:, m, :], scalar=ALPHA, in1=G.banks[:, m, :],
                                         op0=ALU.mult, op1=ALU.add).then_inc(S["added"], 1)

        G.first += halves // 2


def layer_norm(G, name, gain, bias):
    nc = G.nc
    with ExitStack() as ctx:
        S = stage(G, name, ctx, "summed", "mean_done", "centred", "squared", "squares_summed", "var_done", "root_done", "rstd_done",
                  "scaled", "shifted")
        sq = G.sb(name + "_squares", [P, KT, SEQ], ctx=ctx)
        mu = G.sb(name + "_mean", [P, SEQ], ctx=ctx)
        rstd = G.sb(name + "_rstd", [P, SEQ], ctx=ctx)
        block = ctx.enter_context(nc.Block())

        @block.tensor
        def _(pe):
            for k in range(KT):
                mm = pe.matmul(G.banks[:, 0, :], G.con("ones"), G.x[:, k, :], start=(k == 0), stop=(k == KT - 1))
            mm.then_inc(S["summed"], 1)
            for k in range(KT):
                pe.wait_ge(S["squared"], k + 1)
                mm = pe.matmul(G.banks[:, 1, :], G.con("ones"), sq[:, k, :], start=(k == 0), stop=(k == KT - 1))
            mm.then_inc(S["squares_summed"], 1)

        @block.scalar
        def _(act):
            for k in range(KT):
                act.wait_ge(S["centred"], k + 1)
                act.activation(sq[:, k, :], G.x[:, k, :], ACT.Square).then_inc(S["squared"], 1)
            act.wait_ge(S["var_done"], 1)
            act.activation(rstd[:, :], rstd[:, :], ACT.Sqrt).then_inc(S["root_done"], 1)
            for k in range(KT):
                act.wait_ge(S["scaled"], k + 1)
                act.activation(G.x[:, k, :], G.x[:, k, :], ACT.Identity, bias=G.col(bias, k)).then_inc(S["shifted"], 1)

        @block.vector
        def _(dve):
            dve.wait_ge(S["summed"], 1)
            dve.tensor_scalar(mu[:, :], G.banks[:, 0, :], 1.0 / D, None, ALU.mult).then_inc(S["mean_done"], 1)
            dve.wait_ge(S["mean_done"], 1)
            for k in range(KT):
                dve.tensor_tensor(G.x[:, k, :], G.x[:, k, :], mu[:, :], ALU.subtract).then_inc(S["centred"], 1)
            dve.wait_ge(S["squares_summed"], 1)
            dve.tensor_scalar(rstd[:, :], G.banks[:, 1, :], 1.0 / D, LN_EPS, ALU.mult, ALU.add).then_inc(S["var_done"], 1)
            dve.wait_ge(S["root_done"], 1)
            dve.reciprocal(rstd[:, :], rstd[:, :]).then_inc(S["rstd_done"], 1)
            dve.wait_ge(S["rstd_done"], 1)
            for k in range(KT):
                dve.scalar_tensor_tensor(out=G.x[:, k, :], in0=G.x[:, k, :], scalar=G.col(gain, k), in1=rstd[:, :],
                                         op0=ALU.mult, op1=ALU.mult).then_inc(S["scaled"], 1)


def third_block(G):
    with ExitStack() as ctx:
        T = Shared()
        T.haT = G.sb("mlstm_out_T", [P, M_HEADS * MT_, SEQ], ctx=ctx)
        T.hbT = G.sb("hgrn_out_T", [P, H_HEADS, SEQ], ctx=ctx)
        with ExitStack() as inner:
            T.masks = G.sb("third_masks_sb", list(G.aps["third_masks"].shape), ctx=inner)
            T.pick = T.masks[0:M_HEADS, SEQ + P:SEQ + P + M_HEADS * P]
            T.brows = G.sb("bias_rows3_sb", [M_HEADS, 3, SEQ], ctx=inner)
            T.nM = G.sb("minus_max", [P, M_HEADS, SEQ], ctx=inner)
            T.ucol = G.sb("gate_columns", [P, N_PAIRS + JT, M_HEADS], ctx=inner)
            mlstm_gates(G, T)
            mlstm(G, T)
            hgrn(G, T)
        gated_merge(G, T)
    layer_norm(G, "ln1", "ln1_g", "ln1_b")
    feed_forward(G, "ffn4", None, None, ACT.Silu, keep=ALPHA)
    layer_norm(G, "ln2", "ln2_g", "ln2_b")



def load(G):
    nc = G.nc
    with ExitStack() as ctx:
        S = stage(G, "load", ctx, "loaded")
        block = ctx.enter_context(nc.Block())

        @block.sync
        def _(sp):
            sp.dma_start(G.x[:, :, :], G.aps["x"].rearrange("(k p) n -> p k n", p=P)).then_inc(S["loaded"], 16)
            sp.dma_start(G.cols[:, :], G.aps["columns"]).then_inc(S["loaded"], 16)
            sp.dma_start(G.const[:, :], G.aps["constants"]).then_inc(S["loaded"], 16)
            for s in range(SLOTS):
                sp.dma_start(G.ring[:, s, :], G.weights[s]).then_inc(G.landed[s], 16)
            sp.wait_ge(S["loaded"], 48)


def store(G):
    nc = G.nc
    with ExitStack() as ctx:
        S = stage(G, "store", ctx, "stored")
        block = ctx.enter_context(nc.Block())

        @block.sync
        def _(sp):
            sp.dma_start(G.aps["out"].rearrange("(k p) n -> p k n", p=P), G.x[:, :, :]).then_inc(S["stored"], 16)
            sp.wait_ge(S["stored"], 16)


def three_blocks_kernel(nc, aps, layout):
    with ExitStack() as ctx:
        G = Core(nc, aps, layout, ctx)
        load(G)
        first_block(G)
        second_block(G)
        third_block(G)
        store(G)



def host_arrays(a):
    second = {n[:-2]: v for n, v in a.items() if n.endswith("_2")}
    third = {n[:-2]: v for n, v in a.items() if n.endswith("_3")}
    L = Layout()
    L.constant("ident", np.eye(P, dtype=np.float32))
    L.constant("ones", np.ones((P, P), np.float32))
    lay_first(L, a)
    lay_second(L, second)
    lay_third(L, third)
    arrays = {"weights": np.stack(L.chunks), "columns": np.concatenate(L.column_parts, 1),
              "constants": np.concatenate(L.constant_parts, 1), "x": a["x"][0].T, "pT": a["p"][0, 0].T,
              "buckets": bucket_rows(), **second_extra(), **third_extra(third)}
    return {n: np.ascontiguousarray(v) for n, v in arrays.items()}, {"columns": L.columns, "constants": L.constants}


def kernel(**inputs):
    import concourse.bacc as bacc
    from concourse.bass_utils import run_bass_kernel_spmd

    arrays, layout = host_arrays({n: np.asarray(v) for n, v in inputs.items()})
    nc = bacc.Bacc("TRN2", target_bir_lowering=False, num_devices=1)
    aps = {n: nc.dram_tensor(n, v.shape, mybir.dt.from_np(v.dtype), kind="ExternalInput").ap() for n, v in arrays.items()}
    aps["out"] = nc.dram_tensor("out", (D, SEQ), F32, kind="ExternalOutput").ap()
    three_blocks_kernel(nc, aps, layout)
    r = run_bass_kernel_spmd(nc, [arrays], core_ids=[0])
    return np.ascontiguousarray(r.results[0]["out"].T)[None]
```
